# Optimizing a Trainium2 kernel written in Bass

```python
import math
import jax, jax.numpy as jnp
from jax import lax
import numpy as np

D_MODEL = 1024
BATCH = 1
SEQ = 512
DEPTH = 1

D_MIX = D_MODEL
N_DN_HEADS = 4
DN_HEAD_DIM = 128
D_DN = N_DN_HEADS * DN_HEAD_DIM
CONV_K = 4
CHUNK = 64
POOL_WINDOWS = (2, 4, 8, 16)
N_POOL_GROUPS = len(POOL_WINDOWS)
D_POOL = D_MIX - D_DN
POOL_GROUP_DIM = D_POOL // N_POOL_GROUPS
D_IN_PROJ = 4 * D_DN + 2 * N_DN_HEADS + D_POOL
SPLITS = (3 * D_DN, 4 * D_DN, 4 * D_DN + N_DN_HEADS, 4 * D_DN + 2 * N_DN_HEADS)
N_EXPERTS = 32
TOP_K = 4
D_EXPERT = D_MODEL
SWIGLU_LIMIT = 7.0
SWIGLU_ALPHA = 1.702
MOE_BLOCK = 256
RMS_EPS = 1e-6
L2_EPS = 1e-6

kernel_name = 'hybrid_deltanet_pool_moe_block'

def _rmsnorm(x, w):
    xf = x.astype(jnp.float32)
    y = xf * lax.rsqrt(jnp.mean(xf * xf, axis=-1, keepdims=True) + RMS_EPS)
    return (y * w.astype(jnp.float32)).astype(x.dtype)

def _l2norm(x):
    return x * lax.rsqrt(jnp.sum(x * x, axis=-1, keepdims=True) + L2_EPS)

def _causal_depthwise_conv(x, w):
    c = x.shape[-1]
    return lax.conv_general_dilated(
        x, w.astype(x.dtype)[:, None, :], window_strides=(1,),
        padding=[(CONV_K - 1, 0)], dimension_numbers=('NWC', 'WIO', 'NWC'),
        feature_group_count=c)

def _chunk_gated_delta_rule(q, k, v, g, beta):
    b, t, h, dk = q.shape
    dv = v.shape[-1]
    n = t // CHUNK

    def heads_chunks(u):
        u = jnp.moveaxis(u, 2, 1)
        return u.reshape(b, h, n, CHUNK, *u.shape[3:])

    q = heads_chunks(q) * (dk ** -0.5)
    k = heads_chunks(k)
    v = heads_chunks(v)
    beta = heads_chunks(beta)
    g = jnp.cumsum(heads_chunks(g), axis=-1)
    pos = jnp.arange(CHUNK)
    causal = pos[:, None] >= pos[None, :]
    strict = pos[:, None] > pos[None, :]
    decay = jnp.exp(jnp.where(causal, g[..., :, None] - g[..., None, :], -jnp.inf))
    k_beta = k * beta[..., None]
    a_mat = jnp.where(strict, jnp.einsum('bhnid,bhnjd->bhnij', k_beta, k) * decay, 0.0)
    eye = jnp.broadcast_to(jnp.eye(CHUNK, dtype=q.dtype), a_mat.shape)
    t_mat = lax.linalg.triangular_solve(a_mat, eye, left_side=True, lower=True, unit_diagonal=True)
    u = jnp.einsum('bhnij,bhnjd->bhnid', t_mat, v * beta[..., None])
    w = jnp.einsum('bhnij,bhnjd->bhnid', t_mat, k_beta * jnp.exp(g)[..., None])
    qk = jnp.where(causal, jnp.einsum('bhnid,bhnjd->bhnij', q, k) * decay, 0.0)
    q_dec = q * jnp.exp(g)[..., None]
    k_dec = k * jnp.exp(g[..., -1:] - g)[..., None]
    g_tot = jnp.exp(g[..., -1])

    def step(state, inp):
        qd, kd, u_c, w_c, qk_c, gt = inp
        v_new = u_c - jnp.einsum('bhid,bhde->bhie', w_c, state)
        o = jnp.einsum('bhid,bhde->bhie', qd, state) + jnp.einsum('bhij,bhje->bhie', qk_c, v_new)
        state = state * gt[..., None, None] + jnp.einsum('bhid,bhie->bhde', kd, v_new)
        return state, o

    xs = tuple(jnp.moveaxis(a, 2, 0) for a in (q_dec, k_dec, u, w, qk, g_tot))
    s0 = jnp.zeros((b, h, dk, dv), q.dtype)
    _, o = lax.scan(step, s0, xs)
    o = jnp.moveaxis(o, 0, 2).reshape(b, h, t, dv)
    return jnp.moveaxis(o, 1, 2)

def _multiscale_pool(p, pool_w, pool_scale):
    b, t, _ = p.shape
    pf = p.astype(jnp.float32).reshape(b, t, N_POOL_GROUPS, POOL_GROUP_DIM)
    cs = jnp.cumsum(pf, axis=1)
    pos = jnp.arange(1, t + 1, dtype=jnp.float32)
    means = []
    for gi, win in enumerate(POOL_WINDOWS):
        c = cs[:, :, gi]
        lag = jnp.pad(c, ((0, 0), (win, 0), (0, 0)))[:, :t]
        cnt = jnp.minimum(pos, float(win))[None, :, None]
        means.append((c - lag) / cnt)
    mixed = jnp.stack(means, axis=2) - pf
    y = jnp.einsum('btgc,gcd->btgd', mixed, pool_w.astype(jnp.float32))
    return (y.reshape(b, t, D_POOL) * pool_scale.astype(jnp.float32)).astype(p.dtype)

def _moe(h, w_router, b_router, w_gate_up, b_gate_up, w_down, b_down):
    d = h.shape[-1]
    xt = h.reshape(-1, d)
    n_tok = xt.shape[0]
    logits = (xt @ w_router + b_router).astype(jnp.float32)
    top_val, top_idx = lax.top_k(logits, TOP_K)
    gates = jax.nn.softmax(top_val, axis=-1)
    n_assign = n_tok * TOP_K
    flat_e = top_idx.reshape(-1)
    flat_tok = jnp.arange(n_assign, dtype=jnp.int32) // TOP_K
    flat_w = gates.reshape(-1)
    order = jnp.argsort(flat_e)
    sorted_e = flat_e[order]
    counts = jnp.bincount(flat_e, length=N_EXPERTS)
    padded = ((counts + MOE_BLOCK - 1) // MOE_BLOCK) * MOE_BLOCK
    pad_end = jnp.cumsum(padded)
    pad_start = pad_end - padded
    start = jnp.cumsum(counts) - counts
    rank = jnp.arange(n_assign, dtype=jnp.int32) - start[sorted_e]
    dest = pad_start[sorted_e] + rank
    n_blocks = -(-n_assign // MOE_BLOCK) + N_EXPERTS
    n_rows = n_blocks * MOE_BLOCK
    row_tok = jnp.zeros((n_rows,), jnp.int32).at[dest].set(flat_tok[order])
    row_w = jnp.zeros((n_rows,), jnp.float32).at[dest].set(flat_w[order])
    block_start = jnp.arange(n_blocks, dtype=jnp.int32) * MOE_BLOCK
    block_e = jnp.minimum(jnp.searchsorted(pad_end, block_start, side='right'), N_EXPERTS - 1)

    def expert_block(args):
        e, tok, wt = args
        xb = xt[tok]
        gu = xb @ w_gate_up[e] + b_gate_up[e]
        gate = jnp.minimum(gu[:, :D_EXPERT], SWIGLU_LIMIT)
        up = jnp.clip(gu[:, D_EXPERT:], -SWIGLU_LIMIT, SWIGLU_LIMIT)
        act = (up + 1.0) * gate * jax.nn.sigmoid(SWIGLU_ALPHA * gate)
        yb = act @ w_down[e] + b_down[e]
        return yb * wt.astype(yb.dtype)[:, None]

    y = lax.map(expert_block, (block_e, row_tok.reshape(n_blocks, MOE_BLOCK),
                               row_w.reshape(n_blocks, MOE_BLOCK)))
    out = jax.ops.segment_sum(y.reshape(n_rows, d), row_tok, num_segments=n_tok)
    return out.reshape(h.shape).astype(h.dtype)

def setup_inputs(seed: int = 0) -> dict:
    key = jax.random.key(seed)
    ks = jax.random.split(key, 18)
    L = DEPTH
    f32 = jnp.float32

    def nrm(k, shape, scale):
        return jax.random.normal(k, shape, f32) * scale

    x = nrm(ks[0], (BATCH, SEQ, D_MODEL), 1.0)
    attn_norm_w = 1.0 + nrm(ks[1], (L, D_MODEL), 0.02)
    w_in = nrm(ks[2], (L, D_MODEL, D_IN_PROJ), D_MODEL ** -0.5)
    conv_w = nrm(ks[3], (L, CONV_K, 3 * D_DN), CONV_K ** -0.5)
    a_log = jnp.log(jax.random.uniform(ks[4], (L, N_DN_HEADS), f32, 1.0, 16.0))
    dt = jnp.exp(jax.random.uniform(ks[5], (L, N_DN_HEADS), f32, math.log(1e-3), math.log(1e-1)))
    dt_bias = dt + jnp.log(-jnp.expm1(-dt))
    dn_norm_w = 1.0 + nrm(ks[6], (L, DN_HEAD_DIM), 0.02)
    pool_w = nrm(ks[7], (L, N_POOL_GROUPS, POOL_GROUP_DIM, POOL_GROUP_DIM), POOL_GROUP_DIM ** -0.5)
    pool_scale = 1.0 + nrm(ks[8], (L, D_POOL), 0.1)
    w_out = nrm(ks[9], (L, D_MIX, D_MODEL), D_MIX ** -0.5)
    ffn_norm_w = 1.0 + nrm(ks[10], (L, D_MODEL), 0.02)
    w_router = nrm(ks[11], (L, D_MODEL, N_EXPERTS), D_MODEL ** -0.5)
    b_router = nrm(ks[12], (L, N_EXPERTS), 0.01)
    w_gate_up = nrm(ks[13], (L, N_EXPERTS, D_MODEL, 2 * D_EXPERT), D_MODEL ** -0.5)
    b_gate_up = nrm(ks[14], (L, N_EXPERTS, 2 * D_EXPERT), 0.01)
    w_down = nrm(ks[15], (L, N_EXPERTS, D_EXPERT, D_MODEL), D_EXPERT ** -0.5)
    b_down = nrm(ks[16], (L, N_EXPERTS, D_MODEL), 0.01)
    final_norm_w = 1.0 + nrm(ks[17], (D_MODEL,), 0.02)
    return {'x': x, 'attn_norm_w': attn_norm_w, 'w_in': w_in, 'conv_w': conv_w,
            'a_log': a_log, 'dt_bias': dt_bias, 'dn_norm_w': dn_norm_w,
            'pool_w': pool_w, 'pool_scale': pool_scale, 'w_out': w_out,
            'ffn_norm_w': ffn_norm_w, 'w_router': w_router, 'b_router': b_router,
            'w_gate_up': w_gate_up, 'b_gate_up': b_gate_up, 'w_down': w_down,
            'b_down': b_down, 'final_norm_w': final_norm_w}

def reference(x, attn_norm_w, w_in, conv_w, a_log, dt_bias, dn_norm_w, pool_w, pool_scale,
              w_out, ffn_norm_w, w_router, b_router, w_gate_up, b_gate_up, w_down, b_down,
              final_norm_w):
    b, t, _ = x.shape
    f32 = jnp.float32
    for l in range(DEPTH):
        h = _rmsnorm(x, attn_norm_w[l])
        proj = h @ w_in[l]
        qkv, z, beta_logit, a_in, p = jnp.split(proj, list(SPLITS), axis=-1)
        qkv = jax.nn.silu(_causal_depthwise_conv(qkv, conv_w[l])).astype(f32)
        q, k, v = jnp.split(qkv, 3, axis=-1)
        q = _l2norm(q.reshape(b, t, N_DN_HEADS, DN_HEAD_DIM))
        k = _l2norm(k.reshape(b, t, N_DN_HEADS, DN_HEAD_DIM))
        v = v.reshape(b, t, N_DN_HEADS, DN_HEAD_DIM)
        beta = jax.nn.sigmoid(beta_logit.astype(f32))
        g = -jnp.exp(a_log[l].astype(f32)) * jax.nn.softplus(a_in.astype(f32) + dt_bias[l].astype(f32))
        o = _chunk_gated_delta_rule(q, k, v, g, beta)
        o = _rmsnorm(o, dn_norm_w[l]) * jax.nn.silu(z.astype(f32).reshape(b, t, N_DN_HEADS, DN_HEAD_DIM))
        dn_out = o.reshape(b, t, D_DN).astype(x.dtype)
        pool_out = _multiscale_pool(p, pool_w[l], pool_scale[l])
        x = x + jnp.concatenate([dn_out, pool_out], axis=-1) @ w_out[l]
        x = x + _moe(_rmsnorm(x, ffn_norm_w[l]), w_router[l], b_router[l],
                     w_gate_up[l], b_gate_up[l], w_down[l], b_down[l])
    return _rmsnorm(x, final_norm_w)


_drawn_inputs = setup_inputs


def setup_inputs(seed=0):
    import zlib

    import numpy as np

    out = dict(_drawn_inputs(seed))
    spreads = {}
    factors = {'b_gate_up': 8.0, 'b_down': 8.0, 'final_norm_w': 2.871}
    for name, (base, spread) in spreads.items():
        noise = np.random.default_rng([zlib.crc32(name.encode()), seed]).standard_normal(out[name].shape)
        drawn = base * np.exp(spread * noise) if base else spread * noise
        out[name] = __import__('jax').numpy.asarray(drawn.astype(out[name].dtype))
    for name, factor in factors.items():
        out[name] = (out[name] * factor).astype(out[name].dtype)
    return out
```

```python
from contextlib import ExitStack

import concourse.bass as bass
from concourse import mybir

F32, I32, U32, BF16 = mybir.dt.float32, mybir.dt.int32, mybir.dt.uint32, mybir.dt.bfloat16
ALU, ACT, AX = mybir.AluOpType, mybir.ActivationFunctionType, mybir.AxisListType

P = 128
D = 1024
T = 512
TB = T // P
KD = D // P
H = 4
CONV = 4
CH = 64
WINDOWS = (2, 4, 8, 16)
PAD = max(WINDOWS)
NQKV = 3 * H
E, TOPK = 32, 4
SLOTS = 32
Q = P // SLOTS
QD = D // Q
MAXB = T * TOPK // SLOTS + E
C_Z, C_BA, C_P = NQKV * P, (NQKV + H) * P, (NQKV + H) * P + 2 * H
RMS_EPS, L2_EPS = 1e-6, 1e-6
LIMIT, ALPHA = 7.0, 1.702
OOB = 4096.0

UNIT = 2 * D
NGU = KD
NU = KD + KD // 2
RING = 16
UNROLL = 4
TURNS = UNROLL * NU // RING
EARLY = 2


def moe_block(nc, x, attn_norm_w, w_in, conv_w, a_log, dt_bias, dn_norm_w, pool_w, pool_scale, w_out,
              ffn_norm_w, w_router, b_router, w_gate_up, b_gate_up, w_down, b_down, final_norm_w,
              out, pair_rows):
    ctx = ExitStack()
    with ctx:
        def sb(name, shape, dt=F32):
            return ctx.enter_context(nc.sbuf_tensor(name, shape, dt))

        def sem(name):
            return ctx.enter_context(nc.semaphore(name))

        ring = sb("ring", [P, RING * UNIT])
        late = ring[:, EARLY * UNIT:]

        def room(at, *dims):
            n = 1
            for d in dims:
                n *= d
            flat = late[:, at:at + n]
            if len(dims) == 2:
                return flat.rearrange("p (a b) -> p a b", a=dims[0])
            if len(dims) == 3:
                return flat.rearrange("p (a b c) -> p a b c", a=dims[0], b=dims[1])
            return flat

        qkv = room(0, NQKV, T)
        zs = room(6144, H, T)
        win = room(8192, 2, KD, 256)
        pbuf = room(12288, 4, PAD + T)
        junk = room(14400, D)
        cbuf = [room(14400 + 512 * i, T) for i in range(2)]
        junk2 = room(12288, D)
        wout = room(16384, KD, D)
        AT, QKT, TM, TR, YM, KTS, VTS, KBG = [room(8192 + 512 * i, H, P) for i in range(8)]
        VB, GUM, BI = [room(14400 + 512 * i, H, P) for i in range(3)]
        OSQ, OB = GUM, BI
        h2T = room(0, KD, T)
        braw = room(4096, 3 * D)[0:96, :]
        brem = room(8192, 3 * D)[0:96, :]

        xs = sb("xs", [P, TB, D])
        hbuf = sb("hbuf", [P, KD * T])
        hT = hbuf[:, :].rearrange("p (k t) -> p k t", k=KD)
        h2 = hbuf[:, :].rearrange("p (b d) -> p b d", b=TB)
        cat = sb("cat", [P, KD * T])
        catT = cat[:, :].rearrange("p (k t) -> p k t", k=KD)
        xn = cat[:, :].rearrange("p (b d) -> p b d", b=TB)
        WS = late[:, 24576:28672].rearrange("p (n a b) -> p n a b", n=8, a=H)
        KDZ0, KDZ1, QD0, QD1, VN, UU, WT, DX = [WS[:, i] for i in range(8)]
        EGI = WT
        wsf = room(24576, 8, T)
        ST = sb("ST", [P, 2, H, P])
        cst = sb("cst", [P, 8, P])
        ident, ones, same, lowS, causal, strict, first, second = [cst[:, i, :] for i in range(8)]
        E3 = sb("E3", [96, SLOTS], BF16)
        iotas = room(15936, 3, P).bitcast(I32)
        iotaf = sb("iotaf", [P, T + SLOTS])
        lvl = sb("lvl", [P, 6, P])
        prow = sb("prow", [61, P])
        pcol = sb("pcol", [P, 61])
        NANW, NCV, NDN, NPS = 0, 8, 56, 57
        sm = sb("sm", [P, 48])
        epsc = sb("epsc", [P, 2])
        gt = sb("gt", [P, 12, TB, H])
        gcs = sb("gcs", [P, 4, TB, H])
        gex = sb("gex", [P, 4, TB, H])
        wrt = sb("wrt", [P, KD, E])
        wba = sb("wba", [P, KD, 2 * H])
        bcr = sb("bcr", [P, 2 * H + E])
        shared = sb("shared", [P, 2 * (PAD + T)])
        pool_t = shared[:, :].rearrange("p (a b) -> p a b", a=2)
        fnw = shared[:, 0:D]
        bias3 = cat[0:96, 0:3 * D // 2].bitcast(BF16)
        poolw = sb("poolw", [P, 4, P])
        icnt = sb("icnt", [P, PAD])
        lgs = sb("lgs", [P, TB, E])
        v8 = sb("v8", [P, TB, 8])
        i8 = sb("i8", [P, TB, 8], U32)
        tk = sb("tk", [P, 4, TB, TOPK])
        oh = cat[:, 2560:3072].rearrange("p (n b e) -> p n b e", n=4, b=TB)
        nbi = sb("nbi", [P, E], I32)
        nbf = sb("nbf", [P, 4, E])
        ebc = sb("ebc", [P, 4])
        rowbase = sb("rowbase", [P, TB])
        pidx = sb("pidx", [P, 1])
        rank = sb("rank", [P, TB, E])
        gi = sb("gi", [P, TB, E, 2])
        tab = sb("tab", [1, 2 * E + 2 + 2 * P], I32)
        USED, PAIRS = E + 1 + 2 * P, 2 * E + 1 + 2 * P
        hot = cat[:, 1536:2048].rearrange("p (b q s) -> p b q s", b=TB, q=Q)
        gie = sb("gie", [P, TB, 2])
        selu = sb("selu", [96, SLOTS], BF16)
        seld = sb("seld", [96, SLOTS], BF16)
        xg = cat[:, 2048:2304]
        xgT = cat[:, 2304:2560].rearrange("p (i c) -> p i c", i=2)
        gc = cat[:, 2560:2816]
        sg = cat[:, 2816:3072]
        uc = cat[:, 3072:3328]
        act_ = cat[:, 3328:3584]
        actT = cat[:, 3584:3840].rearrange("p (i c) -> p i c", i=2)
        ys = [cat[:, 3840:4096], sb("ys1", [P, QD])[:, :]]
        wslot = sb("wslot", [P, 2])
        rowf = sb("rowf", [P, 2])
        rowi = sb("rowi", [P, 2], I32)
        qcol = sb("qcol", [P, 1])

        ps = ctx.enter_context(nc.psum_tensor("ps", [P, 8, 512], F32))

        def bank(b, a=None):
            v = ps[:, b, :]
            return v.rearrange("p (a b) -> p a b", a=a) if a else v

        def bc(v, n, at):
            return v.unsqueeze(at).to_broadcast([*v.shape[:at], n, *v.shape[at:]])

        x_in = [sem(f"x_in{i}") for i in range(TB)]
        par_in, wba_in, bc_in, pw_in, wrt_in, fnw_in, wout_in, braw_in = [sem(n) for n in (
            "par_in", "wba_in", "bc_in", "pw_in", "wrt_in", "fnw_in", "wout_in", "braw_in")]
        win_in = [sem(f"win_in{i}") for i in range(2)]
        slot_in = [sem(f"slot_in{i}") for i in range(RING)]
        y_in = [sem(f"y_in{i}") for i in range(TB)]
        iota_ok, const_ok, zero_ok, lvl_ok, pool_step, pool_mix, bias_ok = [sem(n) for n in (
            "iota_ok", "const_ok", "zero_ok", "lvl_ok", "pool_step", "pool_mix", "bias_ok")]
        ssq_ok, std_ok, rstd_ok, xn_ok, pcol_ps, pcol_ok, xt_ps, ht_even, ht_odd = [sem(n) for n in (
            "ssq_ok", "std_ok", "rstd_ok", "xn_ok", "pcol_ps", "pcol_ok", "xt_ps", "ht_even", "ht_odd")]
        proj_ps, tap_ok, conv_step, conv_ok, silu_ok, sq_ok, nrm_ps, nroot_ok, qk_ok, ba_ps = [sem(n) for n in (
            "proj_ps", "tap_ok", "conv_step", "conv_ok", "silu_ok", "sq_ok", "nrm_ps", "nroot_ok", "qk_ok", "ba_ps")]
        dve_step, gin_ok, gexp_in, gln_in, gln_ok, g_ok, gcum_ps, gcs_ok, gex_ok, bkg_ok = [sem(n) for n in (
            "dve_step", "gin_ok", "gexp_in", "gln_in", "gln_ok", "g_ok", "gcum_ps", "gcs_ok", "gex_ok", "bkg_ok")]
        grow_ok, kv_ok, grow_ps, brow_ps, kk_ps, ktok_ps, dx_ok, dexp_ok, delta_step, t_in = [sem(n) for n in (
            "grow_ok", "kv_ok", "grow_ps", "brow_ps", "kk_ps", "ktok_ps", "dx_ok", "dexp_ok", "delta_step", "t_in")]
        r2_ok, t2_ps, t_ok, y_ps, ym_ok, tr_ps, uw_ps, uw_ok, ws_ps, vn_ok, su_ps, st_ok = [sem(n) for n in (
            "r2_ok", "t2_ps", "t_ok", "y_ps", "ym_ok", "tr_ps", "uw_ps", "uw_ok", "ws_ps", "vn_ok", "su_ps", "st_ok")]
        o_ps, osq_ok, oms_ok, ort_ok, on_ok, ot_ps, cat_ok = [sem(n) for n in (
            "o_ps", "osq_ok", "oms_ok", "ort_ok", "on_ok", "ot_ps", "cat_ok")]
        pool_ps, pooled_ok, op_ps, x1_ok, s2_ok, v2_ok, h2_ok, h2t_ps, h2t_lo, lg_ps = [sem(n) for n in (
            "pool_ps", "pooled_ok", "op_ps", "x1_ok", "s2_ok", "v2_ok", "h2_ok", "h2t_ps", "h2t_lo", "lg_ps")]
        route_step, top_ok, texp_ok, mask_ok, rank_ps, ebc_ok, tab_ps, tab_ok, r_ok = [sem(n) for n in (
            "route_step", "top_ok", "texp_ok", "mask_ok", "rank_ps", "ebc_ok", "tab_ps", "tab_ok", "r_ok")]
        info_step, slot_ok, seld_ok, sel_step, hot_ok, gat_ps, idx_ps, xg_ok, xgt_ps, xgt_ok = [sem(n) for n in (
            "info_step", "slot_ok", "seld_ok", "sel_step", "hot_ok", "gat_ps", "idx_ps", "xg_ok", "xgt_ps", "xgt_ok")]
        gub_used, w_used, gc_ok, uc_step, sg_ok, act_ok, at_ps, actt_ok, dnb_used, ys_ok, scat0, scat1 = [sem(n) for n in (
            "gub_used", "w_used", "gc_ok", "uc_step", "sg_ok", "act_ok", "at_ps", "actt_ok", "dnb_used", "ys_ok",
            "scattered_even", "scattered_odd")]
        scat = (scat0, scat1)
        fin_add, fin_sum, fin_sq, fin_rt, fin_rc, fin_o, out_ok, act_step, h2t_hi, t_lvl = [sem(n) for n in (
            "fin_add", "fin_sum", "fin_sq", "fin_rt", "fin_rc", "fin_o", "out_stored", "act_step", "h2t_hi", "t_lvl")]

        def chain(eng, s, start=0):
            n = [0]

            def link(ins):
                n[0] += 1
                ins.then_inc(s, 1)
                eng.wait_ge(s, start + n[0])
            link.n = n
            return link

        def unit_src(e, u):
            if u < NGU:
                return w_gate_up[0, bass.ds(e, 1), u * P:(u + 1) * P, :].rearrange("a p c -> (a p) c")
            c = 2 * (u - NGU)
            return w_down[0, bass.ds(e, 1), c * P:(c + 2) * P, :].rearrange("a (c p) n -> p (a c) n", c=2)

        def unit_dst(slot, u):
            v = ring[:, slot * UNIT:(slot + 1) * UNIT]
            return v if u < NGU else v.rearrange("p (c n) -> p c n", c=2)

        def slot_of(j, u):
            return (NU * j + u) % RING, (NU * j + u) // RING

        block = ctx.enter_context(nc.Block())
        y_pairs = pair_rows.rearrange("(t k q) c -> t (k q c)", k=TOPK, q=Q)
        n_conv = CONV - 1
        DELTA_LINKS = 13
        LEVELS = 5

        @block.sync
        def _(sp):
            def param(row, n, src):
                sp.dma_start(prow[row:row + n, :], src).then_inc(par_in, 16)

            for b in range(TB):
                sp.dma_start(xs[:, b, :], x[0, b * P:(b + 1) * P, :]).then_inc(x_in[b], 16)
            param(NANW, KD, attn_norm_w.rearrange("l (k p) -> (l k) p", p=P))
            for j in range(CONV):
                param(NCV + NQKV * j, NQKV, conv_w[0, j:j + 1, :].rearrange("l (k p) -> (l k) p", p=P))
            param(NDN, 1, dn_norm_w)
            param(NPS, 4, pool_scale.rearrange("l (k p) -> (l k) p", p=P))

            w_in_v = w_in[0].rearrange("(k p) c -> p k c", p=P)

            def load_piece(buf, c0):
                sp.dma_start(win[:, buf], w_in_v[:, :, bass.ds(c0, 256)]).then_inc(win_in[buf], 16)

            load_piece(0, 0)
            load_piece(1, 256)
            sp.dma_start(wba[:, :, :], w_in_v[:, :, C_BA:C_BA + 2 * H]).then_inc(wba_in, 16)
            sp.dma_start(bcr[:, 0:H], dt_bias.to_broadcast([P, H])).then_inc(bc_in, 16)
            sp.dma_start(bcr[:, H:2 * H], a_log.to_broadcast([P, H])).then_inc(bc_in, 16)
            sp.dma_start(bcr[:, 2 * H:], b_router.to_broadcast([P, E])).then_inc(bc_in, 16)
            sp.dma_start(poolw[:, :, :], pool_w[0].rearrange("g c d -> c g d")).then_inc(pw_in, 16)
            sp.dma_start(wrt[:, :, :], w_router[0].rearrange("(k p) e -> p k e", p=P)).then_inc(wrt_in, 16)
            with sp.Fori(0, 2) as i:
                for buf in range(2):
                    sp.wait_ge(proj_ps, 4 * i + 2 * (buf + 1))
                    load_piece(buf, 512 * (i + 1) + 256 * buf)
            for n, c0 in ((6, C_Z), (7, C_Z + 256), (8, C_P), (9, C_P + 256)):
                sp.wait_ge(proj_ps, 2 * (n - 1))
                load_piece(n % 2, c0)
            sp.dma_start(wout[:, :, :], w_out[0].rearrange("(k p) c -> p k c", p=P)).then_inc(wout_in, 16)

            def load_unit(e, u, slot):
                sp.dma_start(unit_dst(slot, u), unit_src(e, u)).then_inc(slot_in[slot], 16)

            for u in range(EARLY):
                load_unit(0, u, u)
            sp.wait_ge(cat_ok, TB)
            sp.wait_ge(pool_mix, 4)
            sp.dma_start(fnw, ffn_norm_w.to_broadcast([P, D])).then_inc(fnw_in, 16)
            for i in range(3):
                sp.dma_start(braw[32 * i:32 * i + 32, 0:2 * D], b_gate_up[0]).then_inc(braw_in, 16)
                sp.dma_start(braw[32 * i:32 * i + 32, 2 * D:], b_down[0]).then_inc(braw_in, 16)
            sp.wait_ge(h2_ok, TB)
            sp.dma_start(fnw, final_norm_w.rearrange("(a n) -> a n", a=1).to_broadcast([P, D])).then_inc(fnw_in, 16)
            sp.wait_ge(lg_ps, 1)
            sp.wait_ge(bias_ok, 1)
            for n in range(EARLY, RING):
                load_unit(n // NU, n % NU, n)
            sp.wait_ge(tab_ok, 1)

            def refill(e, j, used):
                for u in range(NU):
                    nu, ne = (u + RING) % NU, (u + RING) // NU
                    if isinstance(e, int) and e + ne >= E:
                        continue
                    sp.wait_ge(w_used, used + (u + 1))
                    load_unit(e + ne, nu, slot_of(j, u)[0])

            with sp.Fori(0, E // UNROLL - 1) as grp:
                for j in range(UNROLL):
                    used = sp.value_load(tab[0:1, bass.ds(UNROLL * grp + (j + USED), 1)], min_val=0, max_val=MAXB * NU)
                    refill(UNROLL * grp + j, j, used)
            for e in range(E - UNROLL, E):
                used = sp.value_load(tab[0:1, USED + e:USED + e + 1], min_val=0, max_val=MAXB * NU)
                refill(e, e % UNROLL, used)
            pairs = sp.value_load(tab[0:1, PAIRS:PAIRS + 1], min_val=E // 2, max_val=MAXB // 2)
            for s in scat:
                sp.wait_ge(s, pairs * 16)
            for b in range(TB):
                sp.dma_start(ring[:, b * TOPK * D:(b + 1) * TOPK * D], y_pairs[b * P:(b + 1) * P, :]).then_inc(y_in[b], 16)
            for b in range(TB):
                sp.wait_ge(fin_o, b + 1)
                sp.dma_start(out[0, b * P:(b + 1) * P, :], ring[:, b * TOPK * D:b * TOPK * D + D]).then_inc(out_ok, 16)
            sp.wait_ge(out_ok, 16 * TB)

        @block.gpsimd
        def _(pool):
            G = nc.gpsimd
            link = chain(pool, pool_step)
            imprecise = dict(allow_small_or_imprecise_dtypes=True)
            G.iota(iotas[:, 0, :], pattern=[[1, P]], base=0, channel_multiplier=0).then_inc(iota_ok, 1)
            G.iota(iotas[:, 1, :], pattern=[[0, P]], base=0, channel_multiplier=1).then_inc(iota_ok, 1)
            G.iota(iotaf[:, :], pattern=[[1, T + SLOTS]], base=0, channel_multiplier=0, **imprecise).then_inc(iota_ok, 1)
            G.iota(rowbase[:, :], pattern=[[TOPK * P, TB]], base=-int(OOB), channel_multiplier=TOPK,
                   **imprecise).then_inc(iota_ok, 1)
            G.iota(pidx[:, :], pattern=[[0, 1]], base=0, channel_multiplier=1, **imprecise).then_inc(iota_ok, 1)
            G.memset(epsc[:, 0:1], RMS_EPS).then_inc(const_ok, 1)
            G.memset(epsc[:, 1:2], L2_EPS).then_inc(const_ok, 1)
            link(G.memset(ident, 0.0))
            link(G.memset(cst[:, 1, :], 1.0))
            link(G.memset(cst[:, 2, :], 0.0))
            link(G.memset(cst[:, 6:8, :], 0.0))
            for c in range(2):
                r = slice(CH * c, CH * (c + 1))
                link(G.memset(cst[r, 2, r], 1.0))
                link(G.memset(cst[r, 6 + c, :], 1.0))
            G.affine_select(out=ident, in_=ident, compare_op=ALU.not_equal, fill=1.0, base=0,
                            pattern=[[-1, P]], channel_multiplier=1).then_inc(const_ok, 1)
            for dst, src, cmp in ((lowS, ones, ALU.is_gt), (causal, same, ALU.is_ge), (strict, same, ALU.is_gt)):
                G.affine_select(out=dst, in_=src, compare_op=cmp, fill=0.0, base=0,
                                pattern=[[1, P]], channel_multiplier=-1).then_inc(const_ok, 1)
            for g in range(3):
                link(G.memset(E3[32 * g:32 * g + 32, :], 0.0))
                link(G.affine_select(out=E3[32 * g:32 * g + 32, :], in_=E3[32 * g:32 * g + 32, :],
                                     compare_op=ALU.not_equal, fill=1.0, base=0, pattern=[[-1, SLOTS]],
                                     channel_multiplier=1))
            for q in range(Q):
                link(G.memset(qcol[SLOTS * q:SLOTS * (q + 1), :], float(q)))
            link(G.memset(pool_t[:, :, 0:PAD], 0.0))
            link(G.memset(pbuf[:, :, 0:PAD], 0.0))
            link(G.memset(ST[:, :, :, :], 0.0))
            pool.wait_ge(qk_ok, 2 * H)
            G.memset(WS[:, 0:5], 0.0).then_inc(zero_ok, 1)
            pool.wait_ge(lvl_ok, 1)
            for g, w in enumerate(WINDOWS):
                pool.wait_ge(silu_ok, NQKV + H + g + 1)
                src, s, i = pbuf[:, g], 1, 0
                while s < w:
                    dst = pool_t[:, i % 2]
                    link(G.tensor_tensor(dst[:, PAD:], src[:, PAD:], src[:, PAD - s:PAD + T - s], ALU.add))
                    src, s, i = dst, 2 * s, i + 1
                link(G.tensor_scalar(catT[:, H + g, :], src[:, PAD:], 1.0 / w, None, ALU.mult))
                link(G.tensor_tensor(catT[:, H + g, :], catT[:, H + g, :], pbuf[:, g, PAD:], ALU.subtract))
                link(G.tensor_tensor(src[:, PAD:PAD + w], src[:, PAD:PAD + w], icnt[:, 0:w], ALU.mult))
                G.tensor_tensor(catT[:, H + g, 0:w], src[:, PAD:PAD + w], pbuf[:, g, PAD:PAD + w],
                                ALU.subtract).then_inc(pool_mix, 1)
                pool.wait_ge(pool_mix, g + 1)
            pool.wait_ge(braw_in, 6 * 16)
            pool.wait_ge(op_ps, 2 * TB)
            link(G.tensor_copy(bias3[:, :], braw))
            for lo in (32, 64):
                for g in range(lo, 96, 32):
                    r = slice(g, g + 32)
                    link(G.tensor_tensor(brem[r], braw[r] if lo == 32 else brem[r], bias3[r, :], ALU.subtract))
                    last = G.tensor_copy(bias3[r, :], brem[r])
                    if lo == 64:
                        last.then_inc(bias_ok, 1)
                    else:
                        link(last)
            pool.wait_ge(tab_ok, 1)
            pairs = pool.value_load(tab[0:1, PAIRS:PAIRS + 1], min_val=E // 2, max_val=MAXB // 2)
            with pool.Fori(0, pairs) as i:
                for p in range(2):
                    pool.wait_ge(ys_ok, 2 * i + (p + 1))
                    limit = pool.snap(i + (T * TOPK * Q + p))
                    G.indirect_dma_start(
                        out=pair_rows, out_offset=bass.IndirectOffsetOnAxis(ap=rowi[:, p:p + 1], axis=0),
                        in_=ys[p], in_offset=None, bounds_check=limit,
                        oob_is_err=False).then_inc(scat[p], 16)

        @block.scalar
        def _(act):
            A = nc.scalar.activation
            link = chain(act, act_step)

            def row(v):
                return v.rearrange("p a t -> p (a t)")

            for b in range(TB):
                act.wait_ge(x_in[b], 16)
                link(A(junk, xs[:, b, :], ACT.Square, accum_out=sm[:, b:b + 1]))
            act.wait_ge(const_ok, 2)
            A(sm[:, 4:8], sm[:, 0:4], ACT.Sqrt, scale=1.0 / D, bias=epsc[:, 0:1]).then_inc(std_ok, 1)
            act.wait_ge(pcol_ok, 1)
            for k in range(0, KD, 2):
                act.wait_ge(xt_ps, k + 1)
                A(hT[:, k, :], bank(k), ACT.Copy, scale=pcol[:, NANW + k:NANW + k + 1]).then_inc(ht_even, 1)
            with act.Fori(0, 3) as i:
                for r in range(4):
                    n = 4 * i + r
                    act.wait_ge(proj_ps, n + 1)
                    A(cbuf[r % 2], bank(r % 2), ACT.Copy,
                      scale=pcol[:, bass.ds(n + (NCV + n_conv * NQKV), 1)]).then_inc(tap_ok, 1)
                    act.wait_ge(conv_ok, n + 1)
                    A(row(qkv[:, bass.ds(n, 1), :]), cbuf[r % 2], ACT.Silu).then_inc(silu_ok, 1)
            for n in range(NQKV, NQKV + 2 * H):
                act.wait_ge(proj_ps, n + 1)
                if n < NQKV + H:
                    A(zs[:, n - NQKV, :], bank(n % 2), ACT.Silu).then_inc(silu_ok, 1)
                else:
                    A(pbuf[:, n - NQKV - H, PAD:], bank(n % 2), ACT.Copy).then_inc(silu_ok, 1)
            for n in range(2 * H):
                act.wait_ge(nrm_ps, n + 1)
                A(wsf[:, n], bank(n), ACT.Sqrt, bias=epsc[:, 1:2]).then_inc(nroot_ok, 1)
            act.wait_ge(gin_ok, 1)
            A(gt[:, 2], gt[:, 1], ACT.Exp).then_inc(gexp_in, 1)
            A(gt[:, 3], gt[:, 10], ACT.Exp, scale=-1.0).then_inc(gexp_in, 1)
            act.wait_ge(bc_in, 48)
            A(gt[:, 4, 0, :], bcr[:, H:2 * H], ACT.Exp).then_inc(gexp_in, 1)
            act.wait_ge(gln_in, 1)
            A(gt[:, 6], gt[:, 5], ACT.Ln).then_inc(gln_ok, 1)
            act.wait_ge(gcs_ok, 1)
            A(gex[:, :, :, :], gcs[:, :, :, :], ACT.Exp).then_inc(gex_ok, 1)
            with act.Fori(0, TB) as tb:
                tok = bass.ds(tb * P, P)
                act.wait_ge(cat_ok, tb)
                A(KTS, qkv[:, H:2 * H, tok], ACT.Copy).then_inc(kv_ok, 1)
                A(VTS, qkv[:, 2 * H:3 * H, tok], ACT.Copy).then_inc(kv_ok, 1)
                act.wait_ge(grow_ps, tb + 1)
                A(EGI, bank(0, H), ACT.Exp).then_inc(dexp_ok, 1)
                act.wait_ge(dx_ok, tb + 1)
                A(DX, DX, ACT.Exp).then_inc(dexp_ok, 1)
                act.wait_ge(t2_ps, tb + 1)
                A(TM, bank(6, H), ACT.Copy).then_inc(t_ok, 1)
                act.wait_ge(uw_ps, tb * 2 + 1)
                act.wait_ge(t_in, tb + 1)
                A(UU, bank(1, H), ACT.Copy).then_inc(uw_ok, 1)
                act.wait_ge(uw_ps, tb * 2 + 2)
                A(WT, bank(2, H), ACT.Copy).then_inc(uw_ok, 1)
                act.wait_ge(o_ps, tb + 1)
                A(OSQ, bank(5, H), ACT.Square).then_inc(osq_ok, 1)
                act.wait_ge(oms_ok, tb + 1)
                A(sm[:, 16:20], sm[:, 12:16], ACT.Sqrt, scale=1.0 / P, bias=epsc[:, 0:1]).then_inc(ort_ok, 1)
            for g in range(4):
                act.wait_ge(pool_ps, g + 1)
                A(catT[:, H + g, :], bank(g), ACT.Copy, scale=pcol[:, NPS + g:NPS + g + 1]).then_inc(pooled_ok, 1)
            for b in range(TB):
                act.wait_ge(x1_ok, 2 * b + 2)
                link(A(junk2, xs[:, b, :], ACT.Square, accum_out=sm[:, 20 + b:21 + b]))
                A(sm[:, 24 + b:25 + b], sm[:, 20 + b:21 + b], ACT.Sqrt, scale=1.0 / D, bias=epsc[:, 0:1]).then_inc(s2_ok, 1)
            for n in range(1, 2 * TB, 2):
                act.wait_ge(h2t_ps, n + 1)
                A(h2T[:, 4:8, (n // 2) * P:(n // 2 + 1) * P], bank(2 * (n // 2 % 2) + 1, 4), ACT.Copy).then_inc(h2t_hi, 1)
            act.wait_ge(top_ok, 1)
            A(tk[:, 1], tk[:, 2], ACT.Exp).then_inc(texp_ok, 1)

            act.wait_ge(gat_ps, 1)
            A(xg[:, :], ps[:, 2, 0:QD], ACT.Copy).then_inc(xg_ok, 1)
            act.wait_ge(xgt_ps, 1)
            A(xgT[:, :, :], bank(3, 4)[:, 0:2, :], ACT.Copy).then_inc(xgt_ok, 1)
            act.wait_ge(tab_ok, 1)
            pairs = act.value_load(tab[0:1, PAIRS:PAIRS + 1], min_val=E // 2, max_val=MAXB // 2)

            def activate(g, i, p):
                act.wait_ge(gc_ok, g + 1)
                act.wait_ge(act_ok, g)
                A(sg[:, :], gc[:, :], ACT.Sigmoid, scale=ALPHA).then_inc(sg_ok, 1)
                act.wait_ge(gat_ps, g + 2)
                act.wait_ge(xgt_ps, g + 1)
                A(xg[:, :], ps[:, 2, 0:QD], ACT.Copy).then_inc(xg_ok, 1)
                act.wait_ge(at_ps, g + 1)
                act.wait_ge(w_used, g * NU)
                A(actT[:, :, :], bank(4, 4)[:, 0:2, :], ACT.Copy).then_inc(actt_ok, 1)
                act.wait_ge(xgt_ps, g + 2)
                act.wait_ge(w_used, g * NU + NGU)
                A(xgT[:, :, :], bank(3, 4)[:, 0:2, :], ACT.Copy).then_inc(xgt_ok, 1)
                act.wait_ge(w_used, g * NU + NU)
                act.wait_ge(slot_ok, g + 1)
                act.wait_ge(scat[p], i * 16)
                A(ys[p], ps[:, 1, 0:QD], ACT.Copy, scale=wslot[:, p:p + 1]).then_inc(ys_ok, 1)

            with act.Fori(0, pairs) as i:
                for p in range(2):
                    activate(2 * i + p, i, p)
            for b in range(TB):
                act.wait_ge(fin_sum, b + 1)
                base = b * TOPK * D + D
                A(ring[:, base:base + D], xs[:, b, :], ACT.Square, accum_out=sm[:, 28 + b:29 + b]).then_inc(fin_sq, 1)
                act.wait_ge(fin_sq, b + 1)
                A(sm[:, 32 + b:33 + b], sm[:, 28 + b:29 + b], ACT.Sqrt, scale=1.0 / D, bias=epsc[:, 0:1]).then_inc(fin_rt, 1)

        @block.vector
        def _(dve):
            V = nc.vector
            link = chain(dve, dve_step)

            def step(ins, s, count):
                ins.then_inc(s, 1)
                dve.wait_ge(s, count)

            dve.wait_ge(pcol_ps, 1)
            step(V.tensor_copy(pcol[:, :], ps[:, 7, 0:61]), pcol_ok, 1)
            dve.wait_ge(std_ok, 1)
            step(V.reciprocal(sm[:, 8:12], sm[:, 4:8]), rstd_ok, 1)
            for b in range(TB):
                V.tensor_scalar(xn[:, b, :], xs[:, b, :], sm[:, 8 + b:9 + b], None, ALU.mult).then_inc(xn_ok, 1)
            dve.wait_ge(iota_ok, 5)
            link(V.tensor_tensor(iotas[:, 2, :], iotas[:, 0, :], iotas[:, 1, :], ALU.bitwise_xor))
            for s in range(6):
                link(V.tensor_scalar(iotas[:, 0, :], iotas[:, 2, :], s, None, ALU.logical_shift_right))
                link(V.tensor_scalar(lvl[:, s, :], iotas[:, 0, :], 1, None, ALU.is_equal))
            dve.wait_ge(const_ok, 6)
            link(V.tensor_tensor(lvl[:, 0, :], lvl[:, 0, :], strict, ALU.mult))
            for s in range(1, 6):
                link(V.tensor_scalar(nbf[:, :, :].rearrange("p a b -> p (a b)"), causal, -1.0, 1.0, ALU.mult, ALU.add))
                link(V.tensor_tensor(lvl[:, s, :], lvl[:, s, :], nbf[:, :, :].rearrange("p a b -> p (a b)"), ALU.mult))
            link(V.tensor_scalar(icnt[:, :], iotaf[:, 0:PAD], 1.0, None, ALU.add))
            V.reciprocal(icnt[:, :], icnt[:, :]).then_inc(lvl_ok, 1)
            for k in range(1, KD, 2):
                dve.wait_ge(xt_ps, k + 1)
                V.tensor_scalar(hT[:, k, :], bank(k), pcol[:, NANW + k:NANW + k + 1], None, ALU.mult).then_inc(ht_odd, 1)

            def conv(n, b, base):
                t = cbuf[b]
                dve.wait_ge(tap_ok, n + 1)
                for m in range(1, CONV):
                    ins = V.scalar_tensor_tensor(
                        out=t[:, m:], in0=bank(b)[:, 0:T - m], scalar=pcol[:, bass.ds(n + (NCV + (n_conv - m) * NQKV), 1)],
                        in1=t[:, m:], op0=ALU.mult, op1=ALU.add)
                    if m < n_conv:
                        step(ins, conv_step, base + m)
                    else:
                        ins.then_inc(conv_ok, 1)

            with dve.Fori(0, 3) as i:
                for r in range(4):
                    conv(4 * i + r, r % 2, (4 * i + r) * (n_conv - 1))
            for n in range(2 * H):
                dve.wait_ge(silu_ok, n + 1)
                V.tensor_tensor(wsf[:, n], qkv[:, n, :], qkv[:, n, :], ALU.mult).then_inc(sq_ok, 1)
            for n in range(2 * H):
                dve.wait_ge(nroot_ok, n + 1)
                link(V.reciprocal(wsf[:, n], wsf[:, n]))
                V.scalar_tensor_tensor(out=qkv[:, n, :], in0=qkv[:, n, :], scalar=float(P) ** -0.5 if n < H else 1.0,
                                       in1=wsf[:, n], op0=ALU.mult, op1=ALU.mult).then_inc(qk_ok, 1)
            dve.wait_ge(ba_ps, 1)
            dve.wait_ge(bc_in, 48)
            ba = ps[:, 0, 0:TB * 2 * H].rearrange("p (b c) -> p b c", b=TB)
            link(V.tensor_copy(gt[:, 10], ba[:, :, 0:H]))
            link(V.tensor_tensor(gt[:, 0], ba[:, :, H:], bc(bcr[:, 0:H], TB, 1), ALU.add))
            link(V.tensor_scalar(gt[:, 1], gt[:, 0], -1.0, None, ALU.mult))
            step(V.tensor_tensor(gt[:, 1], gt[:, 1], gt[:, 0], ALU.min), gin_ok, 1)
            dve.wait_ge(gexp_in, 3)
            step(V.tensor_scalar(gt[:, 5], gt[:, 2], 1.0, None, ALU.add), gln_in, 1)
            link(V.tensor_scalar(gt[:, 7], gt[:, 5], -1.0, None, ALU.add))
            link(V.tensor_tensor(gt[:, 7], gt[:, 2], gt[:, 7], ALU.subtract))
            link(V.reciprocal(gt[:, 11], gt[:, 5]))
            link(V.tensor_tensor(gt[:, 7], gt[:, 7], gt[:, 11], ALU.mult))
            link(V.tensor_scalar(gt[:, 0], gt[:, 0], 0.0, None, ALU.max))
            dve.wait_ge(gln_ok, 1)
            link(V.tensor_tensor(gt[:, 7], gt[:, 7], gt[:, 6], ALU.add))
            link(V.tensor_tensor(gt[:, 7], gt[:, 7], gt[:, 0], ALU.add))
            step(V.scalar_tensor_tensor(out=gt[:, 8], in0=gt[:, 7], scalar=-1.0, in1=bc(gt[:, 4, 0, :], TB, 1),
                                        op0=ALU.mult, op1=ALU.mult), g_ok, 1)
            link(V.tensor_scalar(gt[:, 9], gt[:, 3], 1.0, None, ALU.add))
            link(V.reciprocal(gt[:, 9], gt[:, 9]))
            dve.wait_ge(gcum_ps, 1)
            cum = ps[:, 1, 0:4 * TB * H].rearrange("p (n b h) -> p n b h", n=4, b=TB)
            link(V.tensor_copy(gcs[:, :, :, :], cum))
            step(V.tensor_tensor(gcs[:, 1], gcs[:, 1], gcs[:, 0], ALU.subtract), gcs_ok, 1)
            dve.wait_ge(gex_ok, 1)
            link(V.tensor_tensor(gt[:, 11], gex[:, 0], gt[:, 9], ALU.mult))
            dve.wait_ge(zero_ok, 1)

            with dve.Fori(0, TB) as tb:
                lk = chain(dve, delta_step, tb * DELTA_LINKS)
                tok = bass.ds(tb * P, P)

                def col(v, parts=slice(0, P)):
                    return bc(v[parts, bass.ds(tb, 1), :].rearrange("p a h -> p (a h)"), P, 2)

                def done(ins, s, k=1, n=1):
                    step(ins, s, tb * n + k)

                done(V.tensor_tensor(GUM, bc(causal, H, 1), col(gt[:, 8]), ALU.mult), grow_ok, 1, 2)
                done(V.tensor_tensor(BI, bc(ident, H, 1), col(gt[:, 9]), ALU.mult), grow_ok, 2, 2)
                dve.wait_ge(dexp_ok, 2 * tb + 1)
                lk(V.tensor_tensor(DX, bank(0, H), col(gcs[:, 0]), ALU.subtract))
                done(V.tensor_scalar(DX, DX, 0.0, None, ALU.min), dx_ok)
                dve.wait_ge(dexp_ok, 2 * tb + 2)
                dve.wait_ge(kk_ps, tb + 1)
                lk(V.tensor_tensor(DX, DX, bc(causal, H, 1), ALU.mult))
                lk(V.tensor_tensor(QKT, bank(3, H), DX, ALU.mult))
                lk(V.tensor_tensor(AT, bank(2, H), DX, ALU.mult))
                lk(V.tensor_tensor(AT, AT, bank(1, H), ALU.mult))
                lk(V.tensor_tensor(AT, AT, bc(strict, H, 1), ALU.mult))
                lk(V.tensor_tensor(YM, AT, bc(lvl[:, 0, :], H, 1), ALU.mult))
                done(V.tensor_tensor(TR, bc(ident, H, 1), YM, ALU.subtract), r2_ok)
                lk(V.tensor_tensor(QD0[:, :, 0:CH], qkv[:, 0:H, bass.ds(tb * P, CH)], EGI[:, :, 0:CH], ALU.mult))
                done(V.tensor_tensor(QD1[:, :, CH:], qkv[:, 0:H, bass.ds(tb * P + CH, CH)], EGI[:, :, CH:],
                                     ALU.mult), t_in)
                dve.wait_ge(ktok_ps, tb + 1)
                lk(V.tensor_tensor(KBG, bank(4, H), col(gt[:, 11]), ALU.mult))
                lk(V.tensor_tensor(KDZ0[0:CH], bank(4, H)[0:CH], col(gex[:, 1], slice(0, CH)), ALU.mult))
                lk(V.tensor_tensor(KDZ1[CH:], bank(4, H)[CH:], col(gex[:, 1], slice(CH, P)), ALU.mult))
                lk(V.tensor_tensor(VB, bank(5, H), col(gt[:, 9]), ALU.mult))
                dve.wait_ge(t_ok, tb + 1)
                for s in range(LEVELS):
                    for a in range(2):
                        dve.wait_ge(y_ps, tb * 2 * LEVELS + 2 * s + a + 1)
                        V.tensor_tensor(YM[:, 2 * a:2 * a + 2], bank(6 - 3 * a, H)[:, 0:2], bc(lvl[:, s + 1, :], 2, 1),
                                        ALU.mult).then_inc(ym_ok, 1)
                    for a in range(2):
                        dve.wait_ge(tr_ps, tb * 2 * LEVELS + 2 * s + a + 1)
                        hp = slice(2 * a, 2 * a + 2)
                        if s < LEVELS - 1:
                            V.tensor_tensor(TM[:, hp], TM[:, hp], bank((7, 1)[a], H)[:, 0:2], ALU.subtract).then_inc(t_lvl, 1)
                        V.tensor_tensor(TR[:, hp], TR[:, hp], bank((0, 2)[a], H)[:, 0:2], ALU.subtract).then_inc(r_ok, 1)
                    if s < LEVELS - 1:
                        dve.wait_ge(t_lvl, tb * 2 * (LEVELS - 1) + 2 * s + 2)
                    dve.wait_ge(r_ok, tb * 2 * LEVELS + 2 * s + 2)
                dve.wait_ge(uw_ok, 2 * tb + 2)
                for c in range(2):
                    r = slice(CH * c, CH * (c + 1))
                    dve.wait_ge(ws_ps, 2 * tb + c + 1)
                    done(V.tensor_tensor(VN[r], UU[r], bank(3, H)[r], ALU.subtract), vn_ok, c + 1, 2)
                    dve.wait_ge(su_ps, 2 * tb + c + 1)
                    if c:
                        dve.wait_ge(o_ps, tb + 1)
                    for h in range(H):
                        ins = V.scalar_tensor_tensor(
                            out=ST[:, 1 - c, h, :], in0=ST[:, c, h, :],
                            scalar=gex[:, 2 + c, bass.ds(tb, 1), h:h + 1].rearrange("p a b -> p (a b)"),
                            in1=bank(4, H)[:, h, :], op0=ALU.mult, op1=ALU.add)
                        ins.then_inc(st_ok, 1)
                    dve.wait_ge(st_ok, (2 * tb + c + 1) * H)
                dve.wait_ge(osq_ok, tb + 1)
                done(V.tensor_reduce(sm[:, 12:16], OSQ, AX.X, ALU.add), oms_ok)
                dve.wait_ge(ort_ok, tb + 1)
                lk(V.reciprocal(sm[:, 36:40], sm[:, 16:20]))
                done(V.tensor_tensor(OB, bank(5, H), bc(sm[:, 36:40], P, 2), ALU.mult), on_ok)
                dve.wait_ge(ot_ps, tb + 1)
                done(V.scalar_tensor_tensor(out=catT[:, 0:H, tok], in0=bank(6, H), scalar=pcol[:, NDN:NDN + 1],
                                            in1=zs[:, :, tok], op0=ALU.mult, op1=ALU.mult), cat_ok)
                assert lk.n[0] == DELTA_LINKS
            dve.wait_ge(fnw_in, 16)
            for b in range(TB):
                for half in range(2):
                    n = 2 * b + half
                    dve.wait_ge(op_ps, n + 1)
                    v = xs[:, b, 512 * half:512 * (half + 1)]
                    V.tensor_tensor(v, v, bank(4 + n % 4), ALU.add).then_inc(x1_ok, 1)
                dve.wait_ge(x1_ok, 2 * b + 2)
                dve.wait_ge(s2_ok, b + 1)
                link(V.reciprocal(sm[:, 40 + b:41 + b], sm[:, 24 + b:25 + b]))
                V.scalar_tensor_tensor(out=h2[:, b, :], in0=xs[:, b, :], scalar=sm[:, 40 + b:41 + b], in1=fnw,
                                       op0=ALU.mult, op1=ALU.mult).then_inc(h2_ok, 1)
            for n in range(0, 2 * TB, 2):
                dve.wait_ge(h2t_ps, n + 1)
                V.tensor_copy(h2T[:, 0:4, (n // 2) * P:(n // 2 + 1) * P], bank(2 * (n // 2 % 2), 4)).then_inc(h2t_lo, 1)
            dve.wait_ge(lg_ps, 1)
            link(V.tensor_tensor(lgs[:, :, :], ps[:, 0, 0:TB * E].rearrange("p (b e) -> p b e", b=TB),
                                 bc(bcr[:, 2 * H:], TB, 1), ALU.add))
            for b in range(TB):
                link(V.max(out=v8[:, b, :], in_=lgs[:, b, :]))
                link(V.max_index(i8[:, b, :], v8[:, b, :], lgs[:, b, :]))
            link(V.tensor_copy(tk[:, 0], i8[:, :, 0:TOPK]))
            step(V.tensor_tensor(tk[:, 2], v8[:, :, 0:TOPK], bc(v8[:, :, 0], TOPK, 2), ALU.subtract), top_ok, 1)
            link(V.memset(oh[:, 2:4], 0.0))
            link(V.memset(gi[:, :, :, :], 0.0))
            dve.wait_ge(texp_ok, 1)
            link(V.tensor_reduce(nbf[:, 0, 0:TB], tk[:, 1], AX.X, ALU.add))
            link(V.reciprocal(nbf[:, 0, 8:8 + TB], nbf[:, 0, 0:TB]))
            link(V.tensor_tensor(tk[:, 3], tk[:, 1], bc(nbf[:, 0, 8:8 + TB], TOPK, 2), ALU.mult))
            for k in range(TOPK):
                link(V.tensor_tensor(oh[:, 0], bc(iotaf[:, 0:E], TB, 1), bc(tk[:, 0, :, k], E, 2), ALU.is_equal))
                link(V.tensor_tensor(oh[:, 1], oh[:, 0], bc(tk[:, 3, :, k], E, 2), ALU.mult))
                link(V.tensor_tensor(gi[:, :, :, 0], gi[:, :, :, 0], oh[:, 1], ALU.add))
                link(V.scalar_tensor_tensor(out=oh[:, 3], in0=oh[:, 0], scalar=float(k), in1=oh[:, 3],
                                            op0=ALU.mult, op1=ALU.add))
                ins = V.tensor_tensor(oh[:, 2], oh[:, 2], oh[:, 0], ALU.add)
                if k < TOPK - 1:
                    link(ins)
                else:
                    step(ins, mask_ok, 1)
            link(V.tensor_tensor(oh[:, 1], oh[:, 2], bc(rowbase[:, :], E, 2), ALU.mult))
            link(V.tensor_tensor(gi[:, :, :, 1], oh[:, 1], oh[:, 3], ALU.add))
            dve.wait_ge(rank_ps, 1)
            rk = ps[:, 1, 0:TB * E].rearrange("p (b e) -> p b e", b=TB)
            link(V.tensor_scalar(rank[:, :, :], rk, 1.0, None, ALU.add))
            link(V.tensor_tensor(rank[:, :, :], rank[:, :, :], oh[:, 2], ALU.mult))
            link(V.tensor_scalar(rank[:, :, :], rank[:, :, :], -1.0, None, ALU.add))
            link(V.tensor_scalar(nbf[:, 0, :], ps[:, 1, TB * E:(TB + 1) * E], float(SLOTS - 1), None, ALU.add))
            link(V.tensor_copy(nbi[:, :], nbf[:, 0, :]))
            link(V.tensor_scalar(nbi[:, :], nbi[:, :], SLOTS.bit_length() - 1, None, ALU.arith_shift_right))
            link(V.tensor_copy(nbf[:, 0, :], nbi[:, :]))
            link(V.tensor_scalar(nbf[:, 0, :], nbf[:, 0, :], 1.0, None, ALU.max))
            link(V.memset(nbf[:, 1, :], 1.0))
            link(V.tensor_tensor_scan(out=nbf[:, 2, :], data0=nbf[:, 1, :], data1=nbf[:, 0, :], initial=0.0,
                                      op0=ALU.mult, op1=ALU.add))
            link(V.tensor_scalar(nbf[:, 3, :], nbf[:, 2, :], pidx[:, 0:1], None, ALU.is_le))
            link(V.tensor_reduce(ebc[:, 0:1], nbf[:, 3, :], AX.X, ALU.add))
            link(V.tensor_tensor(nbf[:, 3, :], nbf[:, 3, :], nbf[:, 2, :], ALU.mult))
            link(V.tensor_reduce(ebc[:, 1:2], nbf[:, 3, :], AX.X, ALU.max))
            link(V.tensor_tensor(ebc[:, 3:4], pidx[:, 0:1], ebc[:, 1:2], ALU.subtract))
            link(V.tensor_scalar(ebc[:, 2:3], ebc[:, 0:1], float(E), float(T), ALU.is_ge, ALU.mult))
            link(V.scalar_tensor_tensor(out=ebc[:, 3:4], in0=ebc[:, 3:4], scalar=float(SLOTS), in1=ebc[:, 2:3],
                                        op0=ALU.mult, op1=ALU.add))
            link(V.tensor_scalar(ebc[:, 1:2], ebc[:, 3:4], float(T), None, ALU.min))
            step(V.tensor_scalar(ebc[:, 0:1], ebc[:, 0:1], float(E - 1), None, ALU.min), ebc_ok, 1)
            link(V.memset(tab[0:1, 0:1], 0))
            link(V.tensor_copy(tab[0:1, 1:E + 1], nbf[0:1, 2, :]))
            dve.wait_ge(tab_ps, 1)
            link(V.tensor_copy(tab[0:1, E + 1:USED], ps[0:1, 2, 0:2 * P]))
            link(V.tensor_scalar(tab[0:1, USED:PAIRS], nbf[0:1, 2, :], float(NU), float(-NU), ALU.mult, ALU.add))
            link(V.tensor_scalar(tab[0:1, E:E + 1], nbf[0:1, 2, E - 1:E], 1.0, None, ALU.add))
            link(V.tensor_scalar(tab[0:1, PAIRS:], tab[0:1, E:E + 1], 1, None, ALU.arith_shift_right))
            step(V.tensor_scalar(tab[0:1, E:E + 1], tab[0:1, PAIRS:], 1, None, ALU.arith_shift_left), tab_ok, 1)

            def make_hot(g, count):
                e = dve.value_load(tab[0:1, bass.ds(g + (E + 1), 1)], min_val=0, max_val=E - 1)
                s0 = dve.value_load(tab[0:1, bass.ds(g + (E + 1 + P), 1)], min_val=0, max_val=T)
                V.tensor_copy(selu[:, :], E3[:, bass.ds(e, 1)].to_broadcast([96, SLOTS])).then_inc(sel_step, 1)
                V.tensor_copy(gie[:, :, :], gi[:, :, bass.ds(e, 1), :].rearrange("p b a c -> p b (a c)")).then_inc(sel_step, 1)
                slots = bc(bc(iotaf[:, bass.ds(s0, SLOTS)], Q, 1), TB, 1)
                mine = bc(bc(rank[:, :, bass.ds(e, 1)].rearrange("p b a -> p (b a)"), Q, 2), SLOTS, 3)
                dve.wait_ge(sel_step, count * 2)
                step(V.tensor_tensor(hot[:, :, :, :], slots, mine, ALU.is_equal), hot_ok, count)

            make_hot(0, 1)
            pairs = dve.value_load(tab[0:1, PAIRS:PAIRS + 1], min_val=E // 2, max_val=MAXB // 2)

            def swiglu(g, i, p):
                dve.wait_ge(idx_ps, g + 1)
                dve.wait_ge(scat[p], i * 16)
                V.tensor_copy(wslot[:, p:p + 1], ps[:, 7, 0:1]).then_inc(info_step, 1)
                step(V.tensor_scalar(rowf[:, p:p + 1], ps[:, 7, 1:2], OOB, float(Q), ALU.add, ALU.mult), info_step, g * 3 + 2)
                step(V.tensor_tensor(rowf[:, p:p + 1], rowf[:, p:p + 1], qcol[:, :], ALU.add), info_step, g * 3 + 3)
                V.tensor_copy(rowi[:, p:p + 1], rowf[:, p:p + 1]).then_inc(slot_ok, 1)
                dve.wait_ge(dnb_used, g)
                step(V.tensor_copy(seld[:, :], selu[:, :]), seld_ok, g + 1)
                dve.wait_ge(gub_used, g + 1)
                make_hot(g + 1, g + 2)
                dve.wait_ge(w_used, g * NU + NGU)
                step(V.tensor_scalar(gc[:, :], ps[:, 0, 0:QD], LIMIT, None, ALU.min), gc_ok, g + 1)
                step(V.tensor_scalar(uc[:, :], ps[:, 0, QD:], -LIMIT, LIMIT, ALU.max, ALU.min), uc_step, g * 2 + 1)
                step(V.scalar_tensor_tensor(out=uc[:, :], in0=uc[:, :], scalar=1.0, in1=gc[:, :], op0=ALU.add,
                                            op1=ALU.mult), uc_step, g * 2 + 2)
                dve.wait_ge(sg_ok, g + 1)
                dve.wait_ge(at_ps, g)
                step(V.tensor_tensor(act_[:, :], uc[:, :], sg[:, :], ALU.mult), act_ok, g + 1)

            with dve.Fori(0, pairs) as i:
                for p in range(2):
                    swiglu(2 * i + p, i, p)
            dve.wait_ge(fnw_in, 32)
            for b in range(TB):
                dve.wait_ge(y_in[b], 16)
                for k in range(TOPK):
                    y = ring[:, (b * TOPK + k) * D:(b * TOPK + k + 1) * D]
                    ins = V.tensor_tensor(xs[:, b, :], xs[:, b, :], y, ALU.add)
                    if k < TOPK - 1:
                        step(ins, fin_add, b * (TOPK - 1) + k + 1)
                    else:
                        step(ins, fin_sum, b + 1)
            for b in range(TB):
                dve.wait_ge(fin_rt, b + 1)
                step(V.reciprocal(sm[:, 44 + b:45 + b], sm[:, 32 + b:33 + b]), fin_rc, b + 1)
                V.scalar_tensor_tensor(out=ring[:, b * TOPK * D:b * TOPK * D + D], in0=xs[:, b, :],
                                       scalar=sm[:, 44 + b:45 + b], in1=fnw, op0=ALU.mult,
                                       op1=ALU.mult).then_inc(fin_o, 1)

        @block.tensor
        def _(pe):
            mm, tr = nc.tensor.matmul, nc.tensor.transpose
            pe.wait_ge(const_ok, 6)
            pe.wait_ge(par_in, 16 * (3 + CONV))
            tr(ps[:, 7, 0:61], prow[:, :], ident[0:61, 0:61]).then_inc(pcol_ps, 1)
            pe.wait_ge(pcol_ok, 1)
            pe.wait_ge(xn_ok, TB)
            for k in range(KD):
                for b in range(TB):
                    last = tr(bank(k)[:, b * P:(b + 1) * P], xn[:, b, k * P:(k + 1) * P], ident)
                last.then_inc(xt_ps, 1)
            pe.wait_ge(ht_even, KD // 2)
            pe.wait_ge(ht_odd, KD // 2)

            def project(buf, half, b):
                for k in range(KD):
                    last = mm(bank(b), win[:, buf, k, half * P:(half + 1) * P], hT[:, k, :], start=k == 0, stop=k == KD - 1)
                last.then_inc(proj_ps, 1)

            with pe.Fori(0, 3) as i:
                for r in range(4):
                    n = 4 * i + r
                    if r % 2 == 0:
                        pe.wait_ge(win_in[r // 2], i * 16 + 16)
                    project(r // 2, r % 2, r % 2)
                    pe.wait_ge(conv_ok, n)
            for n in range(NQKV, NQKV + 2 * H):
                piece = n // 2
                if n % 2 == 0:
                    pe.wait_ge(win_in[piece % 2], (piece // 2 + 1) * 16)
                if n == NQKV + 1:
                    pe.wait_ge(conv_ok, NQKV)
                if n > NQKV + 1:
                    pe.wait_ge(silu_ok, n - 1)
                project(piece % 2, n % 2, n % 2)
            for n in range(2 * H):
                pe.wait_ge(sq_ok, n + 1)
                if n < 2:
                    pe.wait_ge(silu_ok, NQKV + 2 * H - 1 + n)
                mm(bank(n), ones, wsf[:, n], start=True, stop=True).then_inc(nrm_ps, 1)
            pe.wait_ge(wba_in, 16)
            pe.wait_ge(nroot_ok, 2)
            for b in range(TB):
                for k in range(KD):
                    last = mm(ps[:, 0, b * 2 * H:(b + 1) * 2 * H], hT[:, k, b * P:(b + 1) * P], wba[:, k, :],
                              start=k == 0, stop=k == KD - 1)
            last.then_inc(ba_ps, 1)
            pe.wait_ge(g_ok, 1)
            for i, c in enumerate((causal, same, first, second)):
                last = mm(ps[:, 1, i * TB * H:(i + 1) * TB * H], c, gt[:, 8].rearrange("p b h -> p (b h)"),
                          start=True, stop=True)
            last.then_inc(gcum_ps, 1)
            pe.wait_ge(qk_ok, 2 * H)
            pe.wait_ge(zero_ok, 1)
            pe.wait_ge(gcs_ok, 1)

            with pe.Fori(0, TB) as tb:
                def heads(b, f, s, more=()):
                    for h in range(H):
                        lhsT, rhs = f(h)
                        last = mm(bank(b, H)[:, h, :], lhsT, rhs, start=True, stop=not more)
                    last.then_inc(s, 1)

                def flat(v):
                    return v.rearrange("p a b -> p (a b)")

                def now(n, h):
                    return qkv[:, n + h, bass.ds(tb * P, P)]

                pe.wait_ge(grow_ok, 2 * tb + 1)
                mm(bank(0), ones, flat(GUM), start=True, stop=True).then_inc(grow_ps, 1)
                pe.wait_ge(grow_ok, 2 * tb + 2)
                mm(bank(1), ones, flat(BI), start=True, stop=True).then_inc(brow_ps, 1)
                pe.wait_ge(kv_ok, 2 * tb + 2)
                for h in range(H):
                    mm(bank(2, H)[:, h, :], KTS[:, h, :], now(H, h), start=True, stop=True)
                heads(3, lambda h: (KTS[:, h, :], now(0, h)), kk_ps)
                for h in range(H):
                    tr(bank(4, H)[:, h, :], KTS[:, h, :], ident)
                for h in range(H):
                    last = tr(bank(5, H)[:, h, :], VTS[:, h, :], ident)
                last.then_inc(ktok_ps, 1)
                pe.wait_ge(r2_ok, tb + 1)
                for h in range(H):
                    last = tr(bank(6, H)[:, h, :], TR[:, h, :], ident)
                last.then_inc(t2_ps, 1)
                pe.wait_ge(t_ok, tb + 1)
                for s in range(LEVELS):
                    for a in range(2):
                        if s:
                            pe.wait_ge(t_lvl, tb * 2 * (LEVELS - 1) + 2 * s - 1 + a)
                            pe.wait_ge(r_ok, tb * 2 * LEVELS + 2 * s - 1 + a)
                        for i in range(2):
                            last = mm(bank(6 - 3 * a, H)[:, i, :], AT[:, 2 * a + i, :], TM[:, 2 * a + i, :],
                                      start=True, stop=True)
                        last.then_inc(y_ps, 1)
                    for a in range(2):
                        pe.wait_ge(ym_ok, tb * 2 * LEVELS + 2 * s + a + 1)
                        if s < LEVELS - 1:
                            for i in range(2):
                                mm(bank((7, 1)[a], H)[:, i, :], TR[:, 2 * a + i, :], YM[:, 2 * a + i, :],
                                   start=True, stop=True)
                        for i in range(2):
                            last = mm(bank((0, 2)[a], H)[:, i, :], YM[:, 2 * a + i, :], TR[:, 2 * a + i, :],
                                      start=True, stop=True)
                        last.then_inc(tr_ps, 1)
                pe.wait_ge(r_ok, tb * 2 * LEVELS + 2 * LEVELS)
                heads(1, lambda h: (TR[:, h, :], VB[:, h, :]), uw_ps)
                heads(2, lambda h: (KBG[:, h, :], TR[:, h, :]), uw_ps)
                pe.wait_ge(uw_ok, 2 * tb + 2)
                for c in range(2):
                    if c:
                        pe.wait_ge(st_ok, (2 * tb + 1) * H)
                    heads(3, lambda h: (WT[:, h, :], ST[:, c, h, :]), ws_ps)
                    pe.wait_ge(vn_ok, 2 * tb + c + 1)
                    kdz = (KDZ0, KDZ1)[c]
                    heads(4, lambda h: (kdz[:, h, :], VN[:, h, :]), su_ps)
                for h in range(H):
                    o = bank(5, H)[:, h, :]
                    mm(o, QD0[:, h, :], ST[:, 0, h, :], start=True, stop=False)
                    mm(o, QD1[:, h, :], ST[:, 1, h, :], start=False, stop=False)
                    last = mm(o, QKT[:, h, :], VN[:, h, :], start=False, stop=True)
                last.then_inc(o_ps, 1)
                pe.wait_ge(on_ok, tb + 1)
                for h in range(H):
                    last = tr(bank(6, H)[:, h, :], OB[:, h, :], ident)
                last.then_inc(ot_ps, 1)
                pe.wait_ge(st_ok, (2 * tb + 2) * H)
                pe.wait_ge(cat_ok, tb + 1)
            pe.wait_ge(pw_in, 16)
            for g in range(4):
                pe.wait_ge(pool_mix, g + 1)
                mm(bank(g), poolw[:, g, :], catT[:, H + g, :], start=True, stop=True).then_inc(pool_ps, 1)
            pe.wait_ge(pooled_ok, 4)
            pe.wait_ge(wout_in, 16)
            for b in range(TB):
                for half in range(2):
                    n = 2 * b + half
                    if n >= 4:
                        pe.wait_ge(x1_ok, n - 3)
                    for k in range(KD):
                        last = mm(bank(4 + n % 4), catT[:, k, b * P:(b + 1) * P], wout[:, k, 512 * half:512 * (half + 1)],
                                  start=k == 0, stop=k == KD - 1)
                    last.then_inc(op_ps, 1)
            for b in range(TB):
                pe.wait_ge(h2_ok, b + 1)
                for half in range(2):
                    n = 2 * b + half
                    if b >= 2:
                        pe.wait_ge((h2t_lo, h2t_hi)[half], b - 1)
                    for i in range(4):
                        k = 4 * half + i
                        last = tr(bank(2 * (b % 2) + half, 4)[:, i, :], h2[:, b, k * P:(k + 1) * P], ident)
                    last.then_inc(h2t_ps, 1)
            pe.wait_ge(h2t_lo, TB)
            pe.wait_ge(h2t_hi, TB)
            pe.wait_ge(wrt_in, 16)
            for b in range(TB):
                for k in range(KD):
                    last = mm(ps[:, 0, b * E:(b + 1) * E], h2T[:, k, b * P:(b + 1) * P], wrt[:, k, :],
                              start=k == 0, stop=k == KD - 1)
            last.then_inc(lg_ps, 1)
            pe.wait_ge(mask_ok, 1)
            for b in range(TB + 1):
                for a in range(min(b + 1, TB)):
                    last = mm(ps[:, 1, b * E:(b + 1) * E], lowS if a == b else ones, oh[:, 2, a, :], start=a == 0,
                              stop=a == min(b, TB - 1))
            last.then_inc(rank_ps, 1)
            pe.wait_ge(ebc_ok, 1)
            for i in range(2):
                last = mm(ps[0:1, 2, i * P:(i + 1) * P], ebc[:, i:i + 1], ident, start=True, stop=True)
            last.then_inc(tab_ps, 1)

            def gather(count, free):
                pe.wait_ge(hot_ok, count)
                if free is not None:
                    pe.wait_ge(xg_ok, free)
                for b in range(TB):
                    for q in range(Q):
                        last = mm(ps[SLOTS * q:SLOTS * (q + 1), 2, 0:QD], hot[:, b, 0, :], h2[:, b, q * QD:(q + 1) * QD],
                                  start=b == 0, stop=b == TB - 1)
                last.then_inc(gat_ps, 1)
                if free is not None:
                    pe.wait_ge(slot_ok, free)
                for b in range(TB):
                    last = mm(ps[:, 7, 0:2], hot[:, b].rearrange("p q s -> p (q s)"), gie[:, b, :], start=b == 0,
                              stop=b == TB - 1)
                last.then_inc(idx_ps, 1)

            def rows_T(count, free):
                pe.wait_ge(xg_ok, count)
                if free is not None:
                    pe.wait_ge(xgt_ok, free)
                for i in range(2):
                    last = tr(bank(3, 4)[:, i, :], xg[:, i * P:(i + 1) * P], ident)
                last.then_inc(xgt_ps, 1)

            pe.wait_ge(tab_ok, 1)
            gather(1, None)
            rows_T(1, None)
            pe.wait_ge(bias_ok, 1)

            def expert_block(g, j, turn):
                def landed(u):
                    slot, t = slot_of(j, u)
                    pe.wait_ge(slot_in[slot], (turn + t + 1) * 16)
                    return ring[:, slot * UNIT:(slot + 1) * UNIT].rearrange("p (s c) -> p s c", s=2)

                pe.wait_ge(xgt_ok, g + 1)
                pe.wait_ge(act_ok, g)
                for q in range(Q):
                    last = mm(ps[SLOTS * q:SLOTS * (q + 1), 0, :], selu[:, :],
                              bias3[:, 0:2 * D].rearrange("p (s c) -> p s c", s=2)[:, :, q * QD:(q + 1) * QD],
                              start=True, stop=False)
                last.then_inc(gub_used, 1)
                for u in range(NGU):
                    w = landed(u)
                    for q in range(Q):
                        last = mm(ps[SLOTS * q:SLOTS * (q + 1), 0, :],
                                  xgT[:, u % 2, SLOTS * (u // 2):SLOTS * (u // 2 + 1)],
                                  w[:, :, q * QD:(q + 1) * QD], start=False, stop=u == NGU - 1)
                    last.then_inc(w_used, 1)
                gather(g + 2, g + 1)
                pe.wait_ge(act_ok, g + 1)
                pe.wait_ge(actt_ok, g)
                for i in range(2):
                    last = tr(bank(4, 4)[:, i, :], act_[:, i * P:(i + 1) * P], ident)
                last.then_inc(at_ps, 1)
                rows_T(g + 2, g + 1)
                pe.wait_ge(seld_ok, g + 1)
                pe.wait_ge(ys_ok, g)
                for q in range(Q):
                    last = mm(ps[SLOTS * q:SLOTS * (q + 1), 1, 0:QD], seld[:, :],
                              bias3[:, 2 * D + q * QD:2 * D + (q + 1) * QD], start=True, stop=False)
                last.then_inc(dnb_used, 1)
                pe.wait_ge(actt_ok, g + 1)
                for u in range(NGU, NU):
                    w = landed(u)
                    for i in range(2):
                        c = 2 * (u - NGU) + i
                        for q in range(Q):
                            last = mm(ps[SLOTS * q:SLOTS * (q + 1), 1, 0:QD],
                                      actT[:, c % 2, SLOTS * (c // 2):SLOTS * (c // 2 + 1)],
                                      w[:, i, q * QD:(q + 1) * QD], start=False, stop=c == KD - 1)
                    last.then_inc(w_used, 1)

            with pe.Fori(0, E // UNROLL) as grp:
                for j in range(UNROLL):
                    lo = pe.value_load(tab[0:1, bass.ds(UNROLL * grp + j, 1)], min_val=0, max_val=MAXB)
                    hi = pe.value_load(tab[0:1, bass.ds(UNROLL * grp + (j + 1), 1)], min_val=0, max_val=MAXB)
                    with pe.Fori(lo, hi) as g:
                        expert_block(g, j, TURNS * grp)


_INS = ['x', 'attn_norm_w', 'w_in', 'conv_w', 'a_log', 'dt_bias', 'dn_norm_w', 'pool_w', 'pool_scale', 'w_out',
        'ffn_norm_w', 'w_router', 'b_router', 'w_gate_up', 'b_gate_up', 'w_down', 'b_down', 'final_norm_w']


def kernel(**inputs):
    import numpy as _np
    import concourse.bacc as _bacc
    from concourse.bass_utils import run_bass_kernel_spmd as _run

    nc = _bacc.Bacc("TRN2", target_bir_lowering=False, num_devices=1)
    arrays, args = {}, []
    for name in _INS:
        a = _np.ascontiguousarray(inputs[name])
        arrays[f"in_{name}_dram"] = a
        args.append(nc.dram_tensor(f"in_{name}_dram", a.shape, mybir.dt.from_np(a.dtype), kind="ExternalInput").ap())
    args.append(nc.dram_tensor("out_dram", (1, T, D), F32, kind="ExternalOutput").ap())
    args.append(nc.dram_tensor("pair_rows_dram", (T * TOPK * Q, QD), F32, kind="Internal").ap())
    moe_block(nc, *args)
    r = _run(nc, [arrays], core_ids=[0])
    return r.results[0]["out_dram"]
```

```python
from contextlib import ExitStack

import concourse.bass as bass
from concourse import mybir

F32, I32, U32, BF16 = mybir.dt.float32, mybir.dt.int32, mybir.dt.uint32, mybir.dt.bfloat16
ALU, ACT, AX = mybir.AluOpType, mybir.ActivationFunctionType, mybir.AxisListType

P = 128
D = 1024
T = 512
TB = T // P
KD = D // P
H = 4
CONV = 4
CH = 64
WINDOWS = (2, 4, 8, 16)
PAD = max(WINDOWS)
NQKV = 3 * H
E, TOPK = 32, 4
SLOTS = 32
Q = P // SLOTS
QD = D // Q
MAXB = T * TOPK // SLOTS + E
C_Z, C_BA, C_P = NQKV * P, (NQKV + H) * P, (NQKV + H) * P + 2 * H
RMS_EPS, L2_EPS = 1e-6, 1e-6
LIMIT, ALPHA = 7.0, 1.702
OOB = 4096.0

UNIT = 2 * D
NGU = KD
NU = KD + KD // 2
RING = 16
UNROLL = 4
TURNS = UNROLL * NU // RING
EARLY = 2


def moe_block(nc, x, attn_norm_w, w_in, conv_w, a_log, dt_bias, dn_norm_w, pool_w, pool_scale, w_out,
              ffn_norm_w, w_router, b_router, w_gate_up, b_gate_up, w_down, b_down, final_norm_w,
              out, pair_rows):
    ctx = ExitStack()
    with ctx:
        def sb(name, shape, dt=F32):
            return ctx.enter_context(nc.sbuf_tensor(name, shape, dt))

        def sem(name):
            return ctx.enter_context(nc.semaphore(name))

        ring = sb("ring", [P, RING * UNIT])
        late = ring[:, EARLY * UNIT:]

        def room(at, *dims):
            n = 1
            for d in dims:
                n *= d
            flat = late[:, at:at + n]
            if len(dims) == 2:
                return flat.rearrange("p (a b) -> p a b", a=dims[0])
            if len(dims) == 3:
                return flat.rearrange("p (a b c) -> p a b c", a=dims[0], b=dims[1])
            return flat

        qkv = room(0, NQKV, T)
        zs = room(6144, H, T)
        win = room(8192, 2, KD, 256)
        pbuf = room(12288, 4, PAD + T)
        junk = room(14400, D)
        cbuf = [room(14400 + 512 * i, T) for i in range(2)]
        junk2 = room(12288, D)
        wout = room(16384, KD, D)
        AT, QKT, TM, TR, YM, KTS, VTS, KBG = [room(8192 + 512 * i, H, P) for i in range(8)]
        VB, GUM, BI = [room(14400 + 512 * i, H, P) for i in range(3)]
        OSQ = (AT, TM, TR, YM)
        h2T = room(0, KD, T)
        braw = room(4096, 3 * D)[0:96, :]
        brem = room(8192, 3 * D)[0:96, :]

        xs = sb("xs", [P, TB, D])
        hbuf = sb("hbuf", [P, KD * T])
        hT = hbuf[:, :].rearrange("p (k t) -> p k t", k=KD)
        h2 = hbuf[:, :].rearrange("p (b d) -> p b d", b=TB)
        cat = sb("cat", [P, KD * T])
        catT = cat[:, :].rearrange("p (k t) -> p k t", k=KD)
        xn = cat[:, :].rearrange("p (b d) -> p b d", b=TB)
        wsf = room(24576, 8, T)
        WS = late[:, 24576:28672].rearrange("p (n a b) -> p n a b", n=8, a=H)
        KDZ0, KDZ1, QD0, QD1, VN, UU, WT, DX = [WS[:, i] for i in range(8)]
        O4 = hbuf[:, 0:TB * H * P].rearrange("p (b h c) -> p b h c", b=TB, h=H)
        QKN, QDN, KDN, EGI = [hbuf[:, (TB + i) * H * P:(TB + i + 1) * H * P].rearrange("p (h c) -> p h c", h=H)
                              for i in range(4)]
        ba_part = wsf[:, 7]
        lg_part = cat[:, 1536:2048]
        ST = sb("ST", [P, 2, H, P])
        cst = sb("cst", [P, 8, P])
        ident, ones, same, lowS, causal, strict, first, second = [cst[:, i, :] for i in range(8)]
        E3 = sb("E3", [96, SLOTS], BF16)
        iotas = room(15936, 3, P).bitcast(I32)
        iotaf = sb("iotaf", [P, T + SLOTS])
        lvl = sb("lvl", [P, 6, P])
        prow = sb("prow", [61, P])
        pcol = sb("pcol", [P, 61])
        NANW, NCV, NDN, NPS = 0, 8, 56, 57
        sm = sb("sm", [P, 48])
        epsc = sb("epsc", [P, 2])
        gt = sb("gt", [P, 12, TB, H])
        gcs = sb("gcs", [P, 4, TB, H])
        gex = sb("gex", [P, 4, TB, H])
        wrt = sb("wrt", [P, KD, E])
        wba = sb("wba", [P, KD, SLOTS])
        S4 = sb("S4", [P, SLOTS])
        so = sb("so", [P, 3, TB, H])
        bcr = sb("bcr", [P, 2 * H + E])
        shared = sb("shared", [P, 2 * (PAD + T)])
        pool_t = shared[:, :].rearrange("p (a b) -> p a b", a=2)
        fnw = shared[:, 0:D]
        bias3 = cat[0:96, 0:3 * D // 2].bitcast(BF16)
        poolw = sb("poolw", [P, 4, P])
        icnt = sb("icnt", [P, PAD])
        lgs = sb("lgs", [P, TB, E])
        v8 = sb("v8", [P, TB, 8])
        i8 = sb("i8", [P, TB, 8], U32)
        tk = sb("tk", [P, 4, TB, TOPK])
        oh = cat[:, 2560:3072].rearrange("p (n b e) -> p n b e", n=4, b=TB)
        nbi = sb("nbi", [P, E], I32)
        nbf = sb("nbf", [P, 4, E])
        ebc = sb("ebc", [P, 4])
        rowbase = sb("rowbase", [P, TB])
        pidx = sb("pidx", [P, 1])
        rank = sb("rank", [P, TB, E])
        gi = sb("gi", [P, TB, E, 2])
        tab = sb("tab", [1, 2 * E + 2 + 2 * P], I32)
        USED, PAIRS = E + 1 + 2 * P, 2 * E + 1 + 2 * P
        hot = cat[:, 1536:2048].rearrange("p (b q s) -> p b q s", b=TB, q=Q)
        gie = sb("gie", [P, TB, 2])
        selu = sb("selu", [96, SLOTS], BF16)
        seld = sb("seld", [96, SLOTS], BF16)
        xg = cat[:, 2048:2304]
        xgT = cat[:, 2304:2560].rearrange("p (i c) -> p i c", i=2)
        gc = cat[:, 2560:2816]
        sg = cat[:, 2816:3072]
        uc = cat[:, 3072:3328]
        act_ = cat[:, 3328:3584]
        actT = cat[:, 3584:3840].rearrange("p (i c) -> p i c", i=2)
        ys = [cat[:, 3840:4096], sb("ys1", [P, QD])[:, :]]
        wslot = sb("wslot", [P, 2])
        rowf = sb("rowf", [P, 2])
        rowi = sb("rowi", [P, 2], I32)
        qcol = sb("qcol", [P, 1])

        ps = ctx.enter_context(nc.psum_tensor("ps", [P, 8, 512], F32))

        def bank(b, a=None):
            v = ps[:, b, :]
            return v.rearrange("p (a b) -> p a b", a=a) if a else v

        def bc(v, n, at):
            return v.unsqueeze(at).to_broadcast([*v.shape[:at], n, *v.shape[at:]])

        x_in = [sem(f"x_in{i}") for i in range(TB)]
        par_in, wba_in, bc_in, pw_in, wrt_in, fnw_in, wout_in, braw_in = [sem(n) for n in (
            "par_in", "wba_in", "bc_in", "pw_in", "wrt_in", "fnw_in", "wout_in", "braw_in")]
        win_in = [sem(f"win_in{i}") for i in range(2)]
        slot_in = [sem(f"slot_in{i}") for i in range(RING)]
        y_in = [sem(f"y_in{i}") for i in range(TB)]
        iota_ok, const_ok, zero_ok, lvl_ok, pool_step, pool_mix, bias_ok = [sem(n) for n in (
            "iota_ok", "const_ok", "zero_ok", "lvl_ok", "pool_step", "pool_mix", "bias_ok")]
        std_ok, rstd_ok, xn_ok, pcol_ps, pcol_ok, xt_ps, ht_even, ht_odd = [sem(n) for n in (
            "std_ok", "rstd_ok", "xn_ok", "pcol_ps", "pcol_ok", "xt_ps", "ht_even", "ht_odd")]
        proj_ps, tap_ok, conv_step, conv_ok, silu_ok, sq_ok, nrm_ps, nroot_ok, qk_ok, ba_ps = [sem(n) for n in (
            "proj_ps", "tap_ok", "conv_step", "conv_ok", "silu_ok", "sq_ok", "nrm_ps", "nroot_ok", "qk_ok", "ba_ps")]
        dve_step, gin_ok, gexp_in, gln_in, gln_ok, g_ok, gcum_ps, gcs_ok, gex_ok = [sem(n) for n in (
            "dve_step", "gin_ok", "gexp_in", "gln_in", "gln_ok", "g_ok", "gcum_ps", "gcs_ok", "gex_ok")]
        grow_ok, kv_ok, grow_ps, brow_ps, kk_ps, ktok_ps, dx_ok, dexp_ok, delta_step, prep_ok = [sem(n) for n in (
            "grow_ok", "kv_ok", "grow_ps", "brow_ps", "kk_ps", "ktok_ps", "dx_ok", "dexp_ok", "delta_step", "prep_ok")]
        r2_ok, t2_ps, t_ok, y_ps, ym_ok, tr_ps, uw_ps, uw_ok, ws_ps, vn_ok, su_ps, st_ok = [sem(n) for n in (
            "r2_ok", "t2_ps", "t_ok", "y_ps", "ym_ok", "tr_ps", "uw_ps", "uw_ok", "ws_ps", "vn_ok", "su_ps", "st_ok")]
        o_ps, osq_ok, oms_ok, ort_ok, on_ok, ot_ps, cat_ok = [sem(n) for n in (
            "o_ps", "osq_ok", "oms_ok", "ort_ok", "on_ok", "ot_ps", "cat_ok")]
        pool_ps, pooled_ok, op_ps, x1_ok, s2_ok, h2_ok, h2t_ps, h2t_lo, lg_ps = [sem(n) for n in (
            "pool_ps", "pooled_ok", "op_ps", "x1_ok", "s2_ok", "h2_ok", "h2t_ps", "h2t_lo", "lg_ps")]
        top_ok, texp_ok, mask_ok, rank_ps, ebc_ok, tab_ps, tab_ok, r_ok = [sem(n) for n in (
            "top_ok", "texp_ok", "mask_ok", "rank_ps", "ebc_ok", "tab_ps", "tab_ok", "r_ok")]
        info_step, slot_ok, seld_ok, sel_step, hot_ok, gat_ps, idx_ps, xg_ok, xgt_ps, xgt_ok = [sem(n) for n in (
            "info_step", "slot_ok", "seld_ok", "sel_step", "hot_ok", "gat_ps", "idx_ps", "xg_ok", "xgt_ps", "xgt_ok")]
        gub_used, w_used, gc_ok, uc_step, sg_ok, act_ok, at_ps, actt_ok, dnb_used, ys_ok, scat0, scat1 = [sem(n) for n in (
            "gub_used", "w_used", "gc_ok", "uc_step", "sg_ok", "act_ok", "at_ps", "actt_ok", "dnb_used", "ys_ok",
            "scattered_even", "scattered_odd")]
        scat = (scat0, scat1)
        fin_add, fin_sum, fin_sq, fin_rt, fin_rc, fin_o, out_ok, act_step, h2t_hi, t_lvl, beta_ok, vtok_ps, cur_ok, oc_ok, part_ps, part_ok = [sem(n) for n in (
            "fin_add", "fin_sum", "fin_sq", "fin_rt", "fin_rc", "fin_o", "out_stored", "act_step", "h2t_hi", "t_lvl", "beta_ok", "vtok_ps", "cur_ok", "oc_ok", "part_ps", "part_ok")]

        def chain(eng, s, start=0):
            n = [0]

            def link(ins):
                n[0] += 1
                ins.then_inc(s, 1)
                eng.wait_ge(s, start + n[0])
            link.n = n
            return link

        def unit_src(e, u):
            if u < NGU:
                return w_gate_up[0, bass.ds(e, 1), u * P:(u + 1) * P, :].rearrange("a p c -> (a p) c")
            c = 2 * (u - NGU)
            return w_down[0, bass.ds(e, 1), c * P:(c + 2) * P, :].rearrange("a (c p) n -> p (a c) n", c=2)

        def unit_dst(slot, u):
            v = ring[:, slot * UNIT:(slot + 1) * UNIT]
            return v if u < NGU else v.rearrange("p (c n) -> p c n", c=2)

        def slot_of(j, u):
            return (NU * j + u) % RING, (NU * j + u) // RING

        block = ctx.enter_context(nc.Block())
        y_pairs = pair_rows.rearrange("(t k q) c -> t (k q c)", k=TOPK, q=Q)
        n_conv = CONV - 1
        DELTA_LINKS = 10
        LEVELS = 5

        def nrm_bank(n):
            return n + 1 if n < 6 else n - 4

        def t_bank(a):
            return (7, 1)[a]

        def r_bank(a):
            return (0, 2)[a]

        @block.sync
        def _(sp):
            def param(row, n, src):
                sp.dma_start(prow[row:row + n, :], src).then_inc(par_in, 16)

            for b in range(TB):
                sp.dma_start(xs[:, b, :], x[0, b * P:(b + 1) * P, :]).then_inc(x_in[b], 16)
            param(NANW, KD, attn_norm_w.rearrange("l (k p) -> (l k) p", p=P))
            for j in range(CONV):
                param(NCV + NQKV * j, NQKV, conv_w[0, j:j + 1, :].rearrange("l (k p) -> (l k) p", p=P))
            param(NDN, 1, dn_norm_w)
            param(NPS, 4, pool_scale.rearrange("l (k p) -> (l k) p", p=P))

            w_in_v = w_in[0].rearrange("(k p) c -> p k c", p=P)

            def load_piece(buf, c0):
                sp.dma_start(win[:, buf], w_in_v[:, :, bass.ds(c0, 256)]).then_inc(win_in[buf], 16)

            load_piece(0, 0)
            load_piece(1, 256)
            sp.dma_start(wba[:, :, :], w_in_v[:, :, C_BA:C_BA + SLOTS]).then_inc(wba_in, 16)
            sp.dma_start(bcr[:, 0:H], dt_bias.to_broadcast([P, H])).then_inc(bc_in, 16)
            sp.dma_start(bcr[:, H:2 * H], a_log.to_broadcast([P, H])).then_inc(bc_in, 16)
            sp.dma_start(bcr[:, 2 * H:], b_router.to_broadcast([P, E])).then_inc(bc_in, 16)
            sp.dma_start(poolw[:, :, :], pool_w[0].rearrange("g c d -> c g d")).then_inc(pw_in, 16)
            sp.dma_start(wrt[:, :, :], w_router[0].rearrange("(k p) e -> p k e", p=P)).then_inc(wrt_in, 16)
            with sp.Fori(0, 2) as i:
                for buf in range(2):
                    sp.wait_ge(proj_ps, 4 * i + 2 * (buf + 1))
                    load_piece(buf, 512 * (i + 1) + 256 * buf)
            for n, c0 in ((6, C_Z), (7, C_Z + 256), (8, C_P), (9, C_P + 256)):
                sp.wait_ge(proj_ps, 2 * (n - 1))
                load_piece(n % 2, c0)
            sp.dma_start(wout[:, :, :], w_out[0].rearrange("(k p) c -> p k c", p=P)).then_inc(wout_in, 16)

            def load_unit(e, u, slot):
                sp.dma_start(unit_dst(slot, u), unit_src(e, u)).then_inc(slot_in[slot], 16)

            for u in range(EARLY):
                load_unit(0, u, u)
            sp.wait_ge(cat_ok, TB)
            sp.wait_ge(pool_mix, 4)
            sp.dma_start(fnw, ffn_norm_w.to_broadcast([P, D])).then_inc(fnw_in, 16)
            for i in range(3):
                sp.dma_start(braw[32 * i:32 * i + 32, 0:2 * D], b_gate_up[0]).then_inc(braw_in, 16)
                sp.dma_start(braw[32 * i:32 * i + 32, 2 * D:], b_down[0]).then_inc(braw_in, 16)
            sp.wait_ge(h2_ok, TB)
            sp.dma_start(fnw, final_norm_w.rearrange("(a n) -> a n", a=1).to_broadcast([P, D])).then_inc(fnw_in, 16)
            sp.wait_ge(lg_ps, 1)
            sp.wait_ge(bias_ok, 1)
            for n in range(EARLY, RING):
                load_unit(n // NU, n % NU, n)
            sp.wait_ge(tab_ok, 1)

            def refill(e, j, used):
                for u in range(NU):
                    nu, ne = (u + RING) % NU, (u + RING) // NU
                    if isinstance(e, int) and e + ne >= E:
                        continue
                    sp.wait_ge(w_used, used + (u + 1))
                    load_unit(e + ne, nu, slot_of(j, u)[0])

            with sp.Fori(0, E // UNROLL - 1) as grp:
                for j in range(UNROLL):
                    used = sp.value_load(tab[0:1, bass.ds(UNROLL * grp + (j + USED), 1)], min_val=0, max_val=MAXB * NU)
                    refill(UNROLL * grp + j, j, used)
            for e in range(E - UNROLL, E):
                used = sp.value_load(tab[0:1, USED + e:USED + e + 1], min_val=0, max_val=MAXB * NU)
                refill(e, e % UNROLL, used)
            pairs = sp.value_load(tab[0:1, PAIRS:PAIRS + 1], min_val=E // 2, max_val=MAXB // 2)
            for s in scat:
                sp.wait_ge(s, pairs * 16)
            for b in range(TB):
                sp.dma_start(ring[:, b * TOPK * D:(b + 1) * TOPK * D], y_pairs[b * P:(b + 1) * P, :]).then_inc(y_in[b], 16)
            for b in range(TB):
                sp.wait_ge(fin_o, b + 1)
                sp.dma_start(out[0, b * P:(b + 1) * P, :], ring[:, b * TOPK * D:b * TOPK * D + D]).then_inc(out_ok, 16)
            sp.wait_ge(out_ok, 16 * TB)

        @block.gpsimd
        def _(pool):
            G = nc.gpsimd
            link = chain(pool, pool_step)
            imprecise = dict(allow_small_or_imprecise_dtypes=True)
            G.iota(iotas[:, 0, :], pattern=[[1, P]], base=0, channel_multiplier=0).then_inc(iota_ok, 1)
            G.iota(iotas[:, 1, :], pattern=[[0, P]], base=0, channel_multiplier=1).then_inc(iota_ok, 1)
            G.iota(iotaf[:, :], pattern=[[1, T + SLOTS]], base=0, channel_multiplier=0, **imprecise).then_inc(iota_ok, 1)
            G.iota(rowbase[:, :], pattern=[[TOPK * P, TB]], base=-int(OOB), channel_multiplier=TOPK,
                   **imprecise).then_inc(iota_ok, 1)
            G.iota(pidx[:, :], pattern=[[0, 1]], base=0, channel_multiplier=1, **imprecise).then_inc(iota_ok, 1)
            G.memset(epsc[:, 0:1], RMS_EPS).then_inc(const_ok, 1)
            G.memset(epsc[:, 1:2], L2_EPS).then_inc(const_ok, 1)
            link(G.memset(ident, 0.0))
            link(G.memset(cst[:, 1, :], 1.0))
            link(G.memset(cst[:, 2, :], 0.0))
            link(G.memset(cst[:, 6:8, :], 0.0))
            for c in range(2):
                r = slice(CH * c, CH * (c + 1))
                link(G.memset(cst[r, 2, r], 1.0))
                link(G.memset(cst[r, 6 + c, :], 1.0))
            G.affine_select(out=ident, in_=ident, compare_op=ALU.not_equal, fill=1.0, base=0,
                            pattern=[[-1, P]], channel_multiplier=1).then_inc(const_ok, 1)
            for dst, src, cmp in ((lowS, ones, ALU.is_gt), (causal, same, ALU.is_ge), (strict, same, ALU.is_gt)):
                G.affine_select(out=dst, in_=src, compare_op=cmp, fill=0.0, base=0,
                                pattern=[[1, P]], channel_multiplier=-1).then_inc(const_ok, 1)
            for g in range(3):
                link(G.memset(E3[32 * g:32 * g + 32, :], 0.0))
                link(G.affine_select(out=E3[32 * g:32 * g + 32, :], in_=E3[32 * g:32 * g + 32, :],
                                     compare_op=ALU.not_equal, fill=1.0, base=0, pattern=[[-1, SLOTS]],
                                     channel_multiplier=1))
            for q in range(Q):
                r = slice(SLOTS * q, SLOTS * (q + 1))
                link(G.memset(S4[r, :], 0.0))
                ins = G.affine_select(out=S4[r, :], in_=S4[r, :], compare_op=ALU.not_equal, fill=1.0, base=0,
                                      pattern=[[-1, SLOTS]], channel_multiplier=1)
                if q < Q - 1:
                    link(ins)
                else:
                    ins.then_inc(const_ok, 1)
            for q in range(Q):
                link(G.memset(qcol[SLOTS * q:SLOTS * (q + 1), :], float(q)))
            link(G.memset(pool_t[:, :, 0:PAD], 0.0))
            link(G.memset(pbuf[:, :, 0:PAD], 0.0))
            link(G.memset(ST[:, :, :, :], 0.0))
            pool.wait_ge(qk_ok, 2 * H)
            G.memset(WS[:, 0:5], 0.0).then_inc(zero_ok, 1)

            def spread(tb):
                def col(v):
                    return bc(v[:, bass.ds(tb, 1), :].rearrange("p a h -> p (a h)"), P, 2)
                G.tensor_tensor(GUM, bc(causal, H, 1), col(gt[:, 8]), ALU.mult).then_inc(grow_ok, 1)
                G.tensor_tensor(BI, bc(ident, H, 1), col(gt[:, 9]), ALU.mult).then_inc(grow_ok, 1)

            pool.wait_ge(beta_ok, 1)
            spread(0)
            pool.wait_ge(lvl_ok, 1)
            for g, w in enumerate(WINDOWS):
                pool.wait_ge(silu_ok, NQKV + H + g + 1)
                src, s, i = pbuf[:, g], 1, 0
                while s < w:
                    dst = pool_t[:, i % 2]
                    link(G.tensor_tensor(dst[:, PAD:], src[:, PAD:], src[:, PAD - s:PAD + T - s], ALU.add))
                    src, s, i = dst, 2 * s, i + 1
                link(G.tensor_scalar(catT[:, H + g, :], src[:, PAD:], 1.0 / w, None, ALU.mult))
                link(G.tensor_tensor(catT[:, H + g, :], catT[:, H + g, :], pbuf[:, g, PAD:], ALU.subtract))
                link(G.tensor_tensor(src[:, PAD:PAD + w], src[:, PAD:PAD + w], icnt[:, 0:w], ALU.mult))
                G.tensor_tensor(catT[:, H + g, 0:w], src[:, PAD:PAD + w], pbuf[:, g, PAD:PAD + w],
                                ALU.subtract).then_inc(pool_mix, 1)
                pool.wait_ge(pool_mix, g + 1)
            with pool.Fori(0, TB - 1) as tb:
                pool.wait_ge(brow_ps, tb + 1)
                spread(tb + 1)
            pool.wait_ge(braw_in, 6 * 16)
            pool.wait_ge(op_ps, 2 * TB)
            link(G.tensor_copy(bias3[:, :], braw))
            for lo in (32, 64):
                for g in range(lo, 96, 32):
                    r = slice(g, g + 32)
                    link(G.tensor_tensor(brem[r], braw[r] if lo == 32 else brem[r], bias3[r, :], ALU.subtract))
                    last = G.tensor_copy(bias3[r, :], brem[r])
                    if lo == 64:
                        last.then_inc(bias_ok, 1)
                    else:
                        link(last)
            pool.wait_ge(tab_ok, 1)
            pairs = pool.value_load(tab[0:1, PAIRS:PAIRS + 1], min_val=E // 2, max_val=MAXB // 2)
            with pool.Fori(0, pairs) as i:
                for p in range(2):
                    pool.wait_ge(ys_ok, 2 * i + (p + 1))
                    limit = pool.snap(i + (T * TOPK * Q + p))
                    G.indirect_dma_start(
                        out=pair_rows, out_offset=bass.IndirectOffsetOnAxis(ap=rowi[:, p:p + 1], axis=0),
                        in_=ys[p], in_offset=None, bounds_check=limit,
                        oob_is_err=False).then_inc(scat[p], 16)

        @block.scalar
        def _(act):
            A = nc.scalar.activation
            link = chain(act, act_step)

            def row(v):
                return v.rearrange("p a t -> p (a t)")

            for b in range(TB):
                act.wait_ge(x_in[b], 16)
                link(A(junk, xs[:, b, :], ACT.Square, accum_out=sm[:, b:b + 1]))
            act.wait_ge(const_ok, 2)
            A(sm[:, 4:8], sm[:, 0:4], ACT.Sqrt, scale=1.0 / D, bias=epsc[:, 0:1]).then_inc(std_ok, 1)
            act.wait_ge(pcol_ok, 1)
            for k in range(0, KD, 2):
                act.wait_ge(xt_ps, k + 1)
                A(hT[:, k, :], bank(k), ACT.Copy, scale=pcol[:, NANW + k:NANW + k + 1]).then_inc(ht_even, 1)
            with act.Fori(0, 3) as i:
                for r in range(4):
                    n = 4 * i + r
                    act.wait_ge(proj_ps, n + 1)
                    A(cbuf[r % 2], bank(r % 2), ACT.Copy,
                      scale=pcol[:, bass.ds(n + (NCV + n_conv * NQKV), 1)]).then_inc(tap_ok, 1)
                    act.wait_ge(conv_ok, n + 1)
                    A(row(qkv[:, bass.ds(n, 1), :]), cbuf[r % 2], ACT.Silu).then_inc(silu_ok, 1)
            act.wait_ge(gin_ok, 1)
            A(gt[:, 2], gt[:, 1], ACT.Exp).then_inc(gexp_in, 1)
            A(gt[:, 3], gt[:, 10], ACT.Exp, scale=-1.0).then_inc(gexp_in, 1)
            act.wait_ge(bc_in, 48)
            A(gt[:, 4, 0, :], bcr[:, H:2 * H], ACT.Exp).then_inc(gexp_in, 1)
            act.wait_ge(gln_in, 1)
            A(gt[:, 6], gt[:, 5], ACT.Ln).then_inc(gln_ok, 1)
            for n in range(2 * H):
                act.wait_ge(nrm_ps, n + 1)
                A(wsf[:, n], bank(nrm_bank(n)), ACT.Sqrt, bias=epsc[:, 1:2]).then_inc(nroot_ok, 1)
            for n in range(NQKV, NQKV + 2 * H):
                act.wait_ge(proj_ps, n + 1)
                if n < NQKV + H:
                    A(zs[:, n - NQKV, :], bank(n % 2), ACT.Silu).then_inc(silu_ok, 1)
                else:
                    A(pbuf[:, n - NQKV - H, PAD:], bank(n % 2), ACT.Copy).then_inc(silu_ok, 1)
                if n == NQKV + H - 1:
                    act.wait_ge(gcs_ok, 1)
                    A(gex[:, :, :, :], gcs[:, :, :, :], ACT.Exp).then_inc(gex_ok, 1)

            def load_kv(t):
                if not isinstance(t, int):
                    act.wait_ge(vtok_ps, t)
                tok = bass.ds(t * P, P)
                A(KTS, qkv[:, H:2 * H, tok], ACT.Copy).then_inc(kv_ok, 1)
                A(VTS, qkv[:, 2 * H:3 * H, tok], ACT.Copy).then_inc(kv_ok, 1)

            def decay(t):
                act.wait_ge(grow_ps, t + 1)
                A(EGI, bank(0, H), ACT.Exp).then_inc(dexp_ok, 1)
                act.wait_ge(dx_ok, t + 1)
                A(DX, DX, ACT.Exp).then_inc(dexp_ok, 1)

            def first_inverse(t):
                act.wait_ge(t2_ps, t + 1)
                A(TM, bank(1, H), ACT.Copy).then_inc(t_ok, 1)

            def delta(t, more):
                act.wait_ge(prep_ok, t + 1)
                act.wait_ge(o_ps, t)
                A(QKT, QKN, ACT.Copy).then_inc(cur_ok, 1)
                A(KDZ0[0:CH], KDN[0:CH], ACT.Copy).then_inc(cur_ok, 1)
                A(KDZ1[CH:], KDN[CH:], ACT.Copy).then_inc(cur_ok, 1)
                A(QD0[:, :, 0:CH], QDN[:, :, 0:CH], ACT.Copy).then_inc(cur_ok, 1)
                A(QD1[:, :, CH:], QDN[:, :, CH:], ACT.Copy).then_inc(cur_ok, 1)
                if more:
                    load_kv(t + 1)
                act.wait_ge(uw_ps, t * 2 + 1)
                A(UU, bank(1, H), ACT.Copy).then_inc(uw_ok, 1)
                act.wait_ge(uw_ps, t * 2 + 2)
                A(WT, bank(2, H), ACT.Copy).then_inc(uw_ok, 1)
                if more:
                    decay(t + 1)
                act.wait_ge(o_ps, t + 1)
                A(O4[:, bass.ds(t, 1)].rearrange("p a h c -> p (a h) c"), bank(5, H), ACT.Copy).then_inc(oc_ok, 1)
                if more:
                    first_inverse(t + 1)

            act.wait_ge(qk_ok, 2 * H)
            load_kv(0)
            decay(0)
            first_inverse(0)
            with act.Fori(0, TB - 1) as tb:
                delta(tb, True)
            delta(TB - 1, False)
            act.wait_ge(oc_ok, TB)
            for b in range(TB):
                A(OSQ[b], O4[:, b], ACT.Square).then_inc(osq_ok, 1)
            act.wait_ge(oms_ok, TB)
            A(so[:, 1], so[:, 0], ACT.Sqrt, scale=1.0 / P, bias=epsc[:, 0:1]).then_inc(ort_ok, 1)
            for g in range(4):
                act.wait_ge(pool_ps, g + 1)
                A(catT[:, H + g, :], bank(g), ACT.Copy, scale=pcol[:, NPS + g:NPS + g + 1]).then_inc(pooled_ok, 1)
            for b in range(TB):
                act.wait_ge(x1_ok, 2 * b + 2)
                link(A(junk2, xs[:, b, :], ACT.Square, accum_out=sm[:, 20 + b:21 + b]))
                A(sm[:, 24 + b:25 + b], sm[:, 20 + b:21 + b], ACT.Sqrt, scale=1.0 / D, bias=epsc[:, 0:1]).then_inc(s2_ok, 1)
            for n in range(1, 2 * TB, 2):
                act.wait_ge(h2t_ps, n + 1)
                A(h2T[:, 4:8, (n // 2) * P:(n // 2 + 1) * P], bank(2 * (n // 2 % 2) + 1, 4), ACT.Copy).then_inc(h2t_hi, 1)
            act.wait_ge(top_ok, 1)
            A(tk[:, 1], tk[:, 2], ACT.Exp).then_inc(texp_ok, 1)

            act.wait_ge(gat_ps, 1)
            A(xg[:, :], ps[:, 2, 0:QD], ACT.Copy).then_inc(xg_ok, 1)
            act.wait_ge(xgt_ps, 1)
            A(xgT[:, :, :], bank(3, 4)[:, 0:2, :], ACT.Copy).then_inc(xgt_ok, 1)
            act.wait_ge(tab_ok, 1)
            pairs = act.value_load(tab[0:1, PAIRS:PAIRS + 1], min_val=E // 2, max_val=MAXB // 2)

            def activate(g, i, p):
                act.wait_ge(gc_ok, g + 1)
                act.wait_ge(act_ok, g)
                A(sg[:, :], gc[:, :], ACT.Sigmoid, scale=ALPHA).then_inc(sg_ok, 1)
                act.wait_ge(gat_ps, g + 2)
                act.wait_ge(xgt_ps, g + 1)
                A(xg[:, :], ps[:, 2, 0:QD], ACT.Copy).then_inc(xg_ok, 1)
                act.wait_ge(at_ps, g + 1)
                act.wait_ge(w_used, g * NU)
                A(actT[:, :, :], bank(4, 4)[:, 0:2, :], ACT.Copy).then_inc(actt_ok, 1)
                act.wait_ge(xgt_ps, g + 2)
                act.wait_ge(w_used, g * NU + NGU)
                A(xgT[:, :, :], bank(3, 4)[:, 0:2, :], ACT.Copy).then_inc(xgt_ok, 1)
                act.wait_ge(w_used, g * NU + NU)
                act.wait_ge(slot_ok, g + 1)
                act.wait_ge(scat[p], i * 16)
                A(ys[p], ps[:, 1, 0:QD], ACT.Copy, scale=wslot[:, p:p + 1]).then_inc(ys_ok, 1)

            with act.Fori(0, pairs) as i:
                for p in range(2):
                    activate(2 * i + p, i, p)
            for b in range(TB):
                act.wait_ge(fin_sum, b + 1)
                base = b * TOPK * D + D
                A(ring[:, base:base + D], xs[:, b, :], ACT.Square, accum_out=sm[:, 28 + b:29 + b]).then_inc(fin_sq, 1)
                act.wait_ge(fin_sq, b + 1)
                A(sm[:, 32 + b:33 + b], sm[:, 28 + b:29 + b], ACT.Sqrt, scale=1.0 / D, bias=epsc[:, 0:1]).then_inc(fin_rt, 1)

        @block.vector
        def _(dve):
            V = nc.vector
            link = chain(dve, dve_step)

            def step(ins, s, count):
                ins.then_inc(s, 1)
                dve.wait_ge(s, count)

            dve.wait_ge(pcol_ps, 1)
            step(V.tensor_copy(pcol[:, :], ps[:, 7, 0:61]), pcol_ok, 1)
            dve.wait_ge(std_ok, 1)
            step(V.reciprocal(sm[:, 8:12], sm[:, 4:8]), rstd_ok, 1)
            for b in range(TB):
                V.tensor_scalar(xn[:, b, :], xs[:, b, :], sm[:, 8 + b:9 + b], None, ALU.mult).then_inc(xn_ok, 1)
            dve.wait_ge(iota_ok, 5)
            link(V.tensor_tensor(iotas[:, 2, :], iotas[:, 0, :], iotas[:, 1, :], ALU.bitwise_xor))
            for s in range(6):
                link(V.tensor_scalar(iotas[:, 0, :], iotas[:, 2, :], s, None, ALU.logical_shift_right))
                link(V.tensor_scalar(lvl[:, s, :], iotas[:, 0, :], 1, None, ALU.is_equal))
            dve.wait_ge(const_ok, 6)
            link(V.tensor_tensor(lvl[:, 0, :], lvl[:, 0, :], strict, ALU.mult))
            for s in range(1, 6):
                link(V.tensor_scalar(nbf[:, :, :].rearrange("p a b -> p (a b)"), causal, -1.0, 1.0, ALU.mult, ALU.add))
                link(V.tensor_tensor(lvl[:, s, :], lvl[:, s, :], nbf[:, :, :].rearrange("p a b -> p (a b)"), ALU.mult))
            link(V.tensor_scalar(icnt[:, :], iotaf[:, 0:PAD], 1.0, None, ALU.add))
            V.reciprocal(icnt[:, :], icnt[:, :]).then_inc(lvl_ok, 1)
            for k in range(1, KD, 2):
                dve.wait_ge(xt_ps, k + 1)
                V.tensor_scalar(hT[:, k, :], bank(k), pcol[:, NANW + k:NANW + k + 1], None, ALU.mult).then_inc(ht_odd, 1)

            def conv(n, b, base):
                t = cbuf[b]
                dve.wait_ge(tap_ok, n + 1)
                for m in range(1, CONV):
                    ins = V.scalar_tensor_tensor(
                        out=t[:, m:], in0=bank(b)[:, 0:T - m], scalar=pcol[:, bass.ds(n + (NCV + (n_conv - m) * NQKV), 1)],
                        in1=t[:, m:], op0=ALU.mult, op1=ALU.add)
                    if m < n_conv:
                        step(ins, conv_step, base + m)
                    else:
                        ins.then_inc(conv_ok, 1)

            dve.wait_ge(part_ps, 1)
            V.tensor_copy(ba_part, bank(6)).then_inc(part_ok, 1)
            with dve.Fori(0, 3) as i:
                for r in range(4):
                    conv(4 * i + r, r % 2, (4 * i + r) * (n_conv - 1))
            dve.wait_ge(ba_ps, 1)
            dve.wait_ge(bc_in, 48)
            ba = ps[:, 7, 0:TB * 2 * H].rearrange("p (b c) -> p b c", b=TB)
            link(V.tensor_copy(gt[:, 10], ba[:, :, 0:H]))
            link(V.tensor_tensor(gt[:, 0], ba[:, :, H:], bc(bcr[:, 0:H], TB, 1), ALU.add))
            link(V.tensor_scalar(gt[:, 1], gt[:, 0], -1.0, None, ALU.mult))
            step(V.tensor_tensor(gt[:, 1], gt[:, 1], gt[:, 0], ALU.min), gin_ok, 1)
            for n in range(2 * H):
                dve.wait_ge(silu_ok, n + 1)
                V.tensor_tensor(wsf[:, n], qkv[:, n, :], qkv[:, n, :], ALU.mult).then_inc(sq_ok, 1)
            dve.wait_ge(gexp_in, 3)
            step(V.tensor_scalar(gt[:, 5], gt[:, 2], 1.0, None, ALU.add), gln_in, 1)
            link(V.tensor_scalar(gt[:, 7], gt[:, 5], -1.0, None, ALU.add))
            link(V.tensor_tensor(gt[:, 7], gt[:, 2], gt[:, 7], ALU.subtract))
            link(V.reciprocal(gt[:, 11], gt[:, 5]))
            link(V.tensor_tensor(gt[:, 7], gt[:, 7], gt[:, 11], ALU.mult))
            link(V.tensor_scalar(gt[:, 0], gt[:, 0], 0.0, None, ALU.max))
            dve.wait_ge(gln_ok, 1)
            link(V.tensor_tensor(gt[:, 7], gt[:, 7], gt[:, 6], ALU.add))
            link(V.tensor_tensor(gt[:, 7], gt[:, 7], gt[:, 0], ALU.add))
            step(V.scalar_tensor_tensor(out=gt[:, 8], in0=gt[:, 7], scalar=-1.0, in1=bc(gt[:, 4, 0, :], TB, 1),
                                        op0=ALU.mult, op1=ALU.mult), g_ok, 1)
            link(V.tensor_scalar(gt[:, 9], gt[:, 3], 1.0, None, ALU.add))
            step(V.reciprocal(gt[:, 9], gt[:, 9]), beta_ok, 1)

            def unit(n):
                dve.wait_ge(nroot_ok, n + 1)
                link(V.reciprocal(wsf[:, n], wsf[:, n]))
                V.scalar_tensor_tensor(out=qkv[:, n, :], in0=qkv[:, n, :], scalar=float(P) ** -0.5 if n < H else 1.0,
                                       in1=wsf[:, n], op0=ALU.mult, op1=ALU.mult).then_inc(qk_ok, 1)

            for n in range(4):
                unit(n)
            dve.wait_ge(gcum_ps, 1)
            cum = ps[:, 7, 64:64 + 4 * TB * H].rearrange("p (n b h) -> p n b h", n=4, b=TB)
            link(V.tensor_copy(gcs[:, :, :, :], cum))
            step(V.tensor_tensor(gcs[:, 1], gcs[:, 1], gcs[:, 0], ALU.subtract), gcs_ok, 1)
            for n in range(4, 2 * H):
                unit(n)
            dve.wait_ge(gex_ok, 1)
            link(V.tensor_tensor(gt[:, 11], gex[:, 0], gt[:, 9], ALU.mult))
            dve.wait_ge(zero_ok, 1)

            def prepare(t):
                lk = chain(dve, delta_step, t * DELTA_LINKS)

                def col(v):
                    return bc(v[:, bass.ds(t, 1), :].rearrange("p a h -> p (a h)"), P, 2)

                def differences():
                    dve.wait_ge(dexp_ok, 2 * t + 1)
                    lk(V.tensor_tensor(DX, bank(0, H), col(gcs[:, 0]), ALU.subtract))
                    V.tensor_scalar(DX, DX, 0.0, None, ALU.min).then_inc(dx_ok, 1)

                def queries():
                    dve.wait_ge(dexp_ok, 2 * t + 2)
                    dve.wait_ge(kk_ps, t + 1)
                    if not isinstance(t, int):
                        dve.wait_ge(cur_ok, t * 5)
                    lk(V.tensor_tensor(DX, DX, bc(causal, H, 1), ALU.mult))
                    lk(V.tensor_tensor(QKN, bank(3, H), DX, ALU.mult))

                def matrix():
                    lk(V.tensor_tensor(AT, bank(2, H), DX, ALU.mult))
                    lk(V.tensor_tensor(AT, AT, bank(1, H), ALU.mult))
                    lk(V.tensor_tensor(AT, AT, bc(strict, H, 1), ALU.mult))
                    lk(V.tensor_tensor(YM, AT, bc(lvl[:, 0, :], H, 1), ALU.mult))
                    V.tensor_tensor(TR, bc(ident, H, 1), YM, ALU.subtract).then_inc(r2_ok, 1)

                def operands():
                    lk(V.tensor_tensor(QDN, qkv[:, 0:H, bass.ds(t * P, P)], EGI, ALU.mult))
                    dve.wait_ge(ktok_ps, t + 1)
                    lk(V.tensor_tensor(KBG, bank(4, H), col(gt[:, 11]), ALU.mult))
                    lk(V.tensor_tensor(KDN, bank(4, H), col(gex[:, 1]), ALU.mult))
                    dve.wait_ge(vtok_ps, t + 1)
                    V.tensor_tensor(VB, bank(0, H), col(gt[:, 9]), ALU.mult).then_inc(prep_ok, 1)
                    assert lk.n[0] == DELTA_LINKS
                return differences, queries, matrix, operands

            def invert(t):
                dve.wait_ge(r2_ok, t + 1)
                dve.wait_ge(t_ok, t + 1)
                for s in range(LEVELS):
                    for a in range(2):
                        dve.wait_ge(y_ps, t * 2 * LEVELS + (2 * s + a + 1))
                        V.tensor_tensor(YM[:, 2 * a:2 * a + 2], bank(6 - 3 * a, H)[:, 0:2], bc(lvl[:, s + 1, :], 2, 1),
                                        ALU.mult).then_inc(ym_ok, 1)
                    for a in range(2):
                        dve.wait_ge(tr_ps, t * 2 * LEVELS + (2 * s + a + 1))
                        hp = slice(2 * a, 2 * a + 2)
                        if s < LEVELS - 1:
                            V.tensor_tensor(TM[:, hp], TM[:, hp], bank(t_bank(a), H)[:, 0:2], ALU.subtract).then_inc(t_lvl, 1)
                        V.tensor_tensor(TR[:, hp], TR[:, hp], bank(r_bank(a), H)[:, 0:2], ALU.subtract).then_inc(r_ok, 1)
                    if s < LEVELS - 1:
                        dve.wait_ge(t_lvl, t * 2 * (LEVELS - 1) + (2 * s + 2))
                    dve.wait_ge(r_ok, t * 2 * LEVELS + (2 * s + 2))

            def new_values(t, c):
                r = slice(CH * c, CH * (c + 1))
                dve.wait_ge(uw_ok, 2 * t + 2)
                dve.wait_ge(ws_ps, 2 * t + (c + 1))
                V.tensor_tensor(VN[r], UU[r], bank(6, H)[r], ALU.subtract).then_inc(vn_ok, 1)

            def new_state(t, c):
                dve.wait_ge(su_ps, 2 * t + (c + 1))
                if c:
                    dve.wait_ge(o_ps, t + 1)
                for h in range(H):
                    V.scalar_tensor_tensor(
                        out=ST[:, 1 - c, h, :], in0=ST[:, c, h, :],
                        scalar=gex[:, 2 + c, bass.ds(t, 1), h:h + 1].rearrange("p a b -> p (a b)"),
                        in1=bank(7, H)[:, h, :], op0=ALU.mult, op1=ALU.add).then_inc(st_ok, 1)
                dve.wait_ge(st_ok, (2 * t + (c + 1)) * H)

            for part in prepare(0):
                part()
            with dve.Fori(0, TB - 1) as tb:
                differences, queries, matrix, operands = prepare(tb + 1)
                invert(tb)
                differences()
                new_values(tb, 0)
                queries()
                new_state(tb, 0)
                new_values(tb, 1)
                matrix()
                new_state(tb, 1)
                operands()
            invert(TB - 1)
            for c in range(2):
                new_values(TB - 1, c)
                if c == 0:
                    new_state(TB - 1, c)
            for b in range(TB):
                dve.wait_ge(osq_ok, b + 1)
                V.tensor_reduce(so[:, 0, b], OSQ[b], AX.X, ALU.add).then_inc(oms_ok, 1)
            dve.wait_ge(ort_ok, 1)
            link(V.reciprocal(so[:, 2], so[:, 1]))
            for b in range(TB):
                V.tensor_tensor(O4[:, b], O4[:, b], bc(so[:, 2, b], P, 2), ALU.mult).then_inc(on_ok, 1)
            for b in range(TB):
                dve.wait_ge(ot_ps, b + 1)
                V.scalar_tensor_tensor(out=catT[:, 0:H, b * P:(b + 1) * P], in0=bank(b, H), scalar=pcol[:, NDN:NDN + 1],
                                       in1=zs[:, :, b * P:(b + 1) * P], op0=ALU.mult, op1=ALU.mult).then_inc(cat_ok, 1)
            dve.wait_ge(fnw_in, 16)
            for b in range(TB):
                for half in range(2):
                    n = 2 * b + half
                    dve.wait_ge(op_ps, n + 1)
                    v = xs[:, b, 512 * half:512 * (half + 1)]
                    V.tensor_tensor(v, v, bank(4 + n % 4), ALU.add).then_inc(x1_ok, 1)
                dve.wait_ge(x1_ok, 2 * b + 2)
                dve.wait_ge(s2_ok, b + 1)
                link(V.reciprocal(sm[:, 40 + b:41 + b], sm[:, 24 + b:25 + b]))
                V.scalar_tensor_tensor(out=h2[:, b, :], in0=xs[:, b, :], scalar=sm[:, 40 + b:41 + b], in1=fnw,
                                       op0=ALU.mult, op1=ALU.mult).then_inc(h2_ok, 1)
            for n in range(0, 2 * TB, 2):
                dve.wait_ge(h2t_ps, n + 1)
                V.tensor_copy(h2T[:, 0:4, (n // 2) * P:(n // 2 + 1) * P], bank(2 * (n // 2 % 2), 4)).then_inc(h2t_lo, 1)
            dve.wait_ge(part_ps, 2)
            V.tensor_copy(lg_part, bank(4)).then_inc(part_ok, 1)
            dve.wait_ge(lg_ps, 1)
            link(V.tensor_tensor(lgs[:, :, :], ps[:, 0, 0:TB * E].rearrange("p (b e) -> p b e", b=TB),
                                 bc(bcr[:, 2 * H:], TB, 1), ALU.add))
            for b in range(TB):
                link(V.max(out=v8[:, b, :], in_=lgs[:, b, :]))
                link(V.max_index(i8[:, b, :], v8[:, b, :], lgs[:, b, :]))
            link(V.tensor_copy(tk[:, 0], i8[:, :, 0:TOPK]))
            step(V.tensor_tensor(tk[:, 2], v8[:, :, 0:TOPK], bc(v8[:, :, 0], TOPK, 2), ALU.subtract), top_ok, 1)
            link(V.memset(oh[:, 2:4], 0.0))
            link(V.memset(gi[:, :, :, :], 0.0))
            dve.wait_ge(texp_ok, 1)
            link(V.tensor_reduce(nbf[:, 0, 0:TB], tk[:, 1], AX.X, ALU.add))
            link(V.reciprocal(nbf[:, 0, 8:8 + TB], nbf[:, 0, 0:TB]))
            link(V.tensor_tensor(tk[:, 3], tk[:, 1], bc(nbf[:, 0, 8:8 + TB], TOPK, 2), ALU.mult))
            for k in range(TOPK):
                link(V.tensor_tensor(oh[:, 0], bc(iotaf[:, 0:E], TB, 1), bc(tk[:, 0, :, k], E, 2), ALU.is_equal))
                link(V.tensor_tensor(oh[:, 1], oh[:, 0], bc(tk[:, 3, :, k], E, 2), ALU.mult))
                link(V.tensor_tensor(gi[:, :, :, 0], gi[:, :, :, 0], oh[:, 1], ALU.add))
                link(V.scalar_tensor_tensor(out=oh[:, 3], in0=oh[:, 0], scalar=float(k), in1=oh[:, 3],
                                            op0=ALU.mult, op1=ALU.add))
                ins = V.tensor_tensor(oh[:, 2], oh[:, 2], oh[:, 0], ALU.add)
                if k < TOPK - 1:
                    link(ins)
                else:
                    step(ins, mask_ok, 1)
            link(V.tensor_tensor(oh[:, 1], oh[:, 2], bc(rowbase[:, :], E, 2), ALU.mult))
            link(V.tensor_tensor(gi[:, :, :, 1], oh[:, 1], oh[:, 3], ALU.add))
            dve.wait_ge(rank_ps, 1)
            rk = ps[:, 1, 0:TB * E].rearrange("p (b e) -> p b e", b=TB)
            link(V.tensor_scalar(rank[:, :, :], rk, 1.0, None, ALU.add))
            link(V.tensor_tensor(rank[:, :, :], rank[:, :, :], oh[:, 2], ALU.mult))
            link(V.tensor_scalar(rank[:, :, :], rank[:, :, :], -1.0, None, ALU.add))
            link(V.tensor_scalar(nbf[:, 0, :], ps[:, 1, TB * E:(TB + 1) * E], float(SLOTS - 1), None, ALU.add))
            link(V.tensor_copy(nbi[:, :], nbf[:, 0, :]))
            link(V.tensor_scalar(nbi[:, :], nbi[:, :], SLOTS.bit_length() - 1, None, ALU.arith_shift_right))
            link(V.tensor_copy(nbf[:, 0, :], nbi[:, :]))
            link(V.tensor_scalar(nbf[:, 0, :], nbf[:, 0, :], 1.0, None, ALU.max))
            link(V.memset(nbf[:, 1, :], 1.0))
            link(V.tensor_tensor_scan(out=nbf[:, 2, :], data0=nbf[:, 1, :], data1=nbf[:, 0, :], initial=0.0,
                                      op0=ALU.mult, op1=ALU.add))
            link(V.tensor_scalar(nbf[:, 3, :], nbf[:, 2, :], pidx[:, 0:1], None, ALU.is_le))
            link(V.tensor_reduce(ebc[:, 0:1], nbf[:, 3, :], AX.X, ALU.add))
            link(V.tensor_tensor(nbf[:, 3, :], nbf[:, 3, :], nbf[:, 2, :], ALU.mult))
            link(V.tensor_reduce(ebc[:, 1:2], nbf[:, 3, :], AX.X, ALU.max))
            link(V.tensor_tensor(ebc[:, 3:4], pidx[:, 0:1], ebc[:, 1:2], ALU.subtract))
            link(V.tensor_scalar(ebc[:, 2:3], ebc[:, 0:1], float(E), float(T), ALU.is_ge, ALU.mult))
            link(V.scalar_tensor_tensor(out=ebc[:, 3:4], in0=ebc[:, 3:4], scalar=float(SLOTS), in1=ebc[:, 2:3],
                                        op0=ALU.mult, op1=ALU.add))
            link(V.tensor_scalar(ebc[:, 1:2], ebc[:, 3:4], float(T), None, ALU.min))
            step(V.tensor_scalar(ebc[:, 0:1], ebc[:, 0:1], float(E - 1), None, ALU.min), ebc_ok, 1)
            link(V.memset(tab[0:1, 0:1], 0))
            link(V.tensor_copy(tab[0:1, 1:E + 1], nbf[0:1, 2, :]))
            dve.wait_ge(tab_ps, 1)
            link(V.tensor_copy(tab[0:1, E + 1:USED], ps[0:1, 2, 0:2 * P]))
            link(V.tensor_scalar(tab[0:1, USED:PAIRS], nbf[0:1, 2, :], float(NU), float(-NU), ALU.mult, ALU.add))
            link(V.tensor_scalar(tab[0:1, E:E + 1], nbf[0:1, 2, E - 1:E], 1.0, None, ALU.add))
            link(V.tensor_scalar(tab[0:1, PAIRS:], tab[0:1, E:E + 1], 1, None, ALU.arith_shift_right))
            step(V.tensor_scalar(tab[0:1, E:E + 1], tab[0:1, PAIRS:], 1, None, ALU.arith_shift_left), tab_ok, 1)

            def make_hot(g, count):
                e = dve.value_load(tab[0:1, bass.ds(g + (E + 1), 1)], min_val=0, max_val=E - 1)
                s0 = dve.value_load(tab[0:1, bass.ds(g + (E + 1 + P), 1)], min_val=0, max_val=T)
                V.tensor_copy(selu[:, :], E3[:, bass.ds(e, 1)].to_broadcast([96, SLOTS])).then_inc(sel_step, 1)
                V.tensor_copy(gie[:, :, :], gi[:, :, bass.ds(e, 1), :].rearrange("p b a c -> p b (a c)")).then_inc(sel_step, 1)
                slots = bc(bc(iotaf[:, bass.ds(s0, SLOTS)], Q, 1), TB, 1)
                mine = bc(bc(rank[:, :, bass.ds(e, 1)].rearrange("p b a -> p (b a)"), Q, 2), SLOTS, 3)
                dve.wait_ge(sel_step, count * 2)
                step(V.tensor_tensor(hot[:, :, :, :], slots, mine, ALU.is_equal), hot_ok, count)

            make_hot(0, 1)
            pairs = dve.value_load(tab[0:1, PAIRS:PAIRS + 1], min_val=E // 2, max_val=MAXB // 2)

            def swiglu(g, i, p):
                dve.wait_ge(idx_ps, g + 1)
                dve.wait_ge(scat[p], i * 16)
                V.tensor_copy(wslot[:, p:p + 1], ps[:, 7, 0:1]).then_inc(info_step, 1)
                step(V.tensor_scalar(rowf[:, p:p + 1], ps[:, 7, 1:2], OOB, float(Q), ALU.add, ALU.mult), info_step, g * 3 + 2)
                step(V.tensor_tensor(rowf[:, p:p + 1], rowf[:, p:p + 1], qcol[:, :], ALU.add), info_step, g * 3 + 3)
                V.tensor_copy(rowi[:, p:p + 1], rowf[:, p:p + 1]).then_inc(slot_ok, 1)
                dve.wait_ge(dnb_used, g)
                step(V.tensor_copy(seld[:, :], selu[:, :]), seld_ok, g + 1)
                dve.wait_ge(gub_used, g + 1)
                make_hot(g + 1, g + 2)
                dve.wait_ge(w_used, g * NU + NGU)
                step(V.tensor_scalar(gc[:, :], ps[:, 0, 0:QD], LIMIT, None, ALU.min), gc_ok, g + 1)
                step(V.tensor_scalar(uc[:, :], ps[:, 0, QD:], -LIMIT, LIMIT, ALU.max, ALU.min), uc_step, g * 2 + 1)
                step(V.scalar_tensor_tensor(out=uc[:, :], in0=uc[:, :], scalar=1.0, in1=gc[:, :], op0=ALU.add,
                                            op1=ALU.mult), uc_step, g * 2 + 2)
                dve.wait_ge(sg_ok, g + 1)
                dve.wait_ge(at_ps, g)
                step(V.tensor_tensor(act_[:, :], uc[:, :], sg[:, :], ALU.mult), act_ok, g + 1)

            with dve.Fori(0, pairs) as i:
                for p in range(2):
                    swiglu(2 * i + p, i, p)
            dve.wait_ge(fnw_in, 32)
            for b in range(TB):
                dve.wait_ge(y_in[b], 16)
                for k in range(TOPK):
                    y = ring[:, (b * TOPK + k) * D:(b * TOPK + k + 1) * D]
                    ins = V.tensor_tensor(xs[:, b, :], xs[:, b, :], y, ALU.add)
                    if k < TOPK - 1:
                        step(ins, fin_add, b * (TOPK - 1) + k + 1)
                    else:
                        step(ins, fin_sum, b + 1)
            for b in range(TB):
                dve.wait_ge(fin_rt, b + 1)
                step(V.reciprocal(sm[:, 44 + b:45 + b], sm[:, 32 + b:33 + b]), fin_rc, b + 1)
                V.scalar_tensor_tensor(out=ring[:, b * TOPK * D:b * TOPK * D + D], in0=xs[:, b, :],
                                       scalar=sm[:, 44 + b:45 + b], in1=fnw, op0=ALU.mult,
                                       op1=ALU.mult).then_inc(fin_o, 1)

        @block.tensor
        def _(pe):
            mm, tr = nc.tensor.matmul, nc.tensor.transpose
            pe.wait_ge(const_ok, 6)
            pe.wait_ge(par_in, 16 * (3 + CONV))
            tr(ps[:, 7, 0:61], prow[:, :], ident[0:61, 0:61]).then_inc(pcol_ps, 1)
            pe.wait_ge(pcol_ok, 1)
            pe.wait_ge(xn_ok, TB)
            for k in range(KD):
                for b in range(TB):
                    last = tr(bank(k)[:, b * P:(b + 1) * P], xn[:, b, k * P:(k + 1) * P], ident)
                last.then_inc(xt_ps, 1)
            pe.wait_ge(ht_even, KD // 2)
            pe.wait_ge(ht_odd, KD // 2)

            def project(buf, half, b):
                for k in range(KD):
                    last = mm(bank(b), win[:, buf, k, half * P:(half + 1) * P], hT[:, k, :], start=k == 0, stop=k == KD - 1)
                last.then_inc(proj_ps, 1)

            def four_chunks(out, w, src, s):
                for k in range(KD):
                    q = k % Q
                    last = mm(out[SLOTS * q:SLOTS * (q + 1), :], w[:, k, :], src[:, k, :], start=k < Q, stop=k >= Q)
                last.then_inc(s, 1)

            def sum_chunks(out, part, n, s):
                for b in range(TB):
                    last = mm(out[:, b * n:(b + 1) * n], part[:, b * P:(b + 1) * P], S4[:, 0:n], start=True, stop=True)
                last.then_inc(s, 1)

            pe.wait_ge(wba_in, 16)
            four_chunks(bank(6), wba, hT, part_ps)
            with pe.Fori(0, 3) as i:
                for r in range(4):
                    n = 4 * i + r
                    if r % 2 == 0:
                        pe.wait_ge(win_in[r // 2], i * 16 + 16)
                    project(r // 2, r % 2, r % 2)
                    pe.wait_ge(conv_ok, n)
            pe.wait_ge(const_ok, 7)
            pe.wait_ge(part_ok, 1)
            sum_chunks(bank(7), ba_part, 2 * H, ba_ps)
            for n in range(NQKV, NQKV + 2 * H):
                piece = n // 2
                if n % 2 == 0:
                    pe.wait_ge(win_in[piece % 2], (piece // 2 + 1) * 16)
                if n == NQKV + 1:
                    pe.wait_ge(conv_ok, NQKV)
                    for i in range(2 * H):
                        pe.wait_ge(sq_ok, i + 1)
                        if i >= 6:
                            pe.wait_ge(nroot_ok, i - 4)
                        mm(bank(nrm_bank(i)), ones, wsf[:, i], start=True, stop=True).then_inc(nrm_ps, 1)
                    pe.wait_ge(nroot_ok, 1)
                if n > NQKV + 1:
                    pe.wait_ge(silu_ok, n - 1)
                if n == NQKV + 2:
                    pe.wait_ge(g_ok, 1)
                    for i, c in enumerate((causal, same, first, second)):
                        last = mm(ps[:, 7, 64 + i * TB * H:64 + (i + 1) * TB * H], c, gt[:, 8].rearrange("p b h -> p (b h)"),
                                  start=True, stop=True)
                    last.then_inc(gcum_ps, 1)
                project(piece % 2, n % 2, n % 2)
            pe.wait_ge(silu_ok, NQKV + 2 * H)
            pe.wait_ge(nroot_ok, 2 * H)
            pe.wait_ge(gcs_ok, 1)

            def heads(b, f, s):
                for h in range(H):
                    lhsT, rhs = f(h)
                    last = mm(bank(b, H)[:, h, :], lhsT, rhs, start=True, stop=True)
                last.then_inc(s, 1)

            def prepare(t):
                def now(n, h):
                    return qkv[:, n + h, bass.ds(t * P, P)]

                def flat(v):
                    return v.rearrange("p a b -> p (a b)")

                def g_rows():
                    pe.wait_ge(grow_ok, 2 * t + 1)
                    mm(bank(0), ones, flat(GUM), start=True, stop=True).then_inc(grow_ps, 1)

                def products():
                    pe.wait_ge(grow_ok, 2 * t + 2)
                    mm(bank(1), ones, flat(BI), start=True, stop=True).then_inc(brow_ps, 1)
                    pe.wait_ge(kv_ok, 2 * t + 2)
                    for h in range(H):
                        mm(bank(2, H)[:, h, :], KTS[:, h, :], now(H, h), start=True, stop=True)
                    heads(3, lambda h: (KTS[:, h, :], now(0, h)), kk_ps)

                def k_tokens():
                    for h in range(H):
                        last = tr(bank(4, H)[:, h, :], KTS[:, h, :], ident)
                    last.then_inc(ktok_ps, 1)

                def v_tokens():
                    pe.wait_ge(dx_ok, t + 1)
                    for h in range(H):
                        last = tr(bank(0, H)[:, h, :], VTS[:, h, :], ident)
                    last.then_inc(vtok_ps, 1)

                def transposed():
                    pe.wait_ge(r2_ok, t + 1)
                    for h in range(H):
                        last = tr(bank(1, H)[:, h, :], TR[:, h, :], ident)
                    last.then_inc(t2_ps, 1)
                return g_rows, products, k_tokens, v_tokens, transposed

            def invert(t):
                pe.wait_ge(t_ok, t + 1)
                for s in range(LEVELS):
                    for a in range(2):
                        if s:
                            pe.wait_ge(t_lvl, t * 2 * (LEVELS - 1) + (2 * s - 1 + a))
                            pe.wait_ge(r_ok, t * 2 * LEVELS + (2 * s - 1 + a))
                        for i in range(2):
                            last = mm(bank(6 - 3 * a, H)[:, i, :], AT[:, 2 * a + i, :], TM[:, 2 * a + i, :],
                                      start=True, stop=True)
                        last.then_inc(y_ps, 1)
                    for a in range(2):
                        pe.wait_ge(ym_ok, t * 2 * LEVELS + (2 * s + a + 1))
                        if s < LEVELS - 1:
                            for i in range(2):
                                mm(bank(t_bank(a), H)[:, i, :], TR[:, 2 * a + i, :], YM[:, 2 * a + i, :],
                                   start=True, stop=True)
                        for i in range(2):
                            last = mm(bank(r_bank(a), H)[:, i, :], YM[:, 2 * a + i, :], TR[:, 2 * a + i, :],
                                      start=True, stop=True)
                        last.then_inc(tr_ps, 1)
                pe.wait_ge(r_ok, t * 2 * LEVELS + 2 * LEVELS)
                heads(1, lambda h: (TR[:, h, :], VB[:, h, :]), uw_ps)
                heads(2, lambda h: (KBG[:, h, :], TR[:, h, :]), uw_ps)

            def state_values(t, c):
                heads(6, lambda h: (WT[:, h, :], ST[:, c, h, :]), ws_ps)

            def state_change(t, c):
                pe.wait_ge(vn_ok, 2 * t + (c + 1))
                pe.wait_ge(cur_ok, 5 * t + 5)
                kdz = (KDZ0, KDZ1)[c]
                heads(7, lambda h: (kdz[:, h, :], VN[:, h, :]), su_ps)

            def outputs(t):
                pe.wait_ge(oc_ok, t)
                for h in range(H):
                    o = bank(5, H)[:, h, :]
                    mm(o, QD0[:, h, :], ST[:, 0, h, :], start=True, stop=False)
                    mm(o, QD1[:, h, :], ST[:, 1, h, :], start=False, stop=False)
                    last = mm(o, QKT[:, h, :], VN[:, h, :], start=False, stop=True)
                last.then_inc(o_ps, 1)

            pe.wait_ge(qk_ok, 2 * H)
            pe.wait_ge(zero_ok, 1)
            for part in prepare(0):
                part()
            with pe.Fori(0, TB - 1) as tb:
                g_rows, products, k_tokens, v_tokens, transposed = prepare(tb + 1)
                invert(tb)
                g_rows()
                pe.wait_ge(uw_ok, 2 * tb + 2)
                pe.wait_ge(st_ok, 2 * tb * H)
                state_values(tb, 0)
                products()
                state_change(tb, 0)
                k_tokens()
                pe.wait_ge(st_ok, (2 * tb + 1) * H)
                state_values(tb, 1)
                v_tokens()
                state_change(tb, 1)
                outputs(tb)
                transposed()
            invert(TB - 1)
            pe.wait_ge(uw_ok, 2 * TB)
            pe.wait_ge(st_ok, 2 * (TB - 1) * H)
            for c in range(2):
                if c:
                    pe.wait_ge(st_ok, (2 * TB - 1) * H)
                state_values(TB - 1, c)
                if c == 0:
                    state_change(TB - 1, c)
                else:
                    pe.wait_ge(vn_ok, 2 * TB)
            outputs(TB - 1)
            for b in range(TB):
                pe.wait_ge(on_ok, b + 1)
                for h in range(H):
                    last = tr(bank(b, H)[:, h, :], O4[:, b, h, :], ident)
                last.then_inc(ot_ps, 1)
            pe.wait_ge(cat_ok, TB)
            pe.wait_ge(pw_in, 16)
            for g in range(4):
                pe.wait_ge(pool_mix, g + 1)
                mm(bank(g), poolw[:, g, :], catT[:, H + g, :], start=True, stop=True).then_inc(pool_ps, 1)
            pe.wait_ge(pooled_ok, 4)
            pe.wait_ge(wout_in, 16)
            for b in range(TB):
                for half in range(2):
                    n = 2 * b + half
                    if n >= 4:
                        pe.wait_ge(x1_ok, n - 3)
                    for k in range(KD):
                        last = mm(bank(4 + n % 4), catT[:, k, b * P:(b + 1) * P], wout[:, k, 512 * half:512 * (half + 1)],
                                  start=k == 0, stop=k == KD - 1)
                    last.then_inc(op_ps, 1)
            for b in range(TB):
                pe.wait_ge(h2_ok, b + 1)
                for half in range(2):
                    n = 2 * b + half
                    if b >= 2:
                        pe.wait_ge((h2t_lo, h2t_hi)[half], b - 1)
                    for i in range(4):
                        k = 4 * half + i
                        last = tr(bank(2 * (b % 2) + half, 4)[:, i, :], h2[:, b, k * P:(k + 1) * P], ident)
                    last.then_inc(h2t_ps, 1)
            pe.wait_ge(h2t_lo, TB)
            pe.wait_ge(h2t_hi, TB)
            pe.wait_ge(wrt_in, 16)
            four_chunks(bank(4), wrt, h2T, part_ps)
            pe.wait_ge(part_ok, 2)
            sum_chunks(bank(0), lg_part, E, lg_ps)
            pe.wait_ge(mask_ok, 1)
            for b in range(TB + 1):
                for a in range(min(b + 1, TB)):
                    last = mm(ps[:, 1, b * E:(b + 1) * E], lowS if a == b else ones, oh[:, 2, a, :], start=a == 0,
                              stop=a == min(b, TB - 1))
            last.then_inc(rank_ps, 1)
            pe.wait_ge(ebc_ok, 1)
            for i in range(2):
                last = mm(ps[0:1, 2, i * P:(i + 1) * P], ebc[:, i:i + 1], ident, start=True, stop=True)
            last.then_inc(tab_ps, 1)

            def gather(count, free):
                pe.wait_ge(hot_ok, count)
                if free is not None:
                    pe.wait_ge(xg_ok, free)
                for b in range(TB):
                    for q in range(Q):
                        last = mm(ps[SLOTS * q:SLOTS * (q + 1), 2, 0:QD], hot[:, b, 0, :], h2[:, b, q * QD:(q + 1) * QD],
                                  start=b == 0, stop=b == TB - 1)
                last.then_inc(gat_ps, 1)
                if free is not None:
                    pe.wait_ge(slot_ok, free)
                for b in range(TB):
                    last = mm(ps[:, 7, 0:2], hot[:, b].rearrange("p q s -> p (q s)"), gie[:, b, :], start=b == 0,
                              stop=b == TB - 1)
                last.then_inc(idx_ps, 1)

            def rows_T(count, free):
                pe.wait_ge(xg_ok, count)
                if free is not None:
                    pe.wait_ge(xgt_ok, free)
                for i in range(2):
                    last = tr(bank(3, 4)[:, i, :], xg[:, i * P:(i + 1) * P], ident)
                last.then_inc(xgt_ps, 1)

            pe.wait_ge(tab_ok, 1)
            gather(1, None)
            rows_T(1, None)
            pe.wait_ge(bias_ok, 1)

            def expert_block(g, j, turn):
                def landed(u):
                    slot, t = slot_of(j, u)
                    pe.wait_ge(slot_in[slot], (turn + t + 1) * 16)
                    return ring[:, slot * UNIT:(slot + 1) * UNIT].rearrange("p (s c) -> p s c", s=2)

                pe.wait_ge(xgt_ok, g + 1)
                pe.wait_ge(act_ok, g)
                for q in range(Q):
                    last = mm(ps[SLOTS * q:SLOTS * (q + 1), 0, :], selu[:, :],
                              bias3[:, 0:2 * D].rearrange("p (s c) -> p s c", s=2)[:, :, q * QD:(q + 1) * QD],
                              start=True, stop=False)
                last.then_inc(gub_used, 1)
                for u in range(NGU):
                    w = landed(u)
                    for q in range(Q):
                        last = mm(ps[SLOTS * q:SLOTS * (q + 1), 0, :],
                                  xgT[:, u % 2, SLOTS * (u // 2):SLOTS * (u // 2 + 1)],
                                  w[:, :, q * QD:(q + 1) * QD], start=False, stop=u == NGU - 1)
                    last.then_inc(w_used, 1)
                gather(g + 2, g + 1)
                pe.wait_ge(act_ok, g + 1)
                pe.wait_ge(actt_ok, g)
                for i in range(2):
                    last = tr(bank(4, 4)[:, i, :], act_[:, i * P:(i + 1) * P], ident)
                last.then_inc(at_ps, 1)
                rows_T(g + 2, g + 1)
                pe.wait_ge(seld_ok, g + 1)
                pe.wait_ge(ys_ok, g)
                for q in range(Q):
                    last = mm(ps[SLOTS * q:SLOTS * (q + 1), 1, 0:QD], seld[:, :],
                              bias3[:, 2 * D + q * QD:2 * D + (q + 1) * QD], start=True, stop=False)
                last.then_inc(dnb_used, 1)
                pe.wait_ge(actt_ok, g + 1)
                for u in range(NGU, NU):
                    w = landed(u)
                    for i in range(2):
                        c = 2 * (u - NGU) + i
                        for q in range(Q):
                            last = mm(ps[SLOTS * q:SLOTS * (q + 1), 1, 0:QD],
                                      actT[:, c % 2, SLOTS * (c // 2):SLOTS * (c // 2 + 1)],
                                      w[:, i, q * QD:(q + 1) * QD], start=False, stop=c == KD - 1)
                    last.then_inc(w_used, 1)

            with pe.Fori(0, E // UNROLL) as grp:
                for j in range(UNROLL):
                    lo = pe.value_load(tab[0:1, bass.ds(UNROLL * grp + j, 1)], min_val=0, max_val=MAXB)
                    hi = pe.value_load(tab[0:1, bass.ds(UNROLL * grp + (j + 1), 1)], min_val=0, max_val=MAXB)
                    with pe.Fori(lo, hi) as g:
                        expert_block(g, j, TURNS * grp)


_INS = ['x', 'attn_norm_w', 'w_in', 'conv_w', 'a_log', 'dt_bias', 'dn_norm_w', 'pool_w', 'pool_scale', 'w_out',
        'ffn_norm_w', 'w_router', 'b_router', 'w_gate_up', 'b_gate_up', 'w_down', 'b_down', 'final_norm_w']


def kernel(**inputs):
    import numpy as _np
    import concourse.bacc as _bacc
    from concourse.bass_utils import run_bass_kernel_spmd as _run

    nc = _bacc.Bacc("TRN2", target_bir_lowering=False, num_devices=1)
    arrays, args = {}, []
    for name in _INS:
        a = _np.ascontiguousarray(inputs[name])
        arrays[f"in_{name}_dram"] = a
        args.append(nc.dram_tensor(f"in_{name}_dram", a.shape, mybir.dt.from_np(a.dtype), kind="ExternalInput").ap())
    args.append(nc.dram_tensor("out_dram", (1, T, D), F32, kind="ExternalOutput").ap())
    args.append(nc.dram_tensor("pair_rows_dram", (T * TOPK * Q, QD), F32, kind="Internal").ap())
    moe_block(nc, *args)
    r = _run(nc, [arrays], core_ids=[0])
    return r.results[0]["out_dram"]
```

```python
from contextlib import ExitStack

import concourse.bass as bass
from concourse import mybir

F32, I32, U32, BF16 = mybir.dt.float32, mybir.dt.int32, mybir.dt.uint32, mybir.dt.bfloat16
ALU, ACT, AX = mybir.AluOpType, mybir.ActivationFunctionType, mybir.AxisListType

P = 128
D = 1024
T = 512
TB = T // P
KD = D // P
H = 4
CONV = 4
CH = 64
WINDOWS = (2, 4, 8, 16)
PAD = max(WINDOWS)
NQKV = 3 * H
E, TOPK = 32, 4
SLOTS = 32
Q = P // SLOTS
QD = D // Q
MAXB = T * TOPK // SLOTS + E
C_Z, C_BA, C_P = NQKV * P, (NQKV + H) * P, (NQKV + H) * P + 2 * H
RMS_EPS, L2_EPS = 1e-6, 1e-6
LIMIT, ALPHA = 7.0, 1.702
OOB = 4096.0

UNIT = 2 * D
NGU = KD
NU = KD + KD // 2
RING = 18
UNROLL = 3
TURNS = UNROLL * NU // RING
AHEAD = 4
EARLY = 2


def moe_block(nc, x, attn_norm_w, w_in, conv_w, a_log, dt_bias, dn_norm_w, pool_w, pool_scale, w_out,
              ffn_norm_w, w_router, b_router, w_gate_up, b_gate_up, w_down, b_down, final_norm_w,
              out, pair_rows, x1_rows):
    ctx = ExitStack()
    with ctx:
        def sb(name, shape, dt=F32):
            return ctx.enter_context(nc.sbuf_tensor(name, shape, dt))

        def sem(name):
            return ctx.enter_context(nc.semaphore(name))

        ring = sb("ring", [P, RING * UNIT])
        late = ring[:, EARLY * UNIT:]

        def room(at, *dims):
            n = 1
            for d in dims:
                n *= d
            flat = late[:, at:at + n]
            if len(dims) == 2:
                return flat.rearrange("p (a b) -> p a b", a=dims[0])
            if len(dims) == 3:
                return flat.rearrange("p (a b c) -> p a b c", a=dims[0], b=dims[1])
            return flat

        qkv = room(0, NQKV, T)
        zs = room(6144, H, T)
        win = room(8192, 2, KD, 256)
        pbuf = room(12288, 4, PAD + T)
        junk = room(14400, D)
        cbuf = [room(14400 + 512 * i, T) for i in range(2)]
        junk2 = room(10240, D)
        wout = room(16384, KD, D)
        AT, QKT, TM, TR, YM, KTS, VTS, KBG = [room(8192 + 512 * i, H, P) for i in range(8)]
        VB, GUM, BI = [room(14400 + 512 * i, H, P) for i in range(3)]
        OSQ = (AT, TM, TR, YM)
        h2T = room(24576, KD, T)
        h2 = room(12288, TB, D)
        braw = room(16384, 3 * D)[0:96, :]
        brem = room(16384 + 3 * D, 3 * D)[0:96, :]
        bias_tmp = ring[0:96, UNIT:UNIT + 3 * D // 2].bitcast(BF16)

        X0 = RING - 2
        xs = ring[:, X0 * UNIT:].rearrange("p (b d) -> p b d", b=TB)
        hbuf = sb("hbuf", [P, KD * T])
        hT = hbuf[:, :].rearrange("p (k t) -> p k t", k=KD)
        cat = sb("cat", [P, KD * T])
        catT = cat[:, :].rearrange("p (k t) -> p k t", k=KD)
        xn = cat[:, :].rearrange("p (b d) -> p b d", b=TB)
        wsf = room(24576, 8, T)
        WS = late[:, 24576:28672].rearrange("p (n a b) -> p n a b", n=8, a=H)
        KDZ0, KDZ1, QD0, QD1, VN, UU, WT, DX = [WS[:, i] for i in range(8)]
        O4 = hbuf[:, 0:TB * H * P].rearrange("p (b h c) -> p b h c", b=TB, h=H)
        QKN, QDN, KDN, EGI = [hbuf[:, (TB + i) * H * P:(TB + i + 1) * H * P].rearrange("p (h c) -> p h c", h=H)
                              for i in range(4)]
        ba_part = wsf[:, 7]
        lg_part = cat[:, 1536:2048]
        aux = sb("aux", [P, 2 * H * P + 10 * P])
        ST = aux[:, 0:2 * H * P].rearrange("p (c h d) -> p c h d", c=2, h=H)
        lvl = aux[:, 2 * H * P:(2 * H + 6) * P].rearrange("p (s c) -> p s c", s=6)
        poolw = aux[:, (2 * H + 6) * P:].rearrange("p (g c) -> p g c", g=4)
        h2p = [v.bitcast(BF16).rearrange("p (b d) -> p b d", b=TB) for v in (
            hbuf[:, 0:TB * D // 2], hbuf[:, TB * D // 2:], aux[:, 0:TB * D // 2])]
        cst = sb("cst", [P, 8, P])
        ident, ones, same, lowS, causal, strict, first, second = [cst[:, i, :] for i in range(8)]
        E3 = sb("E3", [96, SLOTS], BF16)
        iotas = room(15936, 3, P).bitcast(I32)
        iotaf = sb("iotaf", [P, T + SLOTS])
        cstb = sb("cstb", [P, 2, P], BF16)
        maskb = sb("maskb", [P, TB, E], BF16)
        prow = sb("prow", [61, P])
        pcol = sb("pcol", [P, 61])
        NANW, NCV, NDN, NPS = 0, 8, 56, 57
        sm = sb("sm", [P, 48])
        epsc = sb("epsc", [P, 2])
        gt = sb("gt", [P, 12, TB, H])
        gcs = sb("gcs", [P, 4, TB, H])
        gex = sb("gex", [P, 4, TB, H])
        wrt = sb("wrt", [P, KD, E])
        wba = sb("wba", [P, KD, SLOTS])
        S4 = sb("S4", [P, SLOTS])
        so = sb("so", [P, 3, TB, H])
        bcr = sb("bcr", [P, 2 * H + E])
        shared = sb("shared", [P, 2 * (PAD + T)])
        pool_t = shared[:, :].rearrange("p (a b) -> p a b", a=2)
        fnw = shared[:, 0:D]
        bias3 = cat[0:96, 0:3 * D // 2].bitcast(BF16)
        icnt = sb("icnt", [P, PAD])
        lgs = sb("lgs", [P, TB, E])
        v8 = sb("v8", [P, TB, 8])
        i8 = sb("i8", [P, TB, 8], U32)
        tk = sb("tk", [P, 4, TB, TOPK])
        oh, ohw = [cat[:, a:a + 512].rearrange("p (b e k) -> p b e k", b=TB, e=E) for a in (2560, 3072)]
        maskf = cat[:, 3712:3840].rearrange("p (b e) -> p b e", b=TB)
        chn = cat[:, 3584:3712].rearrange("p (b e) -> p b e", b=TB)
        nbi = sb("nbi", [P, E], I32)
        nbf = sb("nbf", [P, 4, E])
        ebc = sb("ebc", [P, 4])
        rowbase = sb("rowbase", [P, TB])
        pidx = sb("pidx", [P, 1])
        rank = sb("rank", [P, TB, E])
        gi = sb("gi", [P, TB, E, 2])
        tab = sb("tab", [1, 3 * E + 2 + 2 * P], I32)
        USED, PAIRS = E + 1 + 2 * P, 2 * E + 1 + 2 * P
        VISIT = PAIRS + 1
        key = cat[:, 2336:2400].rearrange("p (n e) -> p n e", n=2)
        kcol = sb("kcol", [P, 4])
        pml = cat[:, 2048:2304].rearrange("p (n c) -> p n c", n=2)
        hot = cat[:, 1536:1792].bitcast(BF16).rearrange("p (b q s) -> p b q s", b=TB, q=Q)
        gip = sb("gip", [P, TB, E, 6], BF16)
        gie = sb("gie", [P, TB, 6], BF16)
        selu = sb("selu", [96, SLOTS], BF16)
        seld = sb("seld", [96, SLOTS], BF16)
        xg = cat[:, 2048:2304]
        xgT = cat[:, 2304:2560].rearrange("p (i c) -> p i c", i=2)
        gc = cat[:, 2560:2816]
        sg = cat[:, 2816:3072]
        uc = cat[:, 3072:3328]
        act_ = cat[:, 3328:3584]
        actT = cat[:, 3584:3840].rearrange("p (i c) -> p i c", i=2)
        ys = [cat[:, 3840:4096], cat[:, 1792:2048]]
        wslot = sb("wslot", [P, 2, 2])
        rowf = sb("rowf", [P, 2])
        rowi = sb("rowi", [P, 2], I32)
        qcol = sb("qcol", [P, 1])

        ps = ctx.enter_context(nc.psum_tensor("ps", [P, 8, 512], F32))

        def bank(b, a=None):
            v = ps[:, b, :]
            return v.rearrange("p (a b) -> p a b", a=a) if a else v

        def bc(v, n, at):
            return v.unsqueeze(at).to_broadcast([*v.shape[:at], n, *v.shape[at:]])

        x_in = [sem(f"x_in{i}") for i in range(TB)]
        par_in, wba_in, bc_in, pw_in, wrt_in, fnw_in, wout_in, braw_in = [sem(n) for n in (
            "par_in", "wba_in", "bc_in", "pw_in", "wrt_in", "fnw_in", "wout_in", "braw_in")]
        win_in = [sem(f"win_in{i}") for i in range(2)]
        slot_in = [sem(f"slot_in{i}") for i in range(RING)]
        y_in = [sem(f"y_in{i}") for i in range(TB)]
        iota_ok, const_ok, zero_ok, lvl_ok, pool_step, pool_mix, bias_ok = [sem(n) for n in (
            "iota_ok", "const_ok", "zero_ok", "lvl_ok", "pool_step", "pool_mix", "bias_ok")]
        std_ok, rstd_ok, xn_ok, pcol_ps, pcol_ok, xt_ps, ht_even, ht_odd = [sem(n) for n in (
            "std_ok", "rstd_ok", "xn_ok", "pcol_ps", "pcol_ok", "xt_ps", "ht_even", "ht_odd")]
        proj_ps, tap_ok, conv_step, conv_ok, silu_ok, sq_ok, nrm_ps, nroot_ok, qk_ok, ba_ps = [sem(n) for n in (
            "proj_ps", "tap_ok", "conv_step", "conv_ok", "silu_ok", "sq_ok", "nrm_ps", "nroot_ok", "qk_ok", "ba_ps")]
        dve_step, gin_ok, gexp_in, gln_in, g_ok, gcum_ps, gcs_ok, gex_ok = [sem(n) for n in (
            "dve_step", "gin_ok", "gexp_in", "gln_in", "g_ok", "gcum_ps", "gcs_ok", "gex_ok")]
        grow_ok, kv_ok, grow_ps, brow_ps, kk_ps, ktok_ps, dx_ok, dexp_ok, delta_step, prep_ok = [sem(n) for n in (
            "grow_ok", "kv_ok", "grow_ps", "brow_ps", "kk_ps", "ktok_ps", "dx_ok", "dexp_ok", "delta_step", "prep_ok")]
        r2_ok, t2_ps, t_ok, y_ps, ym_ok, tr_ps, uw_ps, uw_ok, ws_ps, vn_ok, su_ps, st_ok = [sem(n) for n in (
            "r2_ok", "t2_ps", "t_ok", "y_ps", "ym_ok", "tr_ps", "uw_ps", "uw_ok", "ws_ps", "vn_ok", "su_ps", "st_ok")]
        o_ps, osq_ok, oms_ok, ort_ok, on_ok, ot_ps, cat_ok = [sem(n) for n in (
            "o_ps", "osq_ok", "oms_ok", "ort_ok", "on_ok", "ot_ps", "cat_ok")]
        pool_ps, pooled_ok, op_ps, x1_ok, s2_ok, h2_ok, h2t_ps, h2t_lo, lg_ps = [sem(n) for n in (
            "pool_ps", "pooled_ok", "op_ps", "x1_ok", "s2_ok", "h2_ok", "h2t_ps", "h2t_lo", "lg_ps")]
        top_ok, texp_ok, mask_ok, rank_ps, ebc_ok, tab_ps, tab_ok, r_ok = [sem(n) for n in (
            "top_ok", "texp_ok", "mask_ok", "rank_ps", "ebc_ok", "tab_ps", "tab_ok", "r_ok")]
        info_step, slot_ok, seld_ok, sel_step, hot_ok, gat_ps, idx_ps, xg_ok, xgt_ps, xgt_ok = [sem(n) for n in (
            "info_step", "slot_ok", "seld_ok", "sel_step", "hot_ok", "gat_ps", "idx_ps", "xg_ok", "xgt_ps", "xgt_ok")]
        gub_used, w_used, gc_ok, uc_step, sg_ok, act_ok, at_ps, actt_ok, dnb_used, ys_ok, scat0, scat1 = [sem(n) for n in (
            "gub_used", "w_used", "gc_ok", "uc_step", "sg_ok", "act_ok", "at_ps", "actt_ok", "dnb_used", "ys_ok",
            "scattered_even", "scattered_odd")]
        scat = (scat0, scat1)
        fin_add, fin_sum, fin_sq, fin_rt, fin_rc, fin_o, stored, act_step = [sem(n) for n in (
            "fin_add", "fin_sum", "fin_sq", "fin_rt", "fin_rc", "fin_o", "stored", "act_step")]
        h2t_hi, t_lvl, bias_home, gi_ok, less_ok, h2p_ok, beta_ok, vtok_ps = [sem(n) for n in (
            "h2t_hi", "t_lvl", "bias_home", "gi_ok", "less_ok", "h2p_ok", "beta_ok", "vtok_ps")]
        cur_ok, oc_ok, part_ps, part_ok = [sem(n) for n in (
            "cur_ok", "oc_ok", "part_ps", "part_ok")]

        def chain(eng, s, start=0):
            n = [0]

            def link(ins):
                n[0] += 1
                ins.then_inc(s, 1)
                eng.wait_ge(s, start + n[0])
            link.n = n
            return link

        def unit_src(e, u):
            if u < NGU:
                return w_gate_up[0, bass.ds(e, 1), u * P:(u + 1) * P, :].rearrange("a p c -> (a p) c")
            c = 2 * (u - NGU)
            return w_down[0, bass.ds(e, 1), c * P:(c + 2) * P, :].rearrange("a (c p) n -> p (a c) n", c=2)

        def unit_dst(slot, u):
            v = ring[:, slot * UNIT:(slot + 1) * UNIT]
            return v if u < NGU else v.rearrange("p (c n) -> p c n", c=2)

        def slot_of(j, u):
            return (NU * j + u) % RING, (NU * j + u) // RING

        block = ctx.enter_context(nc.Block())
        y_pairs = pair_rows.rearrange("(t k q) c -> t (k q c)", k=TOPK, q=Q)
        n_conv = CONV - 1
        DELTA_LINKS = 10
        LEVELS = 5

        def nrm_bank(n):
            return n + 1 if n < 6 else n - 4

        def pool_bank(g):
            return (4, 6, 7, 5)[g]

        def t_bank(a):
            return (7, 1)[a]

        def r_bank(a):
            return (0, 2)[a]

        @block.sync
        def _(sp):
            def param(row, n, src):
                sp.dma_start(prow[row:row + n, :], src).then_inc(par_in, 16)

            for b in range(TB):
                sp.dma_start(xs[:, b, :], x[0, b * P:(b + 1) * P, :]).then_inc(x_in[b], 16)
            param(NANW, KD, attn_norm_w.rearrange("l (k p) -> (l k) p", p=P))
            for j in range(CONV):
                param(NCV + NQKV * j, NQKV, conv_w[0, j:j + 1, :].rearrange("l (k p) -> (l k) p", p=P))
            param(NDN, 1, dn_norm_w)
            param(NPS, 4, pool_scale.rearrange("l (k p) -> (l k) p", p=P))

            w_in_v = w_in[0].rearrange("(k p) c -> p k c", p=P)

            def load_piece(buf, c0):
                sp.dma_start(win[:, buf], w_in_v[:, :, bass.ds(c0, 256)]).then_inc(win_in[buf], 16)

            load_piece(0, 0)
            load_piece(1, 256)
            sp.dma_start(wba[:, :, :], w_in_v[:, :, C_BA:C_BA + SLOTS]).then_inc(wba_in, 16)
            sp.dma_start(bcr[:, 0:H], dt_bias.to_broadcast([P, H])).then_inc(bc_in, 16)
            sp.dma_start(bcr[:, H:2 * H], a_log.to_broadcast([P, H])).then_inc(bc_in, 16)
            sp.dma_start(bcr[:, 2 * H:], b_router.to_broadcast([P, E])).then_inc(bc_in, 16)
            sp.dma_start(poolw[:, :, :], pool_w[0].rearrange("g c d -> c g d")).then_inc(pw_in, 16)
            sp.dma_start(wrt[:, :, :], w_router[0].rearrange("(k p) e -> p k e", p=P)).then_inc(wrt_in, 16)
            for i in range(3):
                sp.dma_start(braw[32 * i:32 * i + 32, 0:2 * D], b_gate_up[0]).then_inc(braw_in, 16)
                sp.dma_start(braw[32 * i:32 * i + 32, 2 * D:], b_down[0]).then_inc(braw_in, 16)
            with sp.Fori(0, 2) as i:
                for buf in range(2):
                    sp.wait_ge(proj_ps, 4 * i + 2 * (buf + 1))
                    load_piece(buf, 512 * (i + 1) + 256 * buf)
            for n, c0 in ((6, C_Z), (7, C_Z + 256), (8, C_P), (9, C_P + 256)):
                sp.wait_ge(proj_ps, 2 * (n - 1))
                load_piece(n % 2, c0)
            sp.wait_ge(bias_ok, 1)
            sp.dma_start(wout[:, :, :], w_out[0].rearrange("(k p) c -> p k c", p=P)).then_inc(wout_in, 16)

            def load_unit(e, u, slot):
                sp.dma_start(unit_dst(slot, u), unit_src(e, u)).then_inc(slot_in[slot], 16)

            load_unit(0, 0, 0)
            sp.wait_ge(cat_ok, TB)
            for n in range(2, 7):
                load_unit(n // NU, n % NU, n)
            sp.wait_ge(pool_mix, 4)
            sp.dma_start(fnw, ffn_norm_w.to_broadcast([P, D])).then_inc(fnw_in, 16)
            sp.wait_ge(h2_ok, TB)
            sp.dma_start(x1_rows.rearrange("(b p) d -> p b d", p=P), xs).then_inc(stored, 16)
            for n in (7, 10, 11, 12, 13):
                load_unit(n // NU, n % NU, n)
            sp.dma_start(fnw, final_norm_w.rearrange("(a n) -> a n", a=1).to_broadcast([P, D])).then_inc(fnw_in, 16)
            sp.wait_ge(bias_home, 1)
            load_unit(0, 1, 1)
            sp.wait_ge(part_ps, 2)
            for n in (14, 15):
                load_unit(n // NU, n % NU, n)
            sp.wait_ge(h2p_ok, 3 * TB)
            for n in (8, 9):
                load_unit(n // NU, n % NU, n)
            sp.wait_ge(stored, 16)
            for n in range(X0, RING):
                load_unit(n // NU, n % NU, n)
            sp.wait_ge(tab_ok, 1)

            def refill(e, j, turn):
                used = sp.value_load(tab[0:1, bass.ds(e + USED, 1)], min_val=0, max_val=MAXB * NU)
                following = {}
                for ne in (1, 2):
                    if not isinstance(e, int) or e + ne < E:
                        following[ne] = sp.value_load(tab[0:1, bass.ds(e + (VISIT + ne), 1)], min_val=0, max_val=E - 1)
                for u in range(NU):
                    nu, ne = (u + RING) % NU, (u + RING) // NU
                    if isinstance(e, int) and e + ne >= E:
                        continue
                    n = NU * j + u + RING - AHEAD
                    sp.wait_ge(w_used, used + (u + 1))
                    sp.wait_ge(slot_in[n % RING], (turn + (n // RING + 1)) * 16)
                    load_unit(following[ne], nu, slot_of(j, u)[0])

            with sp.Fori(0, E // UNROLL) as grp:
                for j in range(UNROLL):
                    refill(UNROLL * grp + j, j, TURNS * grp)
            for e in range(E // UNROLL * UNROLL, E - 1):
                refill(e, e % UNROLL, TURNS * (e // UNROLL))
            pairs = sp.value_load(tab[0:1, PAIRS:PAIRS + 1], min_val=E // 2, max_val=MAXB // 2)
            sp.wait_ge(w_used, pairs * (2 * NU))
            for b in range(TB):
                sp.dma_start(xs[:, b, :], x1_rows[b * P:(b + 1) * P, :]).then_inc(y_in[b], 16)
            for s in scat:
                sp.wait_ge(s, pairs * 16)
            for b in range(TB):
                sp.dma_start(ring[:, b * TOPK * D:(b + 1) * TOPK * D], y_pairs[b * P:(b + 1) * P, :]).then_inc(y_in[b], 16)
            for b in range(TB):
                sp.wait_ge(fin_o, b + 1)
                sp.dma_start(out[0, b * P:(b + 1) * P, :], ring[:, b * TOPK * D:b * TOPK * D + D]).then_inc(stored, 16)
            sp.wait_ge(stored, 16 * (TB + 1))

        @block.gpsimd
        def _(pool):
            G = nc.gpsimd
            link = chain(pool, pool_step)
            imprecise = dict(allow_small_or_imprecise_dtypes=True)
            G.iota(iotas[:, 0, :], pattern=[[1, P]], base=0, channel_multiplier=0).then_inc(iota_ok, 1)
            G.iota(iotas[:, 1, :], pattern=[[0, P]], base=0, channel_multiplier=1).then_inc(iota_ok, 1)
            G.iota(iotaf[:, :], pattern=[[1, T + SLOTS]], base=0, channel_multiplier=0, **imprecise).then_inc(iota_ok, 1)
            G.iota(rowbase[:, :], pattern=[[TOPK * P, TB]], base=-int(OOB), channel_multiplier=TOPK,
                   **imprecise).then_inc(iota_ok, 1)
            G.iota(pidx[:, :], pattern=[[0, 1]], base=0, channel_multiplier=1, **imprecise).then_inc(iota_ok, 1)
            G.memset(epsc[:, 0:1], RMS_EPS).then_inc(const_ok, 1)
            G.memset(epsc[:, 1:2], L2_EPS).then_inc(const_ok, 1)
            link(G.memset(ident, 0.0))
            link(G.memset(cst[:, 1, :], 1.0))
            link(G.memset(cst[:, 2, :], 0.0))
            link(G.memset(cst[:, 6:8, :], 0.0))
            for c in range(2):
                r = slice(CH * c, CH * (c + 1))
                link(G.memset(cst[r, 2, r], 1.0))
                link(G.memset(cst[r, 6 + c, :], 1.0))
            G.affine_select(out=ident, in_=ident, compare_op=ALU.not_equal, fill=1.0, base=0,
                            pattern=[[-1, P]], channel_multiplier=1).then_inc(const_ok, 1)
            for dst, src, cmp in ((lowS, ones, ALU.is_gt), (causal, same, ALU.is_ge), (strict, same, ALU.is_gt)):
                G.affine_select(out=dst, in_=src, compare_op=cmp, fill=0.0, base=0,
                                pattern=[[1, P]], channel_multiplier=-1).then_inc(const_ok, 1)
            for g in range(3):
                link(G.memset(E3[32 * g:32 * g + 32, :], 0.0))
                link(G.affine_select(out=E3[32 * g:32 * g + 32, :], in_=E3[32 * g:32 * g + 32, :],
                                     compare_op=ALU.not_equal, fill=1.0, base=0, pattern=[[-1, SLOTS]],
                                     channel_multiplier=1))
            pool.wait_ge(const_ok, 6)
            link(G.tensor_copy(cstb[:, 0, :], lowS))
            link(G.tensor_copy(cstb[:, 1, :], ones))
            for q in range(Q):
                r = slice(SLOTS * q, SLOTS * (q + 1))
                link(G.memset(S4[r, :], 0.0))
                ins = G.affine_select(out=S4[r, :], in_=S4[r, :], compare_op=ALU.not_equal, fill=1.0, base=0,
                                      pattern=[[-1, SLOTS]], channel_multiplier=1)
                if q < Q - 1:
                    link(ins)
                else:
                    ins.then_inc(const_ok, 1)
            for q in range(Q):
                link(G.memset(qcol[SLOTS * q:SLOTS * (q + 1), :], float(q)))
            link(G.memset(pool_t[:, :, 0:PAD], 0.0))
            link(G.memset(pbuf[:, :, 0:PAD], 0.0))
            link(G.memset(ST[:, :, :, :], 0.0))
            pool.wait_ge(braw_in, 6 * 16)
            link(G.tensor_copy(bias_tmp[:, :], braw))
            for lo in (32, 64):
                for g in range(lo, 96, 32):
                    r = slice(g, g + 32)
                    link(G.tensor_tensor(brem[r], braw[r] if lo == 32 else brem[r], bias_tmp[r, :], ALU.subtract))
                    last = G.tensor_copy(bias_tmp[r, :], brem[r])
                    if lo == 64:
                        last.then_inc(bias_ok, 1)
                    else:
                        link(last)
            pool.wait_ge(bias_ok, 1)
            pool.wait_ge(qk_ok, 2 * H)
            G.memset(WS[:, 0:5], 0.0).then_inc(zero_ok, 1)

            def spread(tb):
                def col(v):
                    return bc(v[:, bass.ds(tb, 1), :].rearrange("p a h -> p (a h)"), P, 2)
                G.tensor_tensor(GUM, bc(causal, H, 1), col(gt[:, 8]), ALU.mult).then_inc(grow_ok, 1)
                G.tensor_tensor(BI, bc(ident, H, 1), col(gt[:, 9]), ALU.mult).then_inc(grow_ok, 1)

            pool.wait_ge(beta_ok, 1)
            spread(0)
            pool.wait_ge(lvl_ok, 1)
            for g, w in enumerate(WINDOWS):
                pool.wait_ge(silu_ok, NQKV + H + g + 1)
                src, s, i = pbuf[:, g], 1, 0
                while s < w:
                    dst = pool_t[:, i % 2]
                    link(G.tensor_tensor(dst[:, PAD:], src[:, PAD:], src[:, PAD - s:PAD + T - s], ALU.add))
                    src, s, i = dst, 2 * s, i + 1
                link(G.tensor_scalar(catT[:, H + g, :], src[:, PAD:], 1.0 / w, None, ALU.mult))
                link(G.tensor_tensor(catT[:, H + g, :], catT[:, H + g, :], pbuf[:, g, PAD:], ALU.subtract))
                link(G.tensor_tensor(src[:, PAD:PAD + w], src[:, PAD:PAD + w], icnt[:, 0:w], ALU.mult))
                G.tensor_tensor(catT[:, H + g, 0:w], src[:, PAD:PAD + w], pbuf[:, g, PAD:PAD + w],
                                ALU.subtract).then_inc(pool_mix, 1)
                pool.wait_ge(pool_mix, g + 1)
            with pool.Fori(0, TB - 1) as tb:
                pool.wait_ge(brow_ps, tb + 1)
                spread(tb + 1)
            for b in range(TB):
                pool.wait_ge(h2t_ps, 2 * b + 2)
                pool.wait_ge(h2p_ok, b + 1)
                G.tensor_tensor(h2[:, b, :], h2[:, b, :], h2p[0][:, b, :], ALU.subtract).then_inc(less_ok, 1)
            for b in range(TB):
                pool.wait_ge(h2p_ok, TB + b + 1)
                G.tensor_tensor(h2[:, b, :], h2[:, b, :], h2p[1][:, b, :], ALU.subtract).then_inc(less_ok, 1)
            def over_choices(weights, out):
                link(G.tensor_tensor(ohw[:, :, :, :], oh[:, :, :, :], weights, ALU.mult))
                for a in range(2):
                    link(G.tensor_tensor(ohw[:, :, :, a], ohw[:, :, :, a], ohw[:, :, :, a + 2], ALU.add))
                link(G.tensor_tensor(out, ohw[:, :, :, 0], ohw[:, :, :, 1], ALU.add))

            pool.wait_ge(mask_ok, 1)
            over_choices(bc(bc(iotaf[:, 0:TOPK], E, 1), TB, 1), chn)
            link(G.tensor_tensor(gi[:, :, :, 1], maskb[:, :, :], bc(rowbase[:, :], E, 2), ALU.mult))
            link(G.tensor_tensor(gi[:, :, :, 1], gi[:, :, :, 1], chn, ALU.add))
            pool.wait_ge(top_ok, 2)
            over_choices(bc(tk[:, 3], E, 2), gi[:, :, :, 0])
            for n in range(3):
                ins = G.tensor_copy(gip[:, :, :, 2 * n:2 * n + 2], gi[:, :, :, :])
                if n < 2:
                    link(ins)
                    link(G.tensor_tensor(gi[:, :, :, :], gi[:, :, :, :], gip[:, :, :, 2 * n:2 * n + 2], ALU.subtract))
                else:
                    ins.then_inc(gi_ok, 1)
            pool.wait_ge(tab_ok, 1)
            pairs = pool.value_load(tab[0:1, PAIRS:PAIRS + 1], min_val=E // 2, max_val=MAXB // 2)
            with pool.Fori(0, pairs) as i:
                for p in range(2):
                    pool.wait_ge(ys_ok, 2 * i + (p + 1))
                    limit = pool.snap(i + (T * TOPK * Q + p))
                    G.indirect_dma_start(
                        out=pair_rows, out_offset=bass.IndirectOffsetOnAxis(ap=rowi[:, p:p + 1], axis=0),
                        in_=ys[p], in_offset=None, bounds_check=limit,
                        oob_is_err=False).then_inc(scat[p], 16)

        @block.scalar
        def _(act):
            A = nc.scalar.activation
            link = chain(act, act_step)

            def row(v):
                return v.rearrange("p a t -> p (a t)")

            for b in range(TB):
                act.wait_ge(x_in[b], 16)
                link(A(junk, xs[:, b, :], ACT.Square, accum_out=sm[:, b:b + 1]))
            act.wait_ge(const_ok, 2)
            A(sm[:, 4:8], sm[:, 0:4], ACT.Sqrt, scale=1.0 / D, bias=epsc[:, 0:1]).then_inc(std_ok, 1)
            act.wait_ge(pcol_ok, 1)
            for k in range(0, KD, 2):
                act.wait_ge(xt_ps, k + 1)
                A(hT[:, k, :], bank(k), ACT.Copy, scale=pcol[:, NANW + k:NANW + k + 1]).then_inc(ht_even, 1)
            with act.Fori(0, 3) as i:
                for r in range(4):
                    n = 4 * i + r
                    act.wait_ge(proj_ps, n + 1)
                    A(cbuf[r % 2], bank(r % 2), ACT.Copy,
                      scale=pcol[:, bass.ds(n + (NCV + n_conv * NQKV), 1)]).then_inc(tap_ok, 1)
                    act.wait_ge(conv_ok, n + 1)
                    A(row(qkv[:, bass.ds(n, 1), :]), cbuf[r % 2], ACT.Silu).then_inc(silu_ok, 1)
            act.wait_ge(gin_ok, 1)
            A(gt[:, 2], gt[:, 1], ACT.Exp).then_inc(gexp_in, 1)
            A(gt[:, 3], gt[:, 10], ACT.Exp, scale=-1.0).then_inc(gexp_in, 1)
            act.wait_ge(bc_in, 48)
            A(gt[:, 4, 0, :], bcr[:, H:2 * H], ACT.Exp).then_inc(gexp_in, 1)
            act.wait_ge(gln_in, 1)
            A(gt[:, 6], gt[:, 5], ACT.Ln).then_inc(gexp_in, 1)
            for n in range(2 * H):
                act.wait_ge(nrm_ps, n + 1)
                A(wsf[:, n], bank(nrm_bank(n)), ACT.Sqrt, bias=epsc[:, 1:2]).then_inc(nroot_ok, 1)
            for n in range(NQKV, NQKV + 2 * H):
                act.wait_ge(proj_ps, n + 1)
                if n < NQKV + H:
                    A(zs[:, n - NQKV, :], bank(n % 2), ACT.Silu).then_inc(silu_ok, 1)
                else:
                    A(pbuf[:, n - NQKV - H, PAD:], bank(n % 2), ACT.Copy).then_inc(silu_ok, 1)
                if n == NQKV + H - 1:
                    act.wait_ge(gcs_ok, 1)
                    A(gex[:, :, :, :], gcs[:, :, :, :], ACT.Exp).then_inc(gex_ok, 1)

            def load_kv(t):
                if not isinstance(t, int):
                    act.wait_ge(vtok_ps, t)
                tok = bass.ds(t * P, P)
                A(KTS, qkv[:, H:2 * H, tok], ACT.Copy).then_inc(kv_ok, 1)
                A(VTS, qkv[:, 2 * H:3 * H, tok], ACT.Copy).then_inc(kv_ok, 1)

            def decay(t):
                act.wait_ge(grow_ps, t + 1)
                A(EGI, bank(0, H), ACT.Exp).then_inc(dexp_ok, 1)
                act.wait_ge(dx_ok, t + 1)
                A(DX, DX, ACT.Exp).then_inc(dexp_ok, 1)

            def first_inverse(t):
                act.wait_ge(t2_ps, t + 1)
                A(TM, bank(1, H), ACT.Copy).then_inc(t_ok, 1)

            def delta(t, more):
                act.wait_ge(prep_ok, t + 1)
                act.wait_ge(o_ps, t)
                A(QKT, QKN, ACT.Copy).then_inc(cur_ok, 1)
                A(KDZ0[0:CH], KDN[0:CH], ACT.Copy).then_inc(cur_ok, 1)
                A(KDZ1[CH:], KDN[CH:], ACT.Copy).then_inc(cur_ok, 1)
                A(QD0[:, :, 0:CH], QDN[:, :, 0:CH], ACT.Copy).then_inc(cur_ok, 1)
                A(QD1[:, :, CH:], QDN[:, :, CH:], ACT.Copy).then_inc(cur_ok, 1)
                if more:
                    load_kv(t + 1)
                act.wait_ge(uw_ps, t * 2 + 1)
                A(UU, bank(1, H), ACT.Copy).then_inc(uw_ok, 1)
                act.wait_ge(uw_ps, t * 2 + 2)
                A(WT, bank(2, H), ACT.Copy).then_inc(uw_ok, 1)
                if more:
                    decay(t + 1)
                act.wait_ge(o_ps, t + 1)
                A(O4[:, bass.ds(t, 1)].rearrange("p a h c -> p (a h) c"), bank(5, H), ACT.Copy).then_inc(oc_ok, 1)
                if more:
                    first_inverse(t + 1)

            act.wait_ge(qk_ok, 2 * H)
            load_kv(0)
            decay(0)
            first_inverse(0)
            with act.Fori(0, TB - 1) as tb:
                delta(tb, True)
            delta(TB - 1, False)
            act.wait_ge(oc_ok, TB)
            for b in range(TB):
                A(OSQ[b], O4[:, b], ACT.Square).then_inc(osq_ok, 1)
            act.wait_ge(oms_ok, TB)
            A(so[:, 1], so[:, 0], ACT.Sqrt, scale=1.0 / P, bias=epsc[:, 0:1]).then_inc(ort_ok, 1)
            for g in range(4):
                act.wait_ge(pool_ps, g + 1)
                A(catT[:, H + g, :], bank(pool_bank(g)), ACT.Copy, scale=pcol[:, NPS + g:NPS + g + 1]).then_inc(pooled_ok, 1)
            for b in range(TB):
                act.wait_ge(x1_ok, 2 * b + 2)
                link(A(junk2, xs[:, b, :], ACT.Square, accum_out=sm[:, 20 + b:21 + b]))
                A(sm[:, 24 + b:25 + b], sm[:, 20 + b:21 + b], ACT.Sqrt, scale=1.0 / D, bias=epsc[:, 0:1]).then_inc(s2_ok, 1)
            for b in range(TB):
                act.wait_ge(h2_ok, b + 1)
                A(h2p[0][:, b, :], h2[:, b, :], ACT.Copy).then_inc(h2p_ok, 1)
                act.wait_ge(h2t_ps, 2 * b + 2)
                A(h2T[:, 4:8, b * P:(b + 1) * P], bank(2 * (b % 2) + 1, 4), ACT.Copy).then_inc(h2t_hi, 1)
            A(bias3[:, :], bias_tmp, ACT.Copy).then_inc(bias_home, 1)
            for b in range(TB):
                act.wait_ge(less_ok, b + 1)
                A(h2p[1][:, b, :], h2[:, b, :], ACT.Copy).then_inc(h2p_ok, 1)
            act.wait_ge(top_ok, 1)
            A(tk[:, 1], tk[:, 2], ACT.Exp).then_inc(texp_ok, 1)
            for b in range(TB):
                act.wait_ge(less_ok, TB + b + 1)
                A(h2p[2][:, b, :], h2[:, b, :], ACT.Copy).then_inc(h2p_ok, 1)

            act.wait_ge(gat_ps, 1)
            A(xg[:, :], ps[:, 2, 0:QD], ACT.Copy).then_inc(xg_ok, 1)
            act.wait_ge(xgt_ps, 1)
            A(xgT[:, :, :], bank(3, 4)[:, 0:2, :], ACT.Copy).then_inc(xgt_ok, 1)
            act.wait_ge(tab_ok, 1)
            pairs = act.value_load(tab[0:1, PAIRS:PAIRS + 1], min_val=E // 2, max_val=MAXB // 2)

            def activate(g, i, p):
                act.wait_ge(gc_ok, g + 1)
                act.wait_ge(act_ok, g)
                A(sg[:, :], gc[:, :], ACT.Sigmoid, scale=ALPHA).then_inc(sg_ok, 1)
                act.wait_ge(gat_ps, g + 2)
                act.wait_ge(xgt_ps, g + 1)
                A(xg[:, :], ps[:, 2, 0:QD], ACT.Copy).then_inc(xg_ok, 1)
                act.wait_ge(at_ps, g + 1)
                act.wait_ge(w_used, g * NU)
                A(actT[:, :, :], bank(4, 4)[:, 0:2, :], ACT.Copy).then_inc(actt_ok, 1)
                act.wait_ge(xgt_ps, g + 2)
                act.wait_ge(w_used, g * NU + NGU)
                A(xgT[:, :, :], bank(3, 4)[:, 0:2, :], ACT.Copy).then_inc(xgt_ok, 1)
                act.wait_ge(w_used, g * NU + NU)
                act.wait_ge(slot_ok, g + 1)
                act.wait_ge(scat[p], i * 16)
                A(ys[p], ps[:, 1, 0:QD], ACT.Copy, scale=wslot[:, p, 0:1]).then_inc(ys_ok, 1)

            with act.Fori(0, pairs) as i:
                for p in range(2):
                    activate(2 * i + p, i, p)
            for b in range(TB):
                act.wait_ge(fin_sum, b + 1)
                base = b * TOPK * D + D
                A(ring[:, base:base + D], xs[:, b, :], ACT.Square, accum_out=sm[:, 28 + b:29 + b]).then_inc(fin_sq, 1)
                act.wait_ge(fin_sq, b + 1)
                A(sm[:, 32 + b:33 + b], sm[:, 28 + b:29 + b], ACT.Sqrt, scale=1.0 / D, bias=epsc[:, 0:1]).then_inc(fin_rt, 1)

        @block.vector
        def _(dve):
            V = nc.vector
            link = chain(dve, dve_step)

            def step(ins, s, count):
                ins.then_inc(s, 1)
                dve.wait_ge(s, count)

            dve.wait_ge(pcol_ps, 1)
            step(V.tensor_copy(pcol[:, :], ps[:, 7, 0:61]), pcol_ok, 1)
            dve.wait_ge(std_ok, 1)
            step(V.reciprocal(sm[:, 8:12], sm[:, 4:8]), rstd_ok, 1)
            for b in range(TB):
                V.tensor_scalar(xn[:, b, :], xs[:, b, :], sm[:, 8 + b:9 + b], None, ALU.mult).then_inc(xn_ok, 1)
            for k in range(1, KD, 2):
                dve.wait_ge(xt_ps, k + 1)
                V.tensor_scalar(hT[:, k, :], bank(k), pcol[:, NANW + k:NANW + k + 1], None, ALU.mult).then_inc(ht_odd, 1)
            dve.wait_ge(iota_ok, 5)
            link(V.tensor_tensor(iotas[:, 2, :], iotas[:, 0, :], iotas[:, 1, :], ALU.bitwise_xor))
            for s in range(6):
                link(V.tensor_scalar(iotas[:, 0, :], iotas[:, 2, :], s, None, ALU.logical_shift_right))
                link(V.tensor_scalar(lvl[:, s, :], iotas[:, 0, :], 1, None, ALU.is_equal))
            dve.wait_ge(const_ok, 6)
            link(V.tensor_tensor(lvl[:, 0, :], lvl[:, 0, :], strict, ALU.mult))
            for s in range(1, 6):
                link(V.tensor_scalar(nbf[:, :, :].rearrange("p a b -> p (a b)"), causal, -1.0, 1.0, ALU.mult, ALU.add))
                link(V.tensor_tensor(lvl[:, s, :], lvl[:, s, :], nbf[:, :, :].rearrange("p a b -> p (a b)"), ALU.mult))
            link(V.tensor_scalar(icnt[:, :], iotaf[:, 0:PAD], 1.0, None, ALU.add))
            V.reciprocal(icnt[:, :], icnt[:, :]).then_inc(lvl_ok, 1)

            def conv(n, b, base):
                t = cbuf[b]
                dve.wait_ge(tap_ok, n + 1)
                for m in range(1, CONV):
                    ins = V.scalar_tensor_tensor(
                        out=t[:, m:], in0=bank(b)[:, 0:T - m], scalar=pcol[:, bass.ds(n + (NCV + (n_conv - m) * NQKV), 1)],
                        in1=t[:, m:], op0=ALU.mult, op1=ALU.add)
                    if m < n_conv:
                        step(ins, conv_step, base + m)
                    else:
                        ins.then_inc(conv_ok, 1)

            dve.wait_ge(part_ps, 1)
            V.tensor_copy(ba_part, bank(6)).then_inc(part_ok, 1)
            with dve.Fori(0, 3) as i:
                for r in range(4):
                    conv(4 * i + r, r % 2, (4 * i + r) * (n_conv - 1))
            dve.wait_ge(ba_ps, 1)
            dve.wait_ge(bc_in, 48)
            ba = ps[:, 7, 0:TB * 2 * H].rearrange("p (b c) -> p b c", b=TB)
            link(V.tensor_copy(gt[:, 10], ba[:, :, 0:H]))
            link(V.tensor_tensor(gt[:, 0], ba[:, :, H:], bc(bcr[:, 0:H], TB, 1), ALU.add))
            link(V.tensor_scalar(gt[:, 1], gt[:, 0], -1.0, None, ALU.mult))
            step(V.tensor_tensor(gt[:, 1], gt[:, 1], gt[:, 0], ALU.min), gin_ok, 1)
            for n in range(2 * H):
                dve.wait_ge(silu_ok, n + 1)
                V.tensor_tensor(wsf[:, n], qkv[:, n, :], qkv[:, n, :], ALU.mult).then_inc(sq_ok, 1)
            dve.wait_ge(gexp_in, 3)
            step(V.tensor_scalar(gt[:, 5], gt[:, 2], 1.0, None, ALU.add), gln_in, 1)
            link(V.tensor_scalar(gt[:, 7], gt[:, 5], -1.0, None, ALU.add))
            link(V.tensor_tensor(gt[:, 7], gt[:, 2], gt[:, 7], ALU.subtract))
            link(V.reciprocal(gt[:, 11], gt[:, 5]))
            link(V.tensor_tensor(gt[:, 7], gt[:, 7], gt[:, 11], ALU.mult))
            link(V.tensor_scalar(gt[:, 0], gt[:, 0], 0.0, None, ALU.max))
            dve.wait_ge(gexp_in, 4)
            link(V.tensor_tensor(gt[:, 7], gt[:, 7], gt[:, 6], ALU.add))
            link(V.tensor_tensor(gt[:, 7], gt[:, 7], gt[:, 0], ALU.add))
            step(V.scalar_tensor_tensor(out=gt[:, 8], in0=gt[:, 7], scalar=-1.0, in1=bc(gt[:, 4, 0, :], TB, 1),
                                        op0=ALU.mult, op1=ALU.mult), g_ok, 1)
            link(V.tensor_scalar(gt[:, 9], gt[:, 3], 1.0, None, ALU.add))
            step(V.reciprocal(gt[:, 9], gt[:, 9]), beta_ok, 1)

            def unit(n):
                dve.wait_ge(nroot_ok, n + 1)
                link(V.reciprocal(wsf[:, n], wsf[:, n]))
                V.scalar_tensor_tensor(out=qkv[:, n, :], in0=qkv[:, n, :], scalar=float(P) ** -0.5 if n < H else 1.0,
                                       in1=wsf[:, n], op0=ALU.mult, op1=ALU.mult).then_inc(qk_ok, 1)

            for n in range(4):
                unit(n)
            dve.wait_ge(gcum_ps, 1)
            cum = ps[:, 7, 64:64 + 4 * TB * H].rearrange("p (n b h) -> p n b h", n=4, b=TB)
            link(V.tensor_copy(gcs[:, :, :, :], cum))
            step(V.tensor_tensor(gcs[:, 1], gcs[:, 1], gcs[:, 0], ALU.subtract), gcs_ok, 1)
            for n in range(4, 2 * H):
                unit(n)
            dve.wait_ge(gex_ok, 1)
            link(V.tensor_tensor(gt[:, 11], gex[:, 0], gt[:, 9], ALU.mult))
            dve.wait_ge(zero_ok, 1)

            def prepare(t):
                lk = chain(dve, delta_step, t * DELTA_LINKS)

                def col(v):
                    return bc(v[:, bass.ds(t, 1), :].rearrange("p a h -> p (a h)"), P, 2)

                def differences():
                    dve.wait_ge(dexp_ok, 2 * t + 1)
                    lk(V.tensor_tensor(DX, bank(0, H), col(gcs[:, 0]), ALU.subtract))
                    V.tensor_scalar(DX, DX, 0.0, None, ALU.min).then_inc(dx_ok, 1)

                def queries():
                    dve.wait_ge(dexp_ok, 2 * t + 2)
                    dve.wait_ge(kk_ps, t + 1)
                    if not isinstance(t, int):
                        dve.wait_ge(cur_ok, t * 5)
                    lk(V.tensor_tensor(DX, DX, bc(causal, H, 1), ALU.mult))
                    lk(V.tensor_tensor(QKN, bank(3, H), DX, ALU.mult))

                def matrix():
                    lk(V.tensor_tensor(AT, bank(2, H), DX, ALU.mult))
                    lk(V.tensor_tensor(AT, AT, bank(1, H), ALU.mult))
                    lk(V.tensor_tensor(AT, AT, bc(strict, H, 1), ALU.mult))
                    lk(V.tensor_tensor(YM, AT, bc(lvl[:, 0, :], H, 1), ALU.mult))
                    V.tensor_tensor(TR, bc(ident, H, 1), YM, ALU.subtract).then_inc(r2_ok, 1)

                def operands():
                    lk(V.tensor_tensor(QDN, qkv[:, 0:H, bass.ds(t * P, P)], EGI, ALU.mult))
                    dve.wait_ge(ktok_ps, t + 1)
                    lk(V.tensor_tensor(KBG, bank(4, H), col(gt[:, 11]), ALU.mult))
                    lk(V.tensor_tensor(KDN, bank(4, H), col(gex[:, 1]), ALU.mult))
                    dve.wait_ge(vtok_ps, t + 1)
                    V.tensor_tensor(VB, bank(0, H), col(gt[:, 9]), ALU.mult).then_inc(prep_ok, 1)
                    assert lk.n[0] == DELTA_LINKS
                return differences, queries, matrix, operands

            def invert(t):
                dve.wait_ge(r2_ok, t + 1)
                dve.wait_ge(t_ok, t + 1)
                for s in range(LEVELS):
                    for a in range(2):
                        dve.wait_ge(y_ps, t * 2 * LEVELS + (2 * s + a + 1))
                        V.tensor_tensor(YM[:, 2 * a:2 * a + 2], bank(6 - 3 * a, H)[:, 0:2], bc(lvl[:, s + 1, :], 2, 1),
                                        ALU.mult).then_inc(ym_ok, 1)
                    for a in range(2):
                        dve.wait_ge(tr_ps, t * 2 * LEVELS + (2 * s + a + 1))
                        hp = slice(2 * a, 2 * a + 2)
                        if s < LEVELS - 1:
                            V.tensor_tensor(TM[:, hp], TM[:, hp], bank(t_bank(a), H)[:, 0:2], ALU.subtract).then_inc(t_lvl, 1)
                        V.tensor_tensor(TR[:, hp], TR[:, hp], bank(r_bank(a), H)[:, 0:2], ALU.subtract).then_inc(r_ok, 1)
                    if s < LEVELS - 1:
                        dve.wait_ge(t_lvl, t * 2 * (LEVELS - 1) + (2 * s + 2))
                    dve.wait_ge(r_ok, t * 2 * LEVELS + (2 * s + 2))

            def new_values(t, c):
                r = slice(CH * c, CH * (c + 1))
                dve.wait_ge(uw_ok, 2 * t + 2)
                dve.wait_ge(ws_ps, 2 * t + (c + 1))
                V.tensor_tensor(VN[r], UU[r], bank(6, H)[r], ALU.subtract).then_inc(vn_ok, 1)

            def new_state(t, c):
                dve.wait_ge(su_ps, 2 * t + (c + 1))
                if c:
                    dve.wait_ge(o_ps, t + 1)
                for h in range(H):
                    V.scalar_tensor_tensor(
                        out=ST[:, 1 - c, h, :], in0=ST[:, c, h, :],
                        scalar=gex[:, 2 + c, bass.ds(t, 1), h:h + 1].rearrange("p a b -> p (a b)"),
                        in1=bank(7, H)[:, h, :], op0=ALU.mult, op1=ALU.add).then_inc(st_ok, 1)
                dve.wait_ge(st_ok, (2 * t + (c + 1)) * H)

            for part in prepare(0):
                part()
            with dve.Fori(0, TB - 1) as tb:
                differences, queries, matrix, operands = prepare(tb + 1)
                invert(tb)
                differences()
                new_values(tb, 0)
                queries()
                new_state(tb, 0)
                new_values(tb, 1)
                matrix()
                new_state(tb, 1)
                operands()
            invert(TB - 1)
            for c in range(2):
                new_values(TB - 1, c)
                if c == 0:
                    new_state(TB - 1, c)
            for b in range(TB):
                dve.wait_ge(osq_ok, b + 1)
                V.tensor_reduce(so[:, 0, b], OSQ[b], AX.X, ALU.add).then_inc(oms_ok, 1)
            dve.wait_ge(ort_ok, 1)
            link(V.reciprocal(so[:, 2], so[:, 1]))
            for b in range(TB):
                V.tensor_tensor(O4[:, b], O4[:, b], bc(so[:, 2, b], P, 2), ALU.mult).then_inc(on_ok, 1)
            for b in range(TB):
                dve.wait_ge(ot_ps, b + 1)
                V.scalar_tensor_tensor(out=catT[:, 0:H, b * P:(b + 1) * P], in0=bank(b, H), scalar=pcol[:, NDN:NDN + 1],
                                       in1=zs[:, :, b * P:(b + 1) * P], op0=ALU.mult, op1=ALU.mult).then_inc(cat_ok, 1)
            dve.wait_ge(fnw_in, 16)
            for b in range(TB):
                for half in range(2):
                    n = 2 * b + half
                    dve.wait_ge(op_ps, n + 1)
                    v = xs[:, b, 512 * half:512 * (half + 1)]
                    V.tensor_tensor(v, v, bank(4 + n % 4), ALU.add).then_inc(x1_ok, 1)
                dve.wait_ge(x1_ok, 2 * b + 2)
                dve.wait_ge(s2_ok, b + 1)
                link(V.reciprocal(sm[:, 40 + b:41 + b], sm[:, 24 + b:25 + b]))
                V.scalar_tensor_tensor(out=h2[:, b, :], in0=xs[:, b, :], scalar=sm[:, 40 + b:41 + b], in1=fnw,
                                       op0=ALU.mult, op1=ALU.mult).then_inc(h2_ok, 1)
            for n in range(0, 2 * TB, 2):
                dve.wait_ge(h2t_ps, n + 1)
                V.tensor_copy(h2T[:, 0:4, (n // 2) * P:(n // 2 + 1) * P], bank(2 * (n // 2 % 2), 4)).then_inc(h2t_lo, 1)
            dve.wait_ge(part_ps, 2)
            V.tensor_copy(lg_part, bank(4)).then_inc(part_ok, 1)
            dve.wait_ge(lg_ps, 1)
            link(V.tensor_tensor(lgs[:, :, :], ps[:, 0, 0:TB * E].rearrange("p (b e) -> p b e", b=TB),
                                 bc(bcr[:, 2 * H:], TB, 1), ALU.add))
            for b in range(TB):
                link(V.max(out=v8[:, b, :], in_=lgs[:, b, :]))
                link(V.max_index(i8[:, b, :], v8[:, b, :], lgs[:, b, :]))
            link(V.tensor_copy(tk[:, 0], i8[:, :, 0:TOPK]))
            step(V.tensor_tensor(tk[:, 2], v8[:, :, 0:TOPK], bc(v8[:, :, 0], TOPK, 2), ALU.subtract), top_ok, 1)
            link(V.tensor_tensor(oh[:, :, :, :], bc(bc(iotaf[:, 0:E], TB, 1), TOPK, 3), bc(tk[:, 0], E, 2), ALU.is_equal))
            link(V.tensor_reduce(maskf, oh[:, :, :, :], AX.X, ALU.add))
            step(V.tensor_copy(maskb[:, :, :], maskf), mask_ok, 1)
            dve.wait_ge(texp_ok, 1)
            link(V.tensor_reduce(nbf[:, 0, 0:TB], tk[:, 1], AX.X, ALU.add))
            link(V.reciprocal(nbf[:, 0, 8:8 + TB], nbf[:, 0, 0:TB]))
            step(V.tensor_tensor(tk[:, 3], tk[:, 1], bc(nbf[:, 0, 8:8 + TB], TOPK, 2), ALU.mult), top_ok, 2)
            dve.wait_ge(rank_ps, 1)
            rk = ps[:, 1, 0:TB * E].rearrange("p (b e) -> p b e", b=TB)
            link(V.tensor_scalar(rank[:, :, :], rk, 1.0, None, ALU.add))
            link(V.tensor_tensor(rank[:, :, :], rank[:, :, :], maskb[:, :, :], ALU.mult))
            link(V.tensor_scalar(rank[:, :, :], rank[:, :, :], -1.0, None, ALU.add))
            link(V.tensor_scalar(nbf[:, 0, :], ps[:, 1, TB * E:(TB + 1) * E], float(SLOTS - 1), None, ALU.add))
            link(V.tensor_copy(nbi[:, :], nbf[:, 0, :]))
            link(V.tensor_scalar(nbi[:, :], nbi[:, :], SLOTS.bit_length() - 1, None, ALU.arith_shift_right))
            link(V.tensor_copy(nbf[:, 0, :], nbi[:, :]))
            link(V.tensor_scalar(nbf[:, 0, :], nbf[:, 0, :], 1.0, None, ALU.max))
            link(V.scalar_tensor_tensor(out=key[:, 0, :], in0=nbf[:, 0, :], scalar=float(E), in1=iotaf[:, 0:E],
                                        op0=ALU.mult, op1=ALU.add))
            link(V.tensor_copy(key[:, 0, 0:2], iotaf[:, 0:2]))
            link(V.tensor_tensor(key[:, 1, :], key[:, 0, :], ident[:, 0:E], ALU.mult))
            link(V.tensor_reduce(kcol[:, 0:1], key[:, 1, :], AX.X, ALU.add))
            link(V.tensor_tensor(key[:, 1, :], nbf[:, 0, :], ident[:, 0:E], ALU.mult))
            link(V.tensor_reduce(kcol[:, 1:2], key[:, 1, :], AX.X, ALU.add))
            link(V.tensor_scalar(key[:, 1, :], key[:, 0, :], kcol[:, 0:1], None, ALU.is_lt))
            link(V.tensor_reduce(kcol[:, 0:1], key[:, 1, :], AX.X, ALU.add))
            link(V.tensor_scalar(kcol[:, 2:3], kcol[:, 0:1], -2.0, float(2 * E + 1), ALU.mult, ALU.add))
            link(V.tensor_scalar(kcol[:, 3:4], kcol[:, 0:1], 2.0, -2.0, ALU.mult, ALU.add))
            link(V.tensor_tensor(kcol[:, 2:3], kcol[:, 2:3], kcol[:, 3:4], ALU.min))
            link(V.tensor_scalar(kcol[:, 3:4], kcol[:, 0:1], 1.0, None, ALU.min))
            link(V.tensor_tensor(kcol[:, 2:3], kcol[:, 2:3], kcol[:, 3:4], ALU.max))
            link(V.tensor_scalar(key[:, 1, :], iotaf[:, 0:E], kcol[:, 2:3], None, ALU.is_equal))
            link(V.tensor_copy(pml[:, 0, :], kcol[:, 1:2].to_broadcast([P, P])))
            step(V.tensor_copy(pml[:, 1, :], pidx[:, 0:1].to_broadcast([P, P])), ebc_ok, 1)
            dve.wait_ge(tab_ps, 1)
            link(V.tensor_copy(nbf[:, 0, :], ps[:, 1, 256:256 + E]))
            link(V.tensor_copy(key[:, 0, :], ps[:, 1, 256 + E:256 + 2 * E]))
            link(V.memset(nbf[:, 1, :], 1.0))
            link(V.tensor_tensor_scan(out=nbf[:, 2, :], data0=nbf[:, 1, :], data1=nbf[:, 0, :], initial=0.0,
                                      op0=ALU.mult, op1=ALU.add))
            link(V.tensor_scalar(nbf[:, 3, :], nbf[:, 2, :], pidx[:, 0:1], None, ALU.is_le))
            link(V.tensor_reduce(ebc[:, 0:1], nbf[:, 3, :], AX.X, ALU.add))
            link(V.tensor_tensor(nbf[:, 3, :], nbf[:, 3, :], nbf[:, 2, :], ALU.mult))
            link(V.tensor_reduce(ebc[:, 1:2], nbf[:, 3, :], AX.X, ALU.max))
            link(V.tensor_tensor(ebc[:, 3:4], pidx[:, 0:1], ebc[:, 1:2], ALU.subtract))
            link(V.tensor_scalar(ebc[:, 2:3], ebc[:, 0:1], float(E), float(T), ALU.is_ge, ALU.mult))
            link(V.scalar_tensor_tensor(out=ebc[:, 3:4], in0=ebc[:, 3:4], scalar=float(SLOTS), in1=ebc[:, 2:3],
                                        op0=ALU.mult, op1=ALU.add))
            link(V.tensor_scalar(ebc[:, 1:2], ebc[:, 3:4], float(T), None, ALU.min))
            link(V.tensor_scalar(ebc[:, 0:1], ebc[:, 0:1], float(E - 1), None, ALU.min))
            link(V.tensor_scalar(key[:, 1, :], iotaf[:, 0:E], ebc[:, 0:1], None, ALU.is_equal))
            link(V.tensor_tensor(key[:, 1, :], key[:, 1, :], key[:, 0, :], ALU.mult))
            step(V.tensor_reduce(ebc[:, 0:1], key[:, 1, :], AX.X, ALU.add), ebc_ok, 2)
            link(V.tensor_copy(tab[0:1, VISIT:VISIT + E], key[0:1, 0, :]))
            link(V.memset(tab[0:1, 0:1], 0))
            link(V.tensor_copy(tab[0:1, 1:E + 1], nbf[0:1, 2, :]))
            dve.wait_ge(tab_ps, 2)
            link(V.tensor_copy(tab[0:1, E + 1:USED], ps[0:1, 2, 0:2 * P]))
            link(V.tensor_scalar(tab[0:1, USED:PAIRS], nbf[0:1, 2, :], float(NU), float(-NU), ALU.mult, ALU.add))
            link(V.tensor_scalar(tab[0:1, E:E + 1], nbf[0:1, 2, E - 1:E], 1.0, None, ALU.add))
            link(V.tensor_scalar(tab[0:1, PAIRS:PAIRS + 1], tab[0:1, E:E + 1], 1, None, ALU.arith_shift_right))
            step(V.tensor_scalar(tab[0:1, E:E + 1], tab[0:1, PAIRS:PAIRS + 1], 1, None, ALU.arith_shift_left), tab_ok, 1)

            def make_hot(g, count):
                e = dve.value_load(tab[0:1, bass.ds(g + (E + 1), 1)], min_val=0, max_val=E - 1)
                s0 = dve.value_load(tab[0:1, bass.ds(g + (E + 1 + P), 1)], min_val=0, max_val=T)
                V.tensor_copy(selu[:, :], E3[:, bass.ds(e, 1)].to_broadcast([96, SLOTS])).then_inc(sel_step, 1)
                V.tensor_copy(gie[:, :, :], gip[:, :, bass.ds(e, 1), :].rearrange("p b a c -> p b (a c)")).then_inc(sel_step, 1)
                slots = bc(bc(iotaf[:, bass.ds(s0, SLOTS)], Q, 1), TB, 1)
                mine = bc(bc(rank[:, :, bass.ds(e, 1)].rearrange("p b a -> p (b a)"), Q, 2), SLOTS, 3)
                dve.wait_ge(sel_step, count * 2)
                step(V.tensor_tensor(hot[:, :, :, :], slots, mine, ALU.is_equal), hot_ok, count)

            dve.wait_ge(gi_ok, 1)
            make_hot(0, 1)
            pairs = dve.value_load(tab[0:1, PAIRS:PAIRS + 1], min_val=E // 2, max_val=MAXB // 2)

            def swiglu(g, i, p):
                dve.wait_ge(idx_ps, g + 1)
                dve.wait_ge(scat[p], i * 16)
                step(V.tensor_reduce(wslot[:, p, :], ps[:, 7, 0:6].rearrange("p (n c) -> p c n", n=3), AX.X, ALU.add),
                     info_step, g * 3 + 1)
                step(V.tensor_scalar(rowf[:, p:p + 1], wslot[:, p, 1:2], OOB, float(Q), ALU.add, ALU.mult), info_step, g * 3 + 2)
                step(V.tensor_tensor(rowf[:, p:p + 1], rowf[:, p:p + 1], qcol[:, :], ALU.add), info_step, g * 3 + 3)
                V.tensor_copy(rowi[:, p:p + 1], rowf[:, p:p + 1]).then_inc(slot_ok, 1)
                dve.wait_ge(dnb_used, g)
                step(V.tensor_copy(seld[:, :], selu[:, :]), seld_ok, g + 1)
                dve.wait_ge(gub_used, g + 1)
                make_hot(g + 1, g + 2)
                dve.wait_ge(w_used, g * NU + NGU)
                step(V.tensor_scalar(gc[:, :], ps[:, 0, 0:QD], LIMIT, None, ALU.min), gc_ok, g + 1)
                step(V.tensor_scalar(uc[:, :], ps[:, 0, QD:], -LIMIT, LIMIT, ALU.max, ALU.min), uc_step, g * 2 + 1)
                step(V.scalar_tensor_tensor(out=uc[:, :], in0=uc[:, :], scalar=1.0, in1=gc[:, :], op0=ALU.add,
                                            op1=ALU.mult), uc_step, g * 2 + 2)
                dve.wait_ge(sg_ok, g + 1)
                dve.wait_ge(at_ps, g)
                step(V.tensor_tensor(act_[:, :], uc[:, :], sg[:, :], ALU.mult), act_ok, g + 1)

            with dve.Fori(0, pairs) as i:
                for p in range(2):
                    swiglu(2 * i + p, i, p)
            dve.wait_ge(fnw_in, 32)
            for b in range(TB):
                dve.wait_ge(y_in[b], 32)
                for k in range(TOPK):
                    y = ring[:, (b * TOPK + k) * D:(b * TOPK + k + 1) * D]
                    ins = V.tensor_tensor(xs[:, b, :], xs[:, b, :], y, ALU.add)
                    if k < TOPK - 1:
                        step(ins, fin_add, b * (TOPK - 1) + k + 1)
                    else:
                        step(ins, fin_sum, b + 1)
            for b in range(TB):
                dve.wait_ge(fin_rt, b + 1)
                step(V.reciprocal(sm[:, 44 + b:45 + b], sm[:, 32 + b:33 + b]), fin_rc, b + 1)
                V.scalar_tensor_tensor(out=ring[:, b * TOPK * D:b * TOPK * D + D], in0=xs[:, b, :],
                                       scalar=sm[:, 44 + b:45 + b], in1=fnw, op0=ALU.mult,
                                       op1=ALU.mult).then_inc(fin_o, 1)

        @block.tensor
        def _(pe):
            mm, tr = nc.tensor.matmul, nc.tensor.transpose
            pe.wait_ge(const_ok, 6)
            pe.wait_ge(par_in, 16 * (3 + CONV))
            tr(ps[:, 7, 0:61], prow[:, :], ident[0:61, 0:61]).then_inc(pcol_ps, 1)
            pe.wait_ge(pcol_ok, 1)
            pe.wait_ge(xn_ok, TB)
            for k in range(KD):
                for b in range(TB):
                    last = tr(bank(k)[:, b * P:(b + 1) * P], xn[:, b, k * P:(k + 1) * P], ident)
                last.then_inc(xt_ps, 1)
            pe.wait_ge(ht_even, KD // 2)
            pe.wait_ge(ht_odd, KD // 2)

            def project(buf, half, b):
                for k in range(KD):
                    last = mm(bank(b), win[:, buf, k, half * P:(half + 1) * P], hT[:, k, :], start=k == 0, stop=k == KD - 1)
                last.then_inc(proj_ps, 1)

            def four_chunks(out, w, src, s):
                for k in range(KD):
                    q = k % Q
                    last = mm(out[SLOTS * q:SLOTS * (q + 1), :], w[:, k, :], src[:, k, :], start=k < Q, stop=k >= Q)
                last.then_inc(s, 1)

            def sum_chunks(out, part, n, s):
                for b in range(TB):
                    last = mm(out[:, b * n:(b + 1) * n], part[:, b * P:(b + 1) * P], S4[:, 0:n], start=True, stop=True)
                last.then_inc(s, 1)

            pe.wait_ge(wba_in, 16)
            four_chunks(bank(6), wba, hT, part_ps)
            with pe.Fori(0, 3) as i:
                for r in range(4):
                    n = 4 * i + r
                    if r % 2 == 0:
                        pe.wait_ge(win_in[r // 2], i * 16 + 16)
                    project(r // 2, r % 2, r % 2)
                    pe.wait_ge(conv_ok, n)
            pe.wait_ge(const_ok, 7)
            pe.wait_ge(part_ok, 1)
            sum_chunks(bank(7), ba_part, 2 * H, ba_ps)
            for n in range(NQKV, NQKV + 2 * H):
                piece = n // 2
                if n % 2 == 0:
                    pe.wait_ge(win_in[piece % 2], (piece // 2 + 1) * 16)
                if n == NQKV + 1:
                    pe.wait_ge(conv_ok, NQKV)
                    for i in range(2 * H):
                        pe.wait_ge(sq_ok, i + 1)
                        if i >= 6:
                            pe.wait_ge(nroot_ok, i - 4)
                        mm(bank(nrm_bank(i)), ones, wsf[:, i], start=True, stop=True).then_inc(nrm_ps, 1)
                    pe.wait_ge(nroot_ok, 1)
                if n > NQKV + 1:
                    pe.wait_ge(silu_ok, n - 1)
                if n == NQKV + 2:
                    pe.wait_ge(g_ok, 1)
                    for i, c in enumerate((causal, same, first, second)):
                        last = mm(ps[:, 7, 64 + i * TB * H:64 + (i + 1) * TB * H], c, gt[:, 8].rearrange("p b h -> p (b h)"),
                                  start=True, stop=True)
                    last.then_inc(gcum_ps, 1)
                project(piece % 2, n % 2, n % 2)
            pe.wait_ge(silu_ok, NQKV + 2 * H)
            pe.wait_ge(nroot_ok, 2 * H)
            pe.wait_ge(gcs_ok, 1)

            def heads(b, f, s):
                for h in range(H):
                    lhsT, rhs = f(h)
                    last = mm(bank(b, H)[:, h, :], lhsT, rhs, start=True, stop=True)
                last.then_inc(s, 1)

            def prepare(t):
                def now(n, h):
                    return qkv[:, n + h, bass.ds(t * P, P)]

                def flat(v):
                    return v.rearrange("p a b -> p (a b)")

                def g_rows():
                    pe.wait_ge(grow_ok, 2 * t + 1)
                    mm(bank(0), ones, flat(GUM), start=True, stop=True).then_inc(grow_ps, 1)

                def products():
                    pe.wait_ge(grow_ok, 2 * t + 2)
                    mm(bank(1), ones, flat(BI), start=True, stop=True).then_inc(brow_ps, 1)
                    pe.wait_ge(kv_ok, 2 * t + 2)
                    for h in range(H):
                        mm(bank(2, H)[:, h, :], KTS[:, h, :], now(H, h), start=True, stop=True)
                    heads(3, lambda h: (KTS[:, h, :], now(0, h)), kk_ps)

                def k_tokens():
                    for h in range(H):
                        last = tr(bank(4, H)[:, h, :], KTS[:, h, :], ident)
                    last.then_inc(ktok_ps, 1)

                def v_tokens():
                    pe.wait_ge(dx_ok, t + 1)
                    for h in range(H):
                        last = tr(bank(0, H)[:, h, :], VTS[:, h, :], ident)
                    last.then_inc(vtok_ps, 1)

                def transposed():
                    pe.wait_ge(r2_ok, t + 1)
                    for h in range(H):
                        last = tr(bank(1, H)[:, h, :], TR[:, h, :], ident)
                    last.then_inc(t2_ps, 1)
                return g_rows, products, k_tokens, v_tokens, transposed

            def invert(t):
                pe.wait_ge(t_ok, t + 1)
                for s in range(LEVELS):
                    for a in range(2):
                        if s:
                            pe.wait_ge(t_lvl, t * 2 * (LEVELS - 1) + (2 * s - 1 + a))
                            pe.wait_ge(r_ok, t * 2 * LEVELS + (2 * s - 1 + a))
                        for i in range(2):
                            last = mm(bank(6 - 3 * a, H)[:, i, :], AT[:, 2 * a + i, :], TM[:, 2 * a + i, :],
                                      start=True, stop=True)
                        last.then_inc(y_ps, 1)
                    for a in range(2):
                        pe.wait_ge(ym_ok, t * 2 * LEVELS + (2 * s + a + 1))
                        if s < LEVELS - 1:
                            for i in range(2):
                                mm(bank(t_bank(a), H)[:, i, :], TR[:, 2 * a + i, :], YM[:, 2 * a + i, :],
                                   start=True, stop=True)
                        for i in range(2):
                            last = mm(bank(r_bank(a), H)[:, i, :], YM[:, 2 * a + i, :], TR[:, 2 * a + i, :],
                                      start=True, stop=True)
                        last.then_inc(tr_ps, 1)
                pe.wait_ge(r_ok, t * 2 * LEVELS + 2 * LEVELS)
                heads(1, lambda h: (TR[:, h, :], VB[:, h, :]), uw_ps)
                heads(2, lambda h: (KBG[:, h, :], TR[:, h, :]), uw_ps)

            def state_values(t, c):
                heads(6, lambda h: (WT[:, h, :], ST[:, c, h, :]), ws_ps)

            def state_change(t, c):
                pe.wait_ge(vn_ok, 2 * t + (c + 1))
                pe.wait_ge(cur_ok, 5 * t + 5)
                kdz = (KDZ0, KDZ1)[c]
                heads(7, lambda h: (kdz[:, h, :], VN[:, h, :]), su_ps)

            def outputs(t):
                pe.wait_ge(oc_ok, t)
                for h in range(H):
                    o = bank(5, H)[:, h, :]
                    mm(o, QD0[:, h, :], ST[:, 0, h, :], start=True, stop=False)
                    mm(o, QD1[:, h, :], ST[:, 1, h, :], start=False, stop=False)
                    last = mm(o, QKT[:, h, :], VN[:, h, :], start=False, stop=True)
                last.then_inc(o_ps, 1)

            pe.wait_ge(qk_ok, 2 * H)
            pe.wait_ge(zero_ok, 1)
            for part in prepare(0):
                part()
            with pe.Fori(0, TB - 1) as tb:
                g_rows, products, k_tokens, v_tokens, transposed = prepare(tb + 1)
                invert(tb)
                g_rows()
                pe.wait_ge(uw_ok, 2 * tb + 2)
                pe.wait_ge(st_ok, 2 * tb * H)
                state_values(tb, 0)
                products()
                state_change(tb, 0)
                k_tokens()
                pe.wait_ge(st_ok, (2 * tb + 1) * H)
                state_values(tb, 1)
                v_tokens()
                state_change(tb, 1)
                outputs(tb)
                transposed()
            invert(TB - 1)
            pe.wait_ge(uw_ok, 2 * TB)
            pe.wait_ge(st_ok, 2 * (TB - 1) * H)
            for c in range(2):
                if c:
                    pe.wait_ge(st_ok, (2 * TB - 1) * H)
                state_values(TB - 1, c)
                if c == 0:
                    state_change(TB - 1, c)
                else:
                    pe.wait_ge(vn_ok, 2 * TB)
            outputs(TB - 1)
            pe.wait_ge(pw_in, 16)
            for g in range(4):
                if g == 3:
                    pe.wait_ge(oc_ok, TB)
                pe.wait_ge(pool_mix, g + 1)
                mm(bank(pool_bank(g)), poolw[:, g, :], catT[:, H + g, :], start=True, stop=True).then_inc(pool_ps, 1)
            for b in range(TB):
                pe.wait_ge(on_ok, b + 1)
                for h in range(H):
                    last = tr(bank(b, H)[:, h, :], O4[:, b, h, :], ident)
                last.then_inc(ot_ps, 1)
            pe.wait_ge(pooled_ok, 4)
            pe.wait_ge(wout_in, 16)
            for b in range(TB):
                pe.wait_ge(cat_ok, b + 1)
                for half in range(2):
                    n = 2 * b + half
                    if n >= 4:
                        pe.wait_ge(x1_ok, n - 3)
                    for k in range(KD):
                        last = mm(bank(4 + n % 4), catT[:, k, b * P:(b + 1) * P], wout[:, k, 512 * half:512 * (half + 1)],
                                  start=k == 0, stop=k == KD - 1)
                    last.then_inc(op_ps, 1)
            for b in range(TB):
                pe.wait_ge(h2_ok, b + 1)
                for half in range(2):
                    n = 2 * b + half
                    if b >= 2:
                        pe.wait_ge((h2t_lo, h2t_hi)[half], b - 1)
                    for i in range(4):
                        k = 4 * half + i
                        last = tr(bank(2 * (b % 2) + half, 4)[:, i, :], h2[:, b, k * P:(k + 1) * P], ident)
                    last.then_inc(h2t_ps, 1)
            pe.wait_ge(h2t_lo, TB)
            pe.wait_ge(h2t_hi, TB)
            pe.wait_ge(wrt_in, 16)
            four_chunks(bank(4), wrt, h2T, part_ps)
            pe.wait_ge(part_ok, 2)
            sum_chunks(bank(0), lg_part, E, lg_ps)
            pe.wait_ge(mask_ok, 1)
            for b in range(TB + 1):
                for a in range(min(b + 1, TB)):
                    last = mm(ps[:, 1, b * E:(b + 1) * E], cstb[:, 0 if a == b else 1, :], maskb[:, a, :], start=a == 0,
                              stop=a == min(b, TB - 1))
            last.then_inc(rank_ps, 1)
            pe.wait_ge(ebc_ok, 1)
            for i in range(2):
                last = mm(ps[:, 1, 256 + i * E:256 + (i + 1) * E], pml[0:E, i, :], key[0:E, 1, :], start=True, stop=True)
            last.then_inc(tab_ps, 1)
            pe.wait_ge(ebc_ok, 2)
            for i in range(2):
                last = mm(ps[0:1, 2, i * P:(i + 1) * P], ebc[:, i:i + 1], ident, start=True, stop=True)
            last.then_inc(tab_ps, 1)

            def gather(count, free):
                pe.wait_ge(hot_ok, count)
                if free is not None:
                    pe.wait_ge(xg_ok, free)
                for b in range(TB):
                    for n in range(3):
                        for q in range(Q):
                            last = mm(ps[SLOTS * q:SLOTS * (q + 1), 2, 0:QD], hot[:, b, 0, :], h2p[n][:, b, q * QD:(q + 1) * QD],
                                      start=b == 0 and n == 0, stop=b == TB - 1 and n == 2)
                last.then_inc(gat_ps, 1)

            def numbers(free):
                if free is not None:
                    pe.wait_ge(slot_ok, free)
                for b in range(TB):
                    last = mm(ps[:, 7, 0:6], hot[:, b].rearrange("p q s -> p (q s)"), gie[:, b], start=b == 0,
                              stop=b == TB - 1)
                last.then_inc(idx_ps, 1)

            def rows_T(count, free):
                pe.wait_ge(xg_ok, count)
                if free is not None:
                    pe.wait_ge(xgt_ok, free)
                for i in range(2):
                    last = tr(bank(3, 4)[:, i, :], xg[:, i * P:(i + 1) * P], ident)
                last.then_inc(xgt_ps, 1)

            pe.wait_ge(tab_ok, 1)
            pe.wait_ge(h2p_ok, 3 * TB)
            gather(1, None)
            numbers(None)
            rows_T(1, None)
            pe.wait_ge(bias_home, 1)

            def expert_block(g, j, turn):
                def landed(u):
                    slot, t = slot_of(j, u)
                    pe.wait_ge(slot_in[slot], (turn + t + 1) * 16)
                    return ring[:, slot * UNIT:(slot + 1) * UNIT].rearrange("p (s c) -> p s c", s=2)

                pe.wait_ge(xgt_ok, g + 1)
                pe.wait_ge(act_ok, g)
                for q in range(Q):
                    last = mm(ps[SLOTS * q:SLOTS * (q + 1), 0, :], selu[:, :],
                              bias3[:, 0:2 * D].rearrange("p (s c) -> p s c", s=2)[:, :, q * QD:(q + 1) * QD],
                              start=True, stop=False)
                last.then_inc(gub_used, 1)
                for u in range(NGU):
                    w = landed(u)
                    for q in range(Q):
                        last = mm(ps[SLOTS * q:SLOTS * (q + 1), 0, :],
                                  xgT[:, u % 2, SLOTS * (u // 2):SLOTS * (u // 2 + 1)],
                                  w[:, :, q * QD:(q + 1) * QD], start=False, stop=u == NGU - 1)
                    last.then_inc(w_used, 1)
                gather(g + 2, g + 1)
                pe.wait_ge(act_ok, g + 1)
                pe.wait_ge(actt_ok, g)
                for i in range(2):
                    last = tr(bank(4, 4)[:, i, :], act_[:, i * P:(i + 1) * P], ident)
                last.then_inc(at_ps, 1)
                numbers(g + 1)
                pe.wait_ge(seld_ok, g + 1)
                pe.wait_ge(ys_ok, g)
                for q in range(Q):
                    last = mm(ps[SLOTS * q:SLOTS * (q + 1), 1, 0:QD], seld[:, :],
                              bias3[:, 2 * D + q * QD:2 * D + (q + 1) * QD], start=True, stop=False)
                last.then_inc(dnb_used, 1)
                rows_T(g + 2, g + 1)
                pe.wait_ge(actt_ok, g + 1)
                for u in range(NGU, NU):
                    w = landed(u)
                    for i in range(2):
                        c = 2 * (u - NGU) + i
                        for q in range(Q):
                            last = mm(ps[SLOTS * q:SLOTS * (q + 1), 1, 0:QD],
                                      actT[:, c % 2, SLOTS * (c // 2):SLOTS * (c // 2 + 1)],
                                      w[:, i, q * QD:(q + 1) * QD], start=False, stop=c == KD - 1)
                    last.then_inc(w_used, 1)

            with pe.Fori(0, E // UNROLL) as grp:
                lo = pe.value_load(tab[0:1, bass.ds(UNROLL * grp, 1)], min_val=0, max_val=MAXB)
                for j in range(UNROLL):
                    hi = pe.value_load(tab[0:1, bass.ds(UNROLL * grp + (j + 1), 1)], min_val=0, max_val=MAXB)
                    with pe.Fori(lo, hi) as g:
                        expert_block(g, j, TURNS * grp)
                    lo = hi
            for e in range(E // UNROLL * UNROLL, E):
                lo = pe.value_load(tab[0:1, e:e + 1], min_val=0, max_val=MAXB)
                hi = pe.value_load(tab[0:1, e + 1:e + 2], min_val=0, max_val=MAXB)
                with pe.Fori(lo, hi) as g:
                    expert_block(g, e % UNROLL, TURNS * (e // UNROLL))


_INS = ['x', 'attn_norm_w', 'w_in', 'conv_w', 'a_log', 'dt_bias', 'dn_norm_w', 'pool_w', 'pool_scale', 'w_out',
        'ffn_norm_w', 'w_router', 'b_router', 'w_gate_up', 'b_gate_up', 'w_down', 'b_down', 'final_norm_w']


def kernel(**inputs):
    import numpy as _np
    import concourse.bacc as _bacc
    from concourse.bass_utils import run_bass_kernel_spmd as _run

    nc = _bacc.Bacc("TRN2", target_bir_lowering=False, num_devices=1)
    arrays, args = {}, []
    for name in _INS:
        a = _np.ascontiguousarray(inputs[name])
        arrays[f"in_{name}_dram"] = a
        args.append(nc.dram_tensor(f"in_{name}_dram", a.shape, mybir.dt.from_np(a.dtype), kind="ExternalInput").ap())
    args.append(nc.dram_tensor("out_dram", (1, T, D), F32, kind="ExternalOutput").ap())
    args.append(nc.dram_tensor("pair_rows_dram", (T * TOPK * Q, QD), F32, kind="Internal").ap())
    args.append(nc.dram_tensor("x1_rows_dram", (T, D), F32, kind="Internal").ap())
    moe_block(nc, *args)
    r = _run(nc, [arrays], core_ids=[0])
    return r.results[0]["out_dram"]
```
